# Optimizing a Trainium2 kernel written in Bass

```python
import math
import jax
import jax.numpy as jnp
from jax import lax
import numpy as np

D_MODEL = 2048
BATCH = 1
SEQ = 512
DEPTH = 1
DEC_BATCH = 8
DEC_SEQ = 16
PAST_LEN = 256

CHUNK = 64
D_MIX = D_MODEL
D_A = D_MIX // 2
D_B = D_MIX - D_A
A_HEADS = 4
A_DV = D_A // A_HEADS
A_DQK = A_DV // 2
QK_W = 2 * A_HEADS * A_DQK
CONV_W = 4
B_GROUP = 16
B_GROUPS = D_B // B_GROUP
B_STATE = 64
D_FF = -(-8 * D_MODEL // (3 * 256)) * 256
N_IN = QK_W + 2 * D_A + 2 * A_HEADS + D_B
EPS = 1e-6

kernel_name = 'hymba_mlstm_s5_stream_step'

def rmsnorm(x, g):
    xf = x.astype(jnp.float32)
    y = xf * lax.rsqrt(jnp.mean(xf * xf, axis=-1, keepdims=True) + EPS)
    return (y * g.astype(jnp.float32)).astype(x.dtype)

def causal_conv(x, buf, w, b):
    seqlen = x.shape[1]
    xp = jnp.concatenate([buf.astype(x.dtype), x], axis=1)
    out = b
    for j in range(CONV_W):
        out = out + xp[:, j:j + seqlen] * w[j]
    return jax.nn.silu(out), xp[:, xp.shape[1] - (CONV_W - 1):]

def mlstm_chunk(c0, n0, m0, q, k, v, li, lf):
    seqlen = q.shape[1]
    li = jnp.swapaxes(li, 1, 2)
    fcum = jnp.cumsum(jnp.swapaxes(lf, 1, 2), axis=-1)
    causal = jnp.tril(jnp.ones((seqlen, seqlen), dtype=bool))
    dmat = jnp.where(causal, fcum[..., :, None] - fcum[..., None, :] + li[..., None, :], -jnp.inf)
    inter = fcum + m0[..., None]
    m_t = jnp.maximum(jnp.max(dmat, axis=-1), inter)
    s = jnp.einsum('bthd,bshd->bhts', q, k) * jnp.exp(dmat - m_t[..., None])
    g_inter = jnp.exp(inter - m_t)
    num = jnp.einsum('bhts,bshv->bthv', s, v) + jnp.einsum('bht,bhvd,bthd->bthv', g_inter, c0, q)
    den = jnp.sum(s, axis=-1) + g_inter * jnp.einsum('bhd,bthd->bht', n0, q)
    scale = jnp.maximum(jnp.abs(den), jnp.exp(-m_t))
    h = num / jnp.swapaxes(scale, 1, 2)[..., None]
    f_last = fcum[..., -1]
    lw = f_last[..., None] - fcum + li
    m_new = jnp.maximum(f_last + m0, jnp.max(lw, axis=-1))
    ws = jnp.exp(lw - m_new[..., None])
    decay = jnp.exp(f_last + m0 - m_new)
    c_new = decay[..., None, None] * c0 + jnp.einsum('bhs,bshv,bshd->bhvd', ws, v, k)
    n_new = decay[..., None] * n0 + jnp.einsum('bhs,bshd->bhd', ws, k)
    return c_new, n_new, m_new, h

def s5_discretise(lam_re, lam_im, log_dt, b_re, b_im):
    f32 = jnp.float32
    lam_re = lam_re.astype(f32)
    lam_im = lam_im.astype(f32)
    b_re = b_re.astype(f32)
    b_im = b_im.astype(f32)
    dt = jnp.exp(log_dt.astype(f32))[:, None]
    mag = jnp.exp(lam_re * dt)
    ang = lam_im * dt
    lb_re = mag * jnp.cos(ang)
    lb_im = mag * jnp.sin(ang)
    den = lam_re * lam_re + lam_im * lam_im
    nr = lb_re - 1.0
    f_re = (nr * lam_re + lb_im * lam_im) / den
    f_im = (lb_im * lam_re - nr * lam_im) / den
    bb_re = f_re[..., None] * b_re - f_im[..., None] * b_im
    bb_im = f_re[..., None] * b_im + f_im[..., None] * b_re
    return lb_re, lb_im, bb_re, bb_im

def _affine_combine(e1, e2):
    a1r, a1i, b1r, b1i = e1
    a2r, a2i, b2r, b2i = e2
    return (a1r * a2r - a1i * a2i,
            a1r * a2i + a1i * a2r,
            a2r * b1r - a2i * b1i + b2r,
            a2r * b1i + a2i * b1r + b2i)

def s5_chunk(x_re, x_im, u, lb_re, lb_im, bb_re, bb_im, c_re, c_im, d_skip):
    bu_re = jnp.einsum('blgi,gpi->blgp', u, bb_re)
    bu_im = jnp.einsum('blgi,gpi->blgp', u, bb_im)
    bu_re = bu_re.at[:, 0].add(lb_re * x_re - lb_im * x_im)
    bu_im = bu_im.at[:, 0].add(lb_re * x_im + lb_im * x_re)
    a_re = jnp.broadcast_to(lb_re, bu_re.shape)
    a_im = jnp.broadcast_to(lb_im, bu_im.shape)
    _, _, s_re, s_im = lax.associative_scan(_affine_combine, (a_re, a_im, bu_re, bu_im), axis=1)
    y = (jnp.einsum('gip,blgp->blgi', c_re, s_re)
         - jnp.einsum('gip,blgp->blgi', c_im, s_im) + d_skip * u)
    return s_re[:, -1], s_im[:, -1], y

def token_mixers(h, conv_buf, c0, n0, m0, sr0, si0, p):
    f32 = jnp.float32
    bt, seqlen, _ = h.shape
    cl = min(seqlen, CHUNK)
    nc = seqlen // cl
    proj = h @ p['w_in']
    o1 = QK_W
    o2 = o1 + D_A
    o3 = o2 + D_A
    o4 = o3 + A_HEADS
    o5 = o4 + A_HEADS
    qk, conv_new = causal_conv(proj[..., :o1], conv_buf, p['w_conv'], p['b_conv'])
    qk = qk.astype(f32)
    q = qk[..., :QK_W // 2].reshape(bt, seqlen, A_HEADS, A_DQK) * (A_DQK ** -0.5)
    k = qk[..., QK_W // 2:].reshape(bt, seqlen, A_HEADS, A_DQK)
    v = proj[..., o1:o2].astype(f32).reshape(bt, seqlen, A_HEADS, A_DV)
    og = proj[..., o2:o3].astype(f32).reshape(bt, seqlen, A_HEADS, A_DV)
    li = proj[..., o3:o4].astype(f32) + p['b_igate'].astype(f32)
    lf = jax.nn.log_sigmoid(proj[..., o4:o5].astype(f32) + p['b_fgate'].astype(f32))
    u = proj[..., o5:].astype(f32).reshape(bt, seqlen, B_GROUPS, B_GROUP)
    d_skip = p['s5_d'].astype(f32).reshape(B_GROUPS, B_GROUP)
    c_re = p['s5_c_re'].astype(f32)
    c_im = p['s5_c_im'].astype(f32)

    def to_chunks(a):
        return jnp.moveaxis(a.reshape((bt, nc, cl) + a.shape[2:]), 1, 0)

    xs = tuple(to_chunks(a) for a in (q, k, v, li, lf, u))

    def step(carry, xc):
        c, n, m, sr, si = carry
        qc, kc, vc, lic, lfc, uc = xc
        c, n, m, hc = mlstm_chunk(c, n, m, qc, kc, vc, lic, lfc)
        sr, si, yc = s5_chunk(sr, si, uc, p['lb_re'], p['lb_im'], p['bb_re'], p['bb_im'],
                              c_re, c_im, d_skip)
        return (c, n, m, sr, si), (hc, yc)

    init = (c0.astype(f32), n0.astype(f32), m0.astype(f32), sr0.astype(f32), si0.astype(f32))
    (c1, n1, m1, sr1, si1), (hs, ys) = lax.scan(step, init, xs)
    hs = jnp.moveaxis(hs, 0, 1).reshape(bt, seqlen, A_HEADS, A_DV)
    ys = jnp.moveaxis(ys, 0, 1).reshape(bt, seqlen, D_B)
    g_mh = p['g_mh'].astype(f32).reshape(A_HEADS, A_DV)
    hn = hs * lax.rsqrt(jnp.mean(hs * hs, axis=-1, keepdims=True) + EPS) * g_mh
    out_a = (hn * jax.nn.sigmoid(og)).reshape(bt, seqlen, D_A)
    z = jax.nn.gelu(ys)
    gate = jax.nn.sigmoid((z.astype(h.dtype) @ p['w_glu'] + p['b_glu']).astype(f32))
    out_b = z * gate
    mix = jnp.concatenate([out_a, out_b], axis=-1).astype(h.dtype) @ p['w_out']
    return mix, (conv_new, c1, n1, m1, sr1, si1)

def layer(x, conv_buf, c0, n0, m0, sr0, si0, p):
    hm = rmsnorm(x, p['g_pre_mix'])
    mix, st = token_mixers(hm, conv_buf, c0, n0, m0, sr0, si0, p)
    x = x + rmsnorm(mix, p['g_post_mix'])
    hf = rmsnorm(x, p['g_pre_ffn'])
    ff = (jax.nn.silu(hf @ p['w_gate']) * (hf @ p['w_up'])) @ p['w_down']
    x = x + rmsnorm(ff, p['g_post_ffn'])
    return x, st

def setup_inputs(seed: int = 0) -> dict:
    key = jax.random.key(seed)
    ks = jax.random.split(key, 32)
    f32 = jnp.float32

    def nrm(k, shape, s):
        return jax.random.normal(k, shape, f32) * s

    L = DEPTH
    n_idx = jnp.arange(B_STATE, dtype=f32)
    return {
        'x_prompt': nrm(ks[0], (BATCH, SEQ, D_MODEL), 1.0),
        'x_sample': nrm(ks[1], (DEC_BATCH, DEC_SEQ, D_MODEL), 1.0),
        'state_conv': nrm(ks[2], (L, DEC_BATCH, CONV_W - 1, QK_W), 1.0),
        'state_mlstm_c': nrm(ks[3], (L, DEC_BATCH, A_HEADS, A_DV, A_DQK), 0.5),
        'state_mlstm_n': nrm(ks[4], (L, DEC_BATCH, A_HEADS, A_DQK), 0.5),
        'state_mlstm_m': nrm(ks[5], (L, DEC_BATCH, A_HEADS), 1.0),
        'state_s5_re': nrm(ks[6], (L, DEC_BATCH, B_GROUPS, B_STATE), 0.5),
        'state_s5_im': nrm(ks[7], (L, DEC_BATCH, B_GROUPS, B_STATE), 0.5),
        'g_pre_mix': 1.0 + nrm(ks[8], (L, D_MODEL), 0.02),
        'w_in': nrm(ks[9], (L, D_MODEL, N_IN), D_MODEL ** -0.5),
        'w_conv': nrm(ks[10], (L, CONV_W, QK_W), CONV_W ** -0.5),
        'b_conv': nrm(ks[11], (L, QK_W), 0.02),
        'b_igate': nrm(ks[12], (L, A_HEADS), 0.1),
        'b_fgate': jnp.linspace(3.0, 6.0, A_HEADS, dtype=f32)[None] + nrm(ks[13], (L, A_HEADS), 0.1),
        'g_mh': 1.0 + nrm(ks[14], (L, D_A), 0.02),
        's5_lam_re': -0.5 + nrm(ks[15], (L, B_GROUPS, B_STATE), 0.01),
        's5_lam_im': math.pi * n_idx + nrm(ks[16], (L, B_GROUPS, B_STATE), 0.01),
        's5_log_dt': jax.random.uniform(ks[17], (L, B_GROUPS), f32, math.log(1e-3), math.log(1e-1)),
        's5_b_re': nrm(ks[18], (L, B_GROUPS, B_STATE, B_GROUP), (2 * B_GROUP) ** -0.5),
        's5_b_im': nrm(ks[19], (L, B_GROUPS, B_STATE, B_GROUP), (2 * B_GROUP) ** -0.5),
        's5_c_re': nrm(ks[20], (L, B_GROUPS, B_GROUP, B_STATE), B_STATE ** -0.5),
        's5_c_im': nrm(ks[21], (L, B_GROUPS, B_GROUP, B_STATE), B_STATE ** -0.5),
        's5_d': nrm(ks[22], (L, D_B), 1.0),
        'w_glu': nrm(ks[23], (L, D_B, D_B), D_B ** -0.5),
        'b_glu': nrm(ks[24], (L, D_B), 0.02),
        'w_out': nrm(ks[25], (L, D_MIX, D_MODEL), D_MIX ** -0.5),
        'g_post_mix': 1.0 + nrm(ks[26], (L, D_MODEL), 0.02),
        'g_pre_ffn': 1.0 + nrm(ks[27], (L, D_MODEL), 0.02),
        'w_gate': nrm(ks[28], (L, D_MODEL, D_FF), D_MODEL ** -0.5),
        'w_up': nrm(ks[29], (L, D_MODEL, D_FF), D_MODEL ** -0.5),
        'w_down': nrm(ks[30], (L, D_FF, D_MODEL), D_FF ** -0.5),
        'g_post_ffn': 1.0 + nrm(ks[31], (L, D_MODEL), 0.02),
    }

def reference(x_prompt, x_sample, state_conv, state_mlstm_c, state_mlstm_n, state_mlstm_m,
              state_s5_re, state_s5_im, g_pre_mix, w_in, w_conv, b_conv, b_igate, b_fgate,
              g_mh, s5_lam_re, s5_lam_im, s5_log_dt, s5_b_re, s5_b_im, s5_c_re, s5_c_im,
              s5_d, w_glu, b_glu, w_out, g_post_mix, g_pre_ffn, w_gate, w_up, w_down,
              g_post_ffn):
    f32 = jnp.float32
    yp = x_prompt
    ys = x_sample
    bp = x_prompt.shape[0]
    new_p = [[] for _ in range(6)]
    new_s = [[] for _ in range(6)]
    for l in range(DEPTH):
        lb_re, lb_im, bb_re, bb_im = s5_discretise(s5_lam_re[l], s5_lam_im[l], s5_log_dt[l],
                                                   s5_b_re[l], s5_b_im[l])
        p = {
            'g_pre_mix': g_pre_mix[l], 'w_in': w_in[l], 'w_conv': w_conv[l], 'b_conv': b_conv[l],
            'b_igate': b_igate[l], 'b_fgate': b_fgate[l], 'g_mh': g_mh[l],
            'lb_re': lb_re, 'lb_im': lb_im, 'bb_re': bb_re, 'bb_im': bb_im,
            's5_c_re': s5_c_re[l], 's5_c_im': s5_c_im[l], 's5_d': s5_d[l],
            'w_glu': w_glu[l], 'b_glu': b_glu[l], 'w_out': w_out[l], 'g_post_mix': g_post_mix[l],
            'g_pre_ffn': g_pre_ffn[l], 'w_gate': w_gate[l], 'w_up': w_up[l], 'w_down': w_down[l],
            'g_post_ffn': g_post_ffn[l],
        }
        yp, st_p = layer(yp,
                         jnp.zeros((bp, CONV_W - 1, QK_W), yp.dtype),
                         jnp.zeros((bp, A_HEADS, A_DV, A_DQK), f32),
                         jnp.zeros((bp, A_HEADS, A_DQK), f32),
                         jnp.zeros((bp, A_HEADS), f32),
                         jnp.zeros((bp, B_GROUPS, B_STATE), f32),
                         jnp.zeros((bp, B_GROUPS, B_STATE), f32),
                         p)
        ys, st_s = layer(ys, state_conv[l], state_mlstm_c[l], state_mlstm_n[l], state_mlstm_m[l],
                         state_s5_re[l], state_s5_im[l], p)
        for i in range(6):
            new_p[i].append(st_p[i])
            new_s[i].append(st_s[i])
    conv_p, c_p, n_p, m_p, s5re_p, s5im_p = [jnp.stack(a) for a in new_p]
    conv_s, c_s, n_s, m_s, s5re_s, s5im_s = [jnp.stack(a) for a in new_s]
    return (yp, ys, conv_p, c_p, n_p, m_p, s5re_p, s5im_p,
            conv_s, c_s, n_s, m_s, s5re_s, s5im_s)


_drawn_inputs = setup_inputs


def setup_inputs(seed=0):
    import zlib

    import numpy as np

    out = dict(_drawn_inputs(seed))
    spreads = {}
    factors = {'g_mh': 4.216,
     's5_lam_re': 16.143,
     'b_glu': 29.92,
     'g_post_mix': 3.5,
     'g_pre_ffn': 3.394,
     'g_post_ffn': 17.723}
    for name, (base, spread) in spreads.items():
        noise = np.random.default_rng([zlib.crc32(name.encode()), seed]).standard_normal(out[name].shape)
        drawn = base * np.exp(spread * noise) if base else spread * noise
        out[name] = jnp.asarray(drawn.astype(out[name].dtype))
    for name, factor in factors.items():
        out[name] = (out[name] * factor).astype(out[name].dtype)
    return out
```

```python
from contextlib import ExitStack

import numpy as np

import concourse.bass as bass
from concourse import mybir
from concourse.alu_op_type import AluOpType as ALU

F32 = mybir.dt.float32
F32R = mybir.dt.float32r
ACT = mybir.ActivationFunctionType
AX = mybir.AxisListType

P = 128
D = 2048
KT = D // P
SEQ, NB, DSEQ = 512, 8, 16
TT = (SEQ + NB * DSEQ) // P
T = TT * P
HALF = T // 2
SAMPLE = SEQ // P
H, DV, DQK = 4, 256, 128
VA1 = DV + 1
QK = 2 * H * DQK
DA = H * DV
DB = D - DA
CONV = 4
HIST = CONV - 1
G, GI, NS = 64, 16, 64
PAIRS = G // 2
FR = P // GI
STEPS = T // FR
PSTEPS = SEQ // FR
BP = 4
BLOCKS = PAIRS // BP
DFF = 5632
FB = 512
NFB = DFF // FB
EPS = 1e-6
UNIT = 2048
U_S5, U_QK, U_V, U_OG = 0, 8, 16, 24
U_GLU, U_OUT, U_FFN = 32, 36, 52
N_UNITS = U_FFN + 12 * NFB
COL_V, COL_OG, COL_GATE, COL_U = QK, QK + DA, QK + 2 * DA, QK + 2 * DA + 2 * H
MASKED = -1.0e30
ROUND = 12582912.0
TWO_PI = 2.0 * np.pi
PI2_A = 6.28125
PI2_B = float(np.float32(np.floor((TWO_PI - PI2_A) * 2.0**20) / 2.0**20))
PI2_C = float(np.float32(TWO_PI - PI2_A - PI2_B))
KB = 1024

R_CONV, R_BCONV, R_BGLU, R_GMH, R_S5D, R_HIST = 0, 4, 5, 6, 7, 8
NROWS = R_HIST + NB * HIST


def build(nc, a, o):
    base = nc.sbuf_base + (-nc.sbuf_base) % 32
    CONST, RING, R1, R2 = 0, 7 * KB, 55 * KB, 135 * KB

    def at(name, shape, offset, dtype=F32):
        return nc.alloc_sbuf_tensor_at(name, shape, dtype, offset=base + offset)

    place = [CONST]

    def const(name, shape, dtype=F32):
        t = at(name, shape, place[0], dtype)
        place[0] += -(-int(np.prod(shape[1:])) * 4 // 32) * 32
        assert place[0] <= 7 * KB, place[0]
        return t

    ident = const("ident", [P, P])
    mask_prompt = const("mask_prompt", [P, P])
    mask_sample = const("mask_sample", [P, P])
    chan = const("chan", [P, 8, NROWS])
    conv_tail = const("conv_tail", [P, 8, 27])
    gate_tok = const("gate_tok", [P, TT, 8])
    gate_w_hi = const("gate_w_hi", [P, KT, 8], F32R)
    gate_w_lo = const("gate_w_lo", [P, KT, 8], F32R)
    diag16 = const("diag16", [P, GI])
    n0 = const("n0", [P, NB, H])
    n_new = const("n_new", [P, NB, H])
    exp_neg_m = const("exp_neg_m", [P, TT, H])
    stat = const("stat", [P, 8, 20])
    bgate = const("bgate", [4, 2])
    m0s = const("m0s", [4, NB])
    decay = const("decay", [P, H, NB])
    vec = const("vec", [P, NROWS])

    raw = [at(f"raw{s}", [P, UNIT], RING + 8 * KB * s) for s in range(2)]
    w_hi = [at(f"w_hi{s}", [P, UNIT], RING + 16 * KB + 8 * KB * s, F32R) for s in range(2)]
    w_lo = [at(f"w_lo{s}", [P, UNIT], RING + 32 * KB + 8 * KB * s, F32R) for s in range(2)]

    xt_hi = at("xt_hi", [P, KT, T], R1, F32R)
    xt_lo = at("xt_lo", [P, KT, T], R1 + 40 * KB, F32R)
    qk = at("qk", [P, 8, T], R2)
    junk = at("junk", [P, D], R2)
    va = at("va", [P, TT, H, VA1], R2 + 20 * KB)
    xrow = [at(f"xrow{s}", [P, D], R2 + (41 + 8 * s) * KB) for s in range(2)]
    gbc = at("gbc", [P, D], R2 + 57 * KB)
    cn = at("cn", [P, 2, 8, NS], R2 + 67 * KB + 512)
    rows_in = at("rows_in", [NROWS, QK], R2 + 20 * KB)
    dis = at("dis", [PAIRS, 16, P], R2 + 24 * KB)
    ldt = at("ldt", [PAIRS, 2, 2], R2 + 32 * KB)
    b_in = at("b_in", [P, 2, PAIRS, GI], R2 + 33 * KB)
    n_in = at("n_in", [NB * H, P], R2 + 37 * KB)
    fct = at("fct", [P, 2, PAIRS], R2 + 37 * KB + 512)
    gate_w = at("gate_w", [P, KT, 8], R2 + 38 * KB)
    stmp = at("stmp", [P, 2, PAIRS, GI], R2 + 8 * KB)
    u_out = [at(f"u_out{s}", [P, FR, STEPS], R2 + 41 * KB + 2560 * s) for s in range(2)]
    conv_in = [at(f"conv_in{s}", [P, HIST + SEQ + NB * (HIST + DSEQ)], R2 + 46 * KB + 2688 * s)
               for s in range(2)]
    og_out = [at(f"og_out{s}", [P, 512], R2 + 51 * KB + 512 + 2048 * s) for s in range(2)]
    bbar = at("bbar", [P, 2, PAIRS, GI], R2 + 57 * KB)
    c0t = at("c0t", [P, 2, PAIRS, GI], R2 + 61 * KB)
    lbp = at("lbp", [P, 2, PAIRS, FR + 1], R2 + 65 * KB)
    conv_acc = at("conv_acc", [P, T], R2 + 67 * KB + 512)

    u_in = at("u_in", [P, G, STEPS], R1)
    sst = at("sst", [P, 2, PAIRS, STEPS], R1 + 20 * KB)
    fin = at("fin", [P, 2, 1 + NB, PAIRS], R1 + 40 * KB)
    Q = R1 + 42 * KB + 256
    bpw = at("bpw", [P, 2, BP, P], Q)
    bwt = at("bwt", [P, 2, BP, P], Q + 4 * KB)
    cpw = [at(f"cpw{s}", [P, 2, BP, (FR + 1) * GI], Q + 8 * KB + 4608 * s) for s in range(2)]
    kpad = at("kpad", [P, 15 * GI], Q + 17 * KB)
    bdiag = at("bdiag", [P, 2, BP, 2 * GI], Q + 18 * KB)
    toep = [at(f"toep{s}", [P, 8, P], Q + 19 * KB + 4 * KB * s) for s in range(2)]
    tail_out = at("tail_out", [27, QK], Q + 19 * KB)
    y_out = [at(f"y_out{s}", [P, BP, 2, STEPS], Q + 27 * KB + 2560 * s) for s in range(2)]
    stream_tmp = [at(f"stream_tmp{s}", [P, 2, PAIRS, NB], Q + 27 * KB + 2560 * s) for s in range(2)]
    ctmp = at("ctmp", [P, BP, (FR + 1) * GI], Q + 32 * KB)
    btmp = at("btmp", [P, BP, P], Q + 34 * KB + 256)
    scan_tmp = at("scan_tmp", [P, 2, 2, PAIRS], Q + 36 * KB + 256)
    lam8 = at("lam8", [P, 2, 2, PAIRS], Q + 36 * KB + 768)
    s5_io = at("s5_io", [P, 2, 2, P], RING + 46 * KB)
    s5p_out = at("s5p_out", [PAIRS, 2, P], R2 + 56 * KB)
    np_out = at("np_out", [H, P], RING + 45 * KB)
    ns_out = at("ns_out", [NB * H, P], RING + 45 * KB + 512)
    g_rows = [at(f"g_rows{s}", [4, T], R2 + 41 * KB + 2560 * s) for s in range(6)]
    r_a, r_b, r_g, r_m, r_li, r_lf = g_rows
    t_rows = [at(f"t_rows{s}", [4, T], RING + 30 * KB + 2560 * s) for s in range(4)]
    qgm = at("qgm", [P, 1152], R2 + 67 * KB + 384)
    ct = at("ct", [P, H, VA1], RING)
    hraw = [at(f"hraw{s}", [P, H, VA1], RING + 4128 * (s + 1)) for s in range(2)]
    dt = at("dt", [P, H, P], RING + 12 * KB + 512)
    pt = at("pt", [P, H, P], RING + 14 * KB + 512)
    qg = at("qg", [P, H, P], RING + 16 * KB + 512)
    kw = at("kw", [P, H, P], RING + 18 * KB + 512)
    ksb = at("ksb", [P, H, P], RING + 20 * KB + 512)
    sel = at("sel", [4, 4, P], RING + 22 * KB + 512)
    kwall = at("kwall", [P, NB, P], RING + 24 * KB + 512)
    cts = at("cts", [P, NB, VA1], RING + 28 * KB + 512)
    c0n = [at("c0n0", [P, 2, NB, P], Q), at("c0n1", [P, 2, NB, P], RING + 37 * KB)]
    cp_out = at("cp_out", [P, 2 * H, P], RING + 4128 * 2)

    ot_hi = at("ot_hi", [P, KT, T], R1, F32R)
    ot_lo = at("ot_lo", [P, KT, T], R1 + 40 * KB, F32R)
    z_hi = at("z_hi", [P, 8, T], R2, F32R)
    z_lo = at("z_lo", [P, 8, T], R2 + 20 * KB, F32R)
    z = at("z", [P, 8, T], R2 + 40 * KB)
    oa = at("oa", [P, H, VA1], R2 + 60 * KB)
    og_in = at("og_in", [P, H, DV], R2 + 60 * KB + 4128)
    ob = at("ob", [P, T], R2 + 68 * KB + 512)
    sq_out = at("sq_out", [P, DV], R2 + 71 * KB)
    mix = at("mix", [P, TT, D], R2)
    g_post = at("g_post", [P, D], R2 + 40 * KB)
    g_ffn = at("g_ffn", [P, D], R2 + 48 * KB)
    xres = [at(f"xres{s}", [P, D], R2 + (56 + 8 * s) * KB) for s in range(2)]
    ht_hi = at("ht_hi", [P, KT, T], R1, F32R)
    ht_lo = at("ht_lo", [P, KT, T], R1 + 40 * KB, F32R)
    acc = at("acc", [P, TT, D], R2)
    h_hi = at("h_hi", [P, 4, T], R2 + 40 * KB, F32R)
    h_lo = at("h_lo", [P, 4, T], R2 + 50 * KB, F32R)
    sg = at("sg", [P, 2, HALF], R2 + 60 * KB)
    hid = at("hid", [P, 2, HALF], R2 + 62 * KB + 512)
    g_last = at("g_last", [P, D], R1 + 16 * KB)
    xlast = [at(f"xlast{s}", [P, D], R1 + 8 * s * KB) for s in range(2)]

    def dram(name, shape):
        return nc.dram_tensor(name, shape, F32, kind="Internal").ap()

    u_dram = dram("u_dram", (DB, T))
    y_dram = dram("y_dram", (DB, T))
    og_dram = dram("og_dram", (T, DA))
    oa_dram = dram("oa_dram", (T, H * VA1))
    k_dram = dram("k_dram", (BLOCKS, P, 15 * GI))
    x_dram = dram("x_dram", (T, D))

    with ExitStack() as ctx:
        psum = ctx.enter_context(nc.psum_tensor("psum", [P, 8, 512], F32))

        def sem(name):
            return ctx.enter_context(nc.semaphore(name))

        raw_loaded = [sem(f"raw_loaded{s}") for s in range(2)]
        hi_ready, lo_ready = sem("hi_ready"), sem("lo_ready")
        pe_done = sem("pe_done")
        const_ready = sem("const_ready")
        x_loaded = [sem(f"x_loaded{s}") for s in range(2)]
        g_loaded, small_loaded = sem("g_loaded"), sem("small_loaded")
        ssq_ready, mean_ready, root_ready = sem("ssq_ready"), sem("mean_ready"), sem("root_ready")
        normed = sem("normed")
        tr_done, tr_hi, tr_lo = sem("tr_done"), sem("tr_hi"), sem("tr_lo")
        dve_chain, act_chain, pool_chain = sem("dve_chain"), sem("act_chain"), sem("pool_chain")
        dis_act, dis_dve = sem("dis_act"), sem("dis_dve")
        small_tr, small_ev = sem("small_tr"), sem("small_ev")
        gate_w_ready, gates_done, gate_tok_ready = (
            sem("gate_w_ready"), sem("gates_done"), sem("gate_tok_ready"))
        s5_consts = sem("s5_consts")
        bank_free = sem("bank_free")
        tok_evac = sem("tok_evac")
        u_evac, u_stored = sem("u_evac"), [sem(f"u_stored{s}") for s in range(2)]
        conv_filled = sem("conv_filled")
        conv_read = sem("conv_read")
        conv_step, conv_summed, silu_done = sem("conv_step"), sem("conv_summed"), sem("silu_done")
        og_stored = [sem(f"og_stored{s}") for s in range(2)]
        ones_ready = sem("ones_ready")
        u_loaded, s5_in = sem("u_loaded"), sem("s5_in")
        row_done, row_act, row_dve = sem("row_done"), sem("row_act"), sem("row_dve")
        tail_done, tail_ev, tail_stored = sem("tail_done"), sem("tail_ev"), sem("tail_stored")
        s5_state_tr, s5_state_in = sem("s5_state_tr"), sem("s5_state_in")
        bpw_ready, bwt_done, bwt_ready = sem("bpw_ready"), sem("bwt_done"), sem("bwt_ready")
        v_done, v_evac = sem("v_done"), sem("v_evac")
        cpw_ready, bdiag_ready = sem("cpw_ready"), sem("bdiag_ready")
        k_done, k_ready, k_stored = sem("k_done"), sem("k_ready"), sem("k_stored")
        scan_step, scan_done = sem("scan_step"), sem("scan_done")
        toep_loaded = [sem(f"toep_loaded{s}") for s in range(2)]
        y_done, y_evac = sem("y_done"), sem("y_evac")
        y_stored = [sem(f"y_stored{s}") for s in range(2)]
        sel_ready, em_done, em_ready = sem("sel_ready"), sem("em_done"), sem("em_ready")
        arg_done, s_done, gb_done, kt_done = (
            sem("arg_done"), sem("s_done"), sem("gb_done"), sem("kt_done"))
        dt_ready, pt_ready, qg_ready, kw_ready, ksb_ready = (
            sem("dt_ready"), sem("pt_ready"), sem("qg_ready"), sem("kw_ready"), sem("ksb_ready"))
        num_done, num_evac, dc_done, ct_ready = (
            sem("num_done"), sem("num_evac"), sem("dc_done"), sem("ct_ready"))
        h_stored = [sem(f"h_stored{s}") for s in range(2)]
        c0_loaded = [sem(f"c0_loaded{s}") for s in range(2)]
        c0_stored = [sem(f"c0_stored{s}") for s in range(2)]
        ctr_done, cts_ready, un_done, c_new = (
            sem("ctr_done"), sem("cts_ready"), sem("un_done"), sem("c_new"))
        qgm_ready, kwall_ready, nn_done = sem("qgm_ready"), sem("kwall_ready"), sem("nn_done")
        fin_tr, fin_ev, out_stored = sem("fin_tr"), sem("fin_ev"), sem("out_stored")
        y_loaded, z_ready, z_hi_ready, z_lo_ready = (
            sem("y_loaded"), sem("z_ready"), sem("z_hi_ready"), sem("z_lo_ready"))
        oa_loaded, oa_sums, oa_mean, oa_root, oa_ready = (
            sem("oa_loaded"), sem("oa_sums"), sem("oa_mean"), sem("oa_root"), sem("oa_ready"))
        oat_done, oat_hi, oat_lo = sem("oat_done"), sem("oat_hi"), sem("oat_lo")
        gate_ready, ob_first, ob_ready, ob_hi, ob_lo = (
            sem("gate_ready"), sem("ob_first"), sem("ob_ready"), sem("ob_hi"), sem("ob_lo"))
        gp_loaded, xr_loaded = sem("gp_loaded"), [sem(f"xr_loaded{s}") for s in range(2)]
        xr_ready, xr_stored = sem("xr_ready"), [sem(f"xr_stored{s}") for s in range(2)]
        acc_zero, sg_ready, hid_ready, h_hi_ready, h_lo_ready = (
            sem("acc_zero"), sem("sg_ready"), sem("hid_ready"), sem("h_hi_ready"), sem("h_lo_ready"))
        last_loaded = [sem(f"last_loaded{s}") for s in range(2)]
        y_ready, res_stored = sem("y_ready"), sem("res_stored")
        def step_slices(tile):
            if tile < SAMPLE:
                return a["x_prompt"][0, P * tile:P * (tile + 1), :]
            return a["x_sample"].rearrange("b t d -> (b t) d")

        w_in, w_glu, w_out = a["w_in"][0], a["w_glu"][0], a["w_out"][0]
        w_gate, w_up, w_down = a["w_gate"][0], a["w_up"][0], a["w_down"][0]

        def cols_of(w, col, width=P):
            return w[:, bass.ds(col, width)].rearrange("(k p) n -> p k n", p=P)

        def rows_of(w, row, col):
            return w[bass.ds(row, 4 * P), bass.ds(col, 512)].rearrange("(k p) n -> p k n", p=P)

        def as_unit(t, k):
            return t[:].rearrange("p (k n) -> p k n", k=k)

        def streams(t):
            return t[:, HIST + SEQ:].rearrange("p (b s) -> p b s", b=NB)

        def output_powers(eng, after, k):
            pairs = slice(BP * k, BP * (k + 1))
            shape = [P, BP, FR + 1, GI]
            lr, li = (lbp[:, r, pairs, :].unsqueeze(3).to_broadcast(shape) for r in range(2))
            cr, ci = (c0t[:, r, pairs, :].unsqueeze(2).to_broadcast(shape) for r in range(2))
            dst = [cpw[k % 2][:, r, :, :].rearrange("p q (k i) -> p q k i", i=GI) for r in range(2)]
            tmp = ctmp[:].rearrange("p q (k i) -> p q k i", i=GI)
            eng.tensor_tensor(dst[0], lr, cr, ALU.mult)
            after(eng.tensor_tensor(tmp, li, ci, ALU.mult))
            after(eng.tensor_tensor(dst[0], dst[0], tmp, ALU.add))
            eng.tensor_tensor(dst[1], lr, ci, ALU.mult)
            after(eng.tensor_tensor(tmp, li, cr, ALU.mult))
            return eng.tensor_tensor(dst[1], dst[1], tmp, ALU.subtract)

        s5_c = {0: a["s5_c_re"], 1: a["s5_c_im"]}
        s5_b = {0: a["s5_b_re"], 1: a["s5_b_im"]}
        s5_state = {0: a["state_s5_re"], 1: a["state_s5_im"]}
        N_SMALL = 18
        block = ctx.enter_context(nc.Block())

        OUT_SMALL = 9

        def store_y(sp, t):
            dst = (o["y_prompt"][0, P * t:P * (t + 1), :] if t < SAMPLE else
                   o["y_sample"].rearrange("b t d -> (b t) d"))
            sp.wait_ge(y_ready, t + 1)
            sp.dma_start(dst, xlast[t % 2][:]).then_inc(res_stored, 16)

        @block.sync
        def _(sp):
            def load(n, s, src, k):
                sp.wait_ge(lo_ready, n - 1)
                sp.dma_start(as_unit(raw[s], k), src).then_inc(raw_loaded[s], 16)

            for s in range(2):
                sp.dma_start(as_unit(raw[s], KT), cols_of(w_in, COL_U + P * s)).then_inc(raw_loaded[s], 16)
            with sp.Fori(1, 4) as i:
                for j in range(2):
                    load(2 * i + j, j, cols_of(w_in, 2 * P * i + (COL_U + P * j)), KT)
            with sp.Fori(0, 4) as i:
                for j in range(2):
                    load(2 * i + (U_QK + j), j, cols_of(w_in, 2 * P * i + P * j), KT)
            with sp.Fori(0, 4) as i:
                for j in range(4):
                    load(4 * i + (U_V + j), j % 2, rows_of(w_in, 4 * P * j, 512 * i + COL_V), 4)
            sp.wait_ge(pe_done, 5 * U_GLU)
            for s in range(2):
                sp.wait_ge(u_stored[s], 16 * 4)
            for r in range(FR):
                sp.dma_start(u_in[GI * (7 - r):GI * (8 - r), :, :],
                             u_dram[:, STEPS * r:STEPS * (r + 1)].rearrange("(g i) c -> i g c", i=GI)
                             ).then_inc(u_loaded, 16)
            for r in range(2):
                sp.dma_start(s5_io[:, r, :, :],
                             s5_state[r][0].rearrange("b (a g) p -> (b a) (g p)", g=2)
                             .rearrange("(q x) p -> x q p", q=2)).then_inc(s5_in, 16)
            for k in range(BLOCKS):
                sp.wait_ge(k_ready, 2 * k + 2)
                sp.dma_start(k_dram[k], kpad[:]).then_inc(k_stored, 16)

            def head_state(x, h, v):
                return x[0, :, h].rearrange("b (v p) d -> v p b d", v=2)[v]

            def load_c0(h):
                for v in range(2):
                    sp.dma_start(c0n[h % 2][:, v, :, :], head_state(a["state_mlstm_c"], h, v)
                                 ).then_inc(c0_loaded[h % 2], 16)

            def load_toep(k):
                sp.wait_ge(k_stored, 16 * (k + 1))
                for r in range(FR):
                    sp.dma_start(toep[k % 2][GI * r:GI * (r + 1), :, :],
                                 k_dram[k].rearrange("(g j) c -> j g c", j=GI)[:, :, GI * r:GI * r + P]
                                 ).then_inc(toep_loaded[k % 2], 16)

            sp.wait_ge(v_done, BLOCKS)
            sp.wait_ge(row_act, 4)
            load_c0(0)
            load_c0(1)
            sp.wait_ge(tail_stored, 32)
            load_toep(0)
            load_toep(1)
            for h in range(H):
                sp.wait_ge(c_new, 4 * (h + 1))
                for v in range(2):
                    sp.dma_start(head_state(o["c_s"], h, v), c0n[h % 2][:, v, :, :]
                                 ).then_inc(c0_stored[h % 2], 16)
                if h + 2 < H:
                    sp.wait_ge(c0_stored[h % 2], 32)
                    load_c0(h + 2)
            for k in range(BLOCKS):
                sp.wait_ge(y_evac, 2 * k + 2)
                for t in range(FR):
                    sp.dma_start(
                        y_dram[P * k:P * (k + 1), STEPS * t:STEPS * (t + 1)].rearrange("(g i) c -> i g c", i=GI),
                        y_out[k % 2][GI * t:GI * (t + 1), :, :, :].rearrange("i q g c -> i (q g) c")
                    ).then_inc(y_stored[k % 2], 16)
                if k + 2 < BLOCKS:
                    sp.wait_ge(y_done, k + 1)
                    load_toep(k + 2)
            sp.wait_ge(ct_ready, H * TT)
            for s in range(2):
                sp.wait_ge(c0_stored[s], 64)
                sp.wait_ge(h_stored[s], 16 * (3 - s))
                sp.wait_ge(y_stored[s], 16 * FR * BLOCKS // 2)
            sp.wait_ge(out_stored, 16 * OUT_SMALL)
            sp.wait_ge(cpw_ready, 2 * BLOCKS)
            sp.dma_start(z[:], y_dram.rearrange("(k p) n -> p k n", p=P)).then_inc(y_loaded, 16)
            for j in range(2):
                load(U_GLU + j, j, cols_of(w_glu, 256 * j, 256), 8)

            def load_oa(t):
                rows = slice(P * t, P * (t + 1))
                sp.dma_start(oa[:].rearrange("p h v -> p (h v)"), oa_dram[rows, :]).then_inc(oa_loaded, 16)
                sp.dma_start(og_in[:].rearrange("p h v -> p (h v)"), og_dram[rows, :]).then_inc(oa_loaded, 16)

            for s in range(2):
                sp.wait_ge(og_stored[s], 16 * TT)
            load_oa(0)
            for t in range(1, TT):
                if t < 3:
                    load(U_GLU + 1 + t, (t - 1) % 2, cols_of(w_glu, 256 * (t + 1), 256), 8)
                else:
                    load(U_OUT + t - 3, (t - 1) % 2, rows_of(w_out, 4 * P * (t - 3), 0), 4)
                sp.wait_ge(oat_done, 2 * t)
                load_oa(t)
            for j in range(2, 4):
                load(U_OUT + j, j % 2, rows_of(w_out, 4 * P * j, 0), 4)
            with sp.Fori(1, 4) as i:
                for j in range(4):
                    load(4 * i + (U_OUT + j), j % 2, rows_of(w_out, 4 * P * j, 512 * i), 4)
            for s in range(2):
                sp.dma_start((g_post, g_ffn)[s][:], a[("g_post_mix", "g_pre_ffn")[s]].broadcast_to((P, D))
                             ).then_inc(gp_loaded, 16)
            for t in range(TT):
                if t >= 2:
                    sp.wait_ge(normed, TT + t - 1)
                    sp.wait_ge(xr_stored[t % 2], 16 * (t // 2))
                sp.dma_start(xres[t % 2][:], step_slices(t)).then_inc(xr_loaded[t % 2], 16)
                if t == 0:
                    load(U_FFN, 0, cols_of(w_gate, 0), KT)
                    load(U_FFN + 1, 1, cols_of(w_up, 0), KT)
            for j in range(2, 8):
                load(U_FFN + j, j % 2, cols_of((w_gate, w_up)[j % 2], P * (j // 2)), KT)
            for j in range(4):
                load(U_FFN + 8 + j, j % 2, rows_of(w_down, 0, 512 * j), 4)
            with sp.Fori(1, NFB) as i:
                for j in range(4):
                    load(12 * i + (U_FFN + 2 * j), 0, cols_of(w_gate, FB * i + P * j), KT)
                    load(12 * i + (U_FFN + 2 * j + 1), 1, cols_of(w_up, FB * i + P * j), KT)
                for j in range(4):
                    load(12 * i + (U_FFN + 8 + j), j % 2, rows_of(w_down, FB * i, 512 * j), 4)
            sp.wait_ge(pe_done, 5 * (N_UNITS - 4))
            sp.dma_start(g_last[:], a["g_post_ffn"].broadcast_to((P, D))).then_inc(gp_loaded, 16)
            for t in range(TT):
                if t >= 2:
                    sp.wait_ge(res_stored, 16 * (t - 1))
                sp.dma_start(xlast[t % 2][:], x_dram[P * t:P * (t + 1), :]).then_inc(last_loaded[t % 2], 16)
                if t >= 1:
                    store_y(sp, t - 1)
            store_y(sp, TT - 1)
            sp.wait_ge(res_stored, 16 * TT)

        @block.tensor
        def _(pe):
            PARTS = ((0, 0), (0, 1), (1, 0))

            def transpose_rows(src, first):
                for q in range(4):
                    n = first + q
                    if n >= 4:
                        pe.wait_ge(tr_lo, n - 3)
                    for k in range(4):
                        m = pe.transpose(psum[:, q, P * k:P * (k + 1)],
                                         src[:, P * (4 * q + k):P * (4 * q + k + 1)], ident[:])
                    m.then_inc(tr_done, 1)

            def channel_unit(slot, bank, rows, kts=KT, part=0):
                w = (w_hi[slot], w_lo[slot])
                width = UNIT // kts
                for k in range(kts):
                    for wp in range(2):
                        lhs = w[wp][:, width * k + P * part:width * k + P * (part + 1)]
                        for rp in range(2 - wp):
                            for h in range(2):
                                m = pe.matmul(psum[:, bank + h, 0:HALF], lhs,
                                              rows[rp][:, k, HALF * h:HALF * (h + 1)],
                                              start=(k == 0 and wp == 0 and rp == 0),
                                              stop=(k == kts - 1 and wp == 1))
                return m

            def row_unit(slot, rows, k0, first, last):
                w = (w_hi[slot], w_lo[slot])
                for t in range(TT):
                    for k in range(4):
                        for wp, rp in PARTS:
                            m = pe.matmul(psum[:, t, :], rows[rp][:, k0 + k, P * t:P * (t + 1)],
                                          w[wp][:, 512 * k:512 * (k + 1)],
                                          start=(first and k == 0 and wp == 0 and rp == 0),
                                          stop=(last and k == 3 and wp == 1))
                    m.then_inc(pe_done, 1)

            xt = (xt_hi, xt_lo)
            pe.wait_ge(const_ready, 3)
            pe.wait_ge(small_loaded, 16 * N_SMALL)
            for c in range(8):
                pe.transpose(psum[:, 4, NROWS * c:NROWS * (c + 1)],
                             rows_in[:, P * c:P * (c + 1)], ident[0:NROWS, 0:NROWS])
            pe.transpose(psum[:, 4, 320:320 + NB * H], n_in[:], ident[0:NB * H, 0:NB * H]
                         ).then_inc(small_tr, 1)
            for r in range(2):
                for k in range(8):
                    for g in range(2):
                        m = pe.matmul(psum[64 * g:64 * g + 64, 5 + r, 64 * k:64 * (k + 1)], cn[:, r, k, :],
                                      ident[:].rearrange("p (a g i) -> p g a i", g=2, i=GI)[:, g],
                                      start=True, stop=True)
            m.then_inc(small_tr, 1)
            for t in range(TT):
                pe.wait_ge(normed, t + 1)
                transpose_rows(xrow[t % 2], 4 * t)
            pe.wait_ge(tr_lo, 4 * TT)
            for j in range(2):
                pe.wait_ge(lo_ready, j + 1)
                channel_unit(j, 2 * j, xt).then_inc(pe_done, 5)
            with pe.Fori(1, 4) as i:
                for j in range(2):
                    pe.wait_ge(lo_ready, 2 * i + (j + 1))
                    pe.wait_ge(bank_free, 2 * i + (j - 1))
                    channel_unit(j, 2 * j, xt).then_inc(pe_done, 5)
            pe.wait_ge(gate_w_ready, 1)
            pe.wait_ge(small_ev, 2)
            for t in range(TT):
                for k in range(KT):
                    for wp, rp in PARTS:
                        m = pe.matmul(psum[:, 5, 8 * t:8 * (t + 1)], xt[rp][:, k, P * t:P * (t + 1)],
                                      (gate_w_hi, gate_w_lo)[wp][:, k, :],
                                      start=(k == 0 and wp == 0 and rp == 0),
                                      stop=(k == KT - 1 and wp == 1))
            m.then_inc(gates_done, 1)
            pe.wait_ge(dis_dve, 2)
            for r in range(4):
                m = pe.transpose(psum[:, 6, PAIRS * r:PAIRS * (r + 1)], dis[:, r, :],
                                 ident[0:PAIRS, 0:PAIRS])
            m.then_inc(small_tr, 1)
            with pe.Fori(0, 4) as i:
                for j in range(2):
                    pe.wait_ge(lo_ready, 2 * i + (U_QK + j + 1))
                    pe.wait_ge(bank_free, 2 * i + (U_QK + j - 1))
                    channel_unit(j, 2 * j, xt).then_inc(pe_done, 5)
            pe.wait_ge(bank_free, 16)
            with pe.Fori(0, 4) as i:
                pe.wait_ge(tok_evac, 5 * i)
                for j in range(4):
                    pe.wait_ge(lo_ready, 4 * i + (U_V + j + 1))
                    row_unit(j % 2, xt, 4 * j, j == 0, j == 3)
            pe.wait_ge(small_ev, 3)
            for c in range(8):
                m = pe.transpose(psum[0:27, 6 + c // 4, P * (c % 4):P * (c % 4 + 1)],
                                 conv_tail[:, c, :], ident[:])
            m.then_inc(tail_done, 1)
            pe.wait_ge(tok_evac, 20)
            pe.wait_ge(gate_tok_ready, 1)
            for g in range(2):
                for t in range(TT):
                    m = pe.matmul(psum[0:4, 2 * g + t // 4, P * (t % 4):P * (t % 4 + 1)],
                                  gate_tok[:, t, 4 * g:4 * g + 4], ident[:], start=True, stop=True)
            m.then_inc(row_done, 1)
            pe.wait_ge(s5_in, 32)
            for r in range(2):
                for q in range(2):
                    m = pe.transpose(psum[:, 5, P * (2 * r + q):P * (2 * r + q + 1)], s5_io[:, r, q, :],
                                     ident[:])
            m.then_inc(s5_state_tr, 1)
            pe.wait_ge(u_loaded, 16 * FR)
            pe.wait_ge(tail_ev, 1)
            pe.wait_ge(row_act, 1)
            pe.wait_ge(s5_state_in, 2)
            for k in range(BLOCKS):
                pe.wait_ge(bpw_ready, k + 1)
                if k:
                    pe.wait_ge(bwt_ready, k)
                for r in range(2):
                    for q in range(BP):
                        m = pe.transpose(psum[:, 6 + r, P * q:P * (q + 1)], bpw[:, r, q, :], ident[:])
                m.then_inc(bwt_done, 1)
                pe.wait_ge(cpw_ready, k + 1)
                pe.wait_ge(bdiag_ready, 2 * k + 2)
                if k:
                    pe.wait_ge(k_ready, 2 * k)
                for q in range(BP):
                    for r in range(2):
                        m = pe.matmul(psum[32 * q:32 * q + 32, 3, 0:P], bdiag[:, r, q, :],
                                      cpw[k % 2][:, r, q, 0:P], start=(r == 0), stop=(r == 1))
                m.then_inc(k_done, 1)
                pe.wait_ge(bwt_ready, k + 1)
                if k:
                    pe.wait_ge(v_evac, k)
                for r in range(2):
                    for q in range(BP):
                        for g in range(2):
                            m = pe.matmul(psum[64 * g:64 * g + 64, 4 + r, STEPS * q:STEPS * (q + 1)],
                                          bwt[:, r, q, 64 * g:64 * g + 64],
                                          u_in[:, 2 * (BP * k + q) + g, :], start=True, stop=True)
                m.then_inc(v_done, 1)
            pe.wait_ge(v_evac, BLOCKS)
            pe.wait_ge(k_ready, 2 * BLOCKS)
            pe.wait_ge(ones_ready, 1)
            pe.wait_ge(sel_ready, 1)
            pe.wait_ge(row_dve, 3)
            for t in range(TT):
                m = pe.matmul(psum[:, 7, 4 * t:4 * t + 4], r_m[:, P * t:P * (t + 1)], ident[0:4, 0:4],
                              start=True, stop=True)
            m.then_inc(em_done, 1)
            pe.wait_ge(row_act, 4)
            pe.wait_ge(silu_done, 8)
            for t in range(TT):
                rows = slice(P * t, P * (t + 1))
                mask = mask_prompt if t < SAMPLE else mask_sample
                if t:
                    pe.wait_ge(ct_ready, H * t)
                for h in range(H):
                    cols = slice(P * h, P * (h + 1))
                    pe.matmul(psum[:, 0, cols], sel[:, h, :], r_a[:, rows], start=True, stop=False)
                    pe.matmul(psum[:, 0, cols], r_b[:, rows], sel[:, h, :], start=False, stop=False)
                    m = pe.matmul(psum[:, 0, cols], ident[:], mask[:], start=False, stop=True)
                m.then_inc(arg_done, 1)
                for h in range(H):
                    m = pe.matmul(psum[:, 1, P * h:P * (h + 1)], qk[:, H + h, rows], qk[:, h, rows],
                                  start=True, stop=True)
                m.then_inc(s_done, 1)
                for h in range(H):
                    m = pe.matmul(psum[:, 2, P * h:P * (h + 1)], sel[:, h, :], r_g[:, rows],
                                  start=True, stop=True)
                m.then_inc(gb_done, 1)
                for h in range(H):
                    m = pe.transpose(psum[:, 3, P * h:P * (h + 1)], qk[:, H + h, rows], ident[:])
                m.then_inc(kt_done, 1)
                pe.wait_ge(pt_ready, t + 1)
                pe.wait_ge(qg_ready, t + 1)
                if t < SAMPLE:
                    pe.wait_ge(kw_ready, t + 1)
                    pe.wait_ge(ct_ready, max(H * t, 0))
                    for h in range(H):
                        n = H * t + h
                        if n >= 2:
                            pe.wait_ge(num_evac, n - 1)
                        pe.matmul(psum[:, 4 + h % 2, 0:VA1], pt[:, h, :], va[:, t, h, :],
                                  start=True, stop=False)
                        pe.matmul(psum[:, 4 + h % 2, 0:VA1], qg[:, h, :], ct[:, h, :],
                                  start=False, stop=True).then_inc(num_done, 1)
                        pe.matmul(psum[:, h, 0:VA1], kw[:, h, :], va[:, t, h, :],
                                  start=True, stop=True).then_inc(dc_done, 1)
                    continue
                pe.wait_ge(ksb_ready, 1)
                for h in range(H):
                    for v in range(2):
                        m = pe.transpose(psum[:, h // 2, P * (2 * (h % 2) + v):P * (2 * (h % 2) + v + 1)],
                                         ct[:, h, P * v:P * (v + 1)], ident[:])
                m.then_inc(fin_tr, 1)
                pe.transpose(psum[0:4, 6, 0:P], ct[:, :, DV], ident[:]).then_inc(fin_tr, 1)
                pe.wait_ge(em_ready, 1)
                for h in range(H):
                    c0 = c0n[h % 2]
                    pe.wait_ge(c0_loaded[h % 2], 32 * (h // 2 + 1))
                    if h == 0:
                        pe.wait_ge(fin_ev, 1)
                    else:
                        pe.wait_ge(c_new, 4 * h)
                    for b in range(NB):
                        for v in range(2):
                            m = pe.transpose(
                                psum[:, b // 2, P * (2 * (b % 2) + v):P * (2 * (b % 2) + v + 1)],
                                c0[:, v, b, :], ident[:])
                        if b % 2:
                            m.then_inc(ctr_done, 1)
                    pe.wait_ge(num_evac, H * t + h - 1)
                    pe.matmul(psum[:, 4 + h % 2, 0:VA1], pt[:, h, :], va[:, t, h, :],
                              start=True, stop=False)
                    pe.wait_ge(qgm_ready, h + 1)
                    pe.wait_ge(cts_ready, 5 * (h + 1))
                    for b in range(NB):
                        m = pe.matmul(psum[:, 4 + h % 2, 0:VA1], qgm[:, P * b:P * (b + 1)],
                                      cts[:, b, :], start=False, stop=(b == NB - 1))
                    m.then_inc(num_done, 1)
                    pe.wait_ge(kwall_ready, h + 1)
                    for v in range(2):
                        for q in range(2):
                            pe.matmul(psum[:, 2 * v + q, :], va[:, t, h, P * v:P * (v + 1)],
                                      kwall[:, 4 * q:4 * q + 4, :], start=True,
                                      stop=True).then_inc(un_done, 1)
                    if h:
                        pe.wait_ge(ct_ready, H * t + h)
                    pe.matmul(psum[:, 7, NB * h:NB * (h + 1)], ksb[:, h, :],
                              dt[:, h, DSEQ - 1::DSEQ], start=True, stop=True).then_inc(nn_done, 1)
            pe.wait_ge(ct_ready, H * TT)
            pe.wait_ge(fin_ev, 2)
            pe.transpose(psum[0:NB * H, 6, P:2 * P], n_new[:].rearrange("p b h -> p (b h)"),
                         ident[:]).then_inc(fin_tr, 1)
            pe.wait_ge(scan_done, 1)
            pe.wait_ge(c_new, 4 * H)
            for r in range(2):
                m = pe.transpose(psum[0:PAIRS, 0, P * r:P * (r + 1)], fin[:, r, 0, :], ident[:])
            m.then_inc(fin_tr, 1)
            for r in range(2):
                for q in range(2):
                    m = pe.transpose(
                        psum[:, 1, P * (2 * r + q):P * (2 * r + q + 1)],
                        fin[:, r, 1 + 4 * q:5 + 4 * q, :].rearrange("p b a -> p (b a)"), ident[:])
            m.then_inc(fin_tr, 1)
            pe.wait_ge(num_evac, H * TT)
            for k in range(BLOCKS):
                pe.wait_ge(cpw_ready, BLOCKS + k + 1)
                pe.wait_ge(toep_loaded[k % 2], 16 * FR * (k // 2 + 1))
                banks = (2, 3) if k % 2 else (4, 5)
                if k >= 2:
                    pe.wait_ge(y_evac, 2 * (k - 1))
                for q in range(BP):
                    for g in range(2):
                        out = psum[:, banks[g], STEPS * q:STEPS * (q + 1)]
                        states = slice(64 * g, 64 * g + 64)
                        pe.matmul(out, toep[k % 2][:, 2 * q + g, :], u_in[:, 2 * (BP * k + q) + g, :],
                                  start=True, stop=False)
                        for r in range(2):
                            m = pe.matmul(out, cpw[k % 2][states, r, q, GI:],
                                          sst[states, r, BP * k + q, :], start=False, stop=(r == 1))
                m.then_inc(y_done, 1)
            def mlstm_to_channels(t):
                pe.wait_ge(oa_ready, t + 1)
                for q in range(2):
                    n = 2 * t + q
                    if n >= 4:
                        pe.wait_ge(oat_lo, n - 3)
                    for k in range(4):
                        m = pe.transpose(psum[:, 4 + n % 4, P * k:P * (k + 1)],
                                         og_in[:, 2 * q + k // 2, P * (k % 2):P * (k % 2 + 1)], ident[:])
                    m.then_inc(oat_done, 1)

            pe.wait_ge(z_lo_ready, 8)
            pe.wait_ge(y_evac, 2 * BLOCKS)
            pe.wait_ge(fin_ev, 5)
            for j in range(4):
                pe.wait_ge(lo_ready, U_GLU + j + 1)
                for c in range(2):
                    if 2 * j + c >= 2:
                        pe.wait_ge(ob_ready, 2 * j + c - 1)
                    channel_unit(j % 2, 2 * c, (z_hi, z_lo), 8, c).then_inc(pe_done, 2 + c)
                mlstm_to_channels(j)
            mlstm_to_channels(TT - 1)
            pe.wait_ge(ob_lo, 8)
            pe.wait_ge(oat_lo, 2 * TT)
            with pe.Fori(0, 4) as i:
                pe.wait_ge(tok_evac, 5 * i + 20)
                for j in range(4):
                    pe.wait_ge(lo_ready, 4 * i + (U_OUT + j + 1))
                    row_unit(j % 2, (ot_hi, ot_lo), 4 * j, j == 0, j == 3)
            pe.wait_ge(tok_evac, 40)
            for t in range(TT):
                pe.wait_ge(normed, TT + t + 1)
                transpose_rows(mix[:, t, :], 4 * TT + 4 * t)
            pe.wait_ge(tr_lo, 8 * TT)
            BANKS = [q % 8 if q < 16 else q - 12 for q in range(20)]
            with pe.Fori(0, NFB) as i:
                for p in range(4):
                    if p == 0:
                        pe.wait_ge(tok_evac, 20 * i + 32)
                    elif p == 1:
                        pe.wait_ge(tok_evac, 20 * i + 40)
                    else:
                        pe.wait_ge(hid_ready, 8 * i + 2 * (p - 1))
                    for j in range(2):
                        pe.wait_ge(lo_ready, 12 * i + (U_FFN + 2 * p + j + 1))
                        channel_unit(j, 4 * (p % 2) + 2 * j, (ht_hi, ht_lo)).then_inc(pe_done, 5)
                for j in range(4):
                    pe.wait_ge(lo_ready, 12 * i + (U_FFN + 8 + j + 1))
                    w = (w_hi[j % 2], w_lo[j % 2])
                    for t in range(TT):
                        q = TT * j + t
                        if q == 0:
                            pe.wait_ge(h_lo_ready, 8 * i + 6)
                        elif q == 4:
                            pe.wait_ge(hid_ready, 8 * i + 8)
                        elif q >= 8:
                            pe.wait_ge(tok_evac, 20 * i + (40 + (q - 8 if q < 16 else q - 4) + 1))
                        for k in range(4):
                            if j == 0 and k == 3 and t == 0:
                                pe.wait_ge(h_lo_ready, 8 * i + 7)
                            if j == 0 and k == 3 and t == 2:
                                pe.wait_ge(h_lo_ready, 8 * i + 8)
                            for wp, rp in PARTS:
                                m = pe.matmul(psum[:, BANKS[q], :],
                                              (h_hi, h_lo)[rp][:, k, P * t:P * (t + 1)],
                                              w[wp][:, 512 * k:512 * (k + 1)],
                                              start=(k == 0 and wp == 0 and rp == 0),
                                              stop=(k == 3 and wp == 1))
                        m.then_inc(pe_done, 1)

        @block.scalar
        def _(act):
            chained = [0]

            def after(ins):
                chained[0] += 1
                ins.then_inc(act_chain, 1)
                act.wait_ge(act_chain, chained[0])

            def split(half, s):
                act.wait_ge(raw_loaded[s], 16 * half + 16)
                act.wait_ge(pe_done, 10 * half + (5 * s - 5))
                act.activation(w_hi[s][:], raw[s][:], ACT.Copy).then_inc(hi_ready, 1)

            act.dma_start(xrow[0][:], step_slices(0)).then_inc(x_loaded[0], 16)
            act.dma_start(gbc[:], a["g_pre_mix"].broadcast_to((P, D))).then_inc(g_loaded, 16)
            act.dma_start(xrow[1][:], step_slices(1)).then_inc(x_loaded[1], 16)
            n_small = [0]

            def small(dst, src):
                n_small[0] += 1
                act.dma_start(dst, src).then_inc(small_loaded, 16)

            small(rows_in[R_CONV:R_CONV + 4, :], a["w_conv"][0])
            for r, name in ((R_BCONV, "b_conv"), (R_BGLU, "b_glu"), (R_GMH, "g_mh"), (R_S5D, "s5_d")):
                small(rows_in[r:r + 1, :], a[name])
            small(rows_in[R_HIST:NROWS, :], a["state_conv"][0].rearrange("b j c -> (b j) c"))
            for r, name in ((4, "s5_lam_re"), (5, "s5_lam_im")):
                small(dis[:, r, :], a[name][0].rearrange("(a g) p -> a (g p)", g=2))
            small(ldt[:, 0, :], a["s5_log_dt"][0].rearrange("(a g) -> a g", g=2))
            for r in range(2):
                small(b_in[:, r, :, :], s5_b[r][0].rearrange("(a g) p i -> (g p) a i", g=2))
                small(cn[:, r, :, :], s5_c[r][0].rearrange("(k q) i p -> (q i) k p", q=8))
            small(bgate[:, 0:1], a["b_igate"].rearrange("o h -> h o"))
            small(bgate[:, 1:2], a["b_fgate"].rearrange("o h -> h o"))
            with nc.allow_non_contiguous_dma(reason="32 words"):
                small(m0s[:], a["state_mlstm_m"][0].rearrange("b h -> h b"))
            small(n_in[:], a["state_mlstm_n"][0].rearrange("b h d -> (b h) d"))
            small(gate_w[:], cols_of(w_in, COL_GATE, 8))
            assert n_small[0] == N_SMALL, n_small
            for s in range(2):
                act.wait_ge(raw_loaded[s], 16)
                act.activation(w_hi[s][:], raw[s][:], ACT.Copy).then_inc(hi_ready, 1)

            def rms_sums(n, src, scratch):
                act.activation(scratch, src, ACT.Square, accum_out=stat[:, 0, n:n + 1]).then_inc(ssq_ready, 1)
                act.wait_ge(mean_ready, n + 1)
                act.activation(stat[:, 2, n:n + 1], stat[:, 1, n:n + 1], ACT.Sqrt).then_inc(root_ready, 1)

            def tile_hi(dst, t, first):
                for q in range(4):
                    act.wait_ge(tr_done, first + q + 1)
                    act.activation(dst[:, 4 * q:4 * q + 4, P * t:P * (t + 1)],
                                   psum[:, q, :].rearrange("p (k n) -> p k n", k=4),
                                   ACT.Copy).then_inc(tr_hi, 1)

            for t in range(TT):
                act.wait_ge(x_loaded[t % 2], 16 * (t // 2 + 1))
                rms_sums(t, xrow[t % 2][:], junk[:])
                tile_hi(xt_hi, t, 4 * t)
                if t + 2 < TT:
                    act.dma_start(xrow[t % 2][:], step_slices(t + 2)).then_inc(x_loaded[t % 2], 16)
            act.wait_ge(small_tr, 1)
            act.activation(chan[:].rearrange("p c r -> p (c r)"), psum[:, 4, 0:8 * NROWS], ACT.Copy)
            act.activation(n0[:].rearrange("p b h -> p (b h)"), psum[:, 4, 320:320 + NB * H],
                           ACT.Copy).then_inc(small_ev, 1)
            act.wait_ge(small_tr, 2)
            act.wait_ge(normed, TT)
            act.activation(c0t[:, 0, :, :].rearrange("p a i -> p (a i)"), psum[:, 5, :], ACT.Copy)
            act.activation(c0t[:, 1, :, :].rearrange("p a i -> p (a i)"), psum[:, 6, :],
                           ACT.Copy, scale=-1.0).then_inc(small_ev, 1)
            act.activation(gate_w_hi[:], gate_w[:], ACT.Copy).then_inc(dis_act, 1)
            act.activation(ldt[:, 1, :], ldt[:, 0, :], ACT.Exp).then_inc(dis_act, 1)
            act.wait_ge(dis_dve, 1)
            act.activation(dis[:, 10, :], dis[:, 6, :], ACT.Exp)
            act.activation(dis[:, 11, :], dis[:, 7, :], ACT.Sin)
            act.activation(dis[:, 12, :], dis[:, 9, :], ACT.Sin).then_inc(dis_act, 1)

            with act.Fori(0, 4) as i:
                for j in range(2):
                    act.wait_ge(pe_done, 10 * i + (5 * j + 5))
                    act.wait_ge(u_stored[j], 16 * i)
                    act.activation(u_out[j][:, :, 0:40],
                                   psum[:, 2 * j, 0:HALF].rearrange("p (c r) -> p r c", r=FR),
                                   ACT.Copy).then_inc(u_evac, 1)
                    act.activation(u_out[j][:, :, 40:80],
                                   psum[:, 2 * j + 1, 0:HALF].rearrange("p (c r) -> p r c", r=FR),
                                   ACT.Copy).then_inc(bank_free, 1)
                    split(i + 1, j)
                    act.wait_ge(u_evac, 2 * i + (j + 1))
                    act.wait_ge(bank_free, 2 * i + (j + 1))
                    act.dma_start(u_dram[bass.ds(2 * P * i + P * j, P), :],
                                  u_out[j][:].rearrange("p r c -> p (r c)")).then_inc(u_stored[j], 16)
            act.wait_ge(s5_consts, 1)
            with act.Fori(0, 4) as i:
                for j in range(2):
                    act.wait_ge(pe_done, 10 * i + (5 * (U_QK + j) + 5))
                    act.wait_ge(conv_read, 2 * i + (j + 1))
                    buf = conv_in[j]
                    act.activation(buf[:, HIST:HIST + HALF], psum[:, 2 * j, 0:HALF],
                                   ACT.Copy).then_inc(conv_filled, 1)
                    act.activation(buf[:, HIST + HALF:HIST + SEQ], psum[:, 2 * j + 1, 0:SEQ - HALF],
                                   ACT.Copy).then_inc(conv_filled, 1)
                    act.activation(streams(buf)[:, :, HIST:],
                                   psum[:, 2 * j + 1, SEQ - HALF:HALF].rearrange("p (b s) -> p b s", b=NB),
                                   ACT.Copy).then_inc(bank_free, 1)
                    split(i + (U_QK // 2 + 1), j)
                    act.wait_ge(conv_summed, 2 * i + (j + 1))
                    act.activation(qk[:, bass.ds(2 * i + j, 1), :], conv_acc[:].unsqueeze(1),
                                   ACT.Silu).then_inc(silu_done, 1)
            act.wait_ge(ones_ready, 1)
            with act.Fori(0, 2) as i:
                for j in range(4):
                    if j == 3:
                        for t in range(TT):
                            act.wait_ge(pe_done, 20 * i + (5 * (U_V + 3) + t + 1))
                            act.activation(va[:, t, bass.ds(2 * i, 2), 0:DV],
                                           psum[:, t, :].rearrange("p (h v) -> p h v", h=2),
                                           ACT.Copy).then_inc(tok_evac, 1)
                    split(2 * i + (U_V // 2 + 1 + j // 2), j % 2)
            for c in range(2):
                for j in range(4):
                    if j == 3:
                        for t in range(TT):
                            n = TT * c + t
                            act.wait_ge(pe_done, 5 * (U_OG + 4 * c + 3) + t + 1)
                            if n >= 2:
                                act.wait_ge(og_stored[n % 2], 16 * (n // 2))
                            act.activation(og_out[n % 2][:], psum[:, t, :], ACT.Sigmoid).then_inc(tok_evac, 1)
                            act.wait_ge(tok_evac, 10 + n + 1)
                            act.dma_start(og_dram[P * t:P * (t + 1), 512 * c:512 * (c + 1)],
                                          og_out[n % 2][:]).then_inc(og_stored[n % 2], 16)
                    if c == 0 or j < 2:
                        split(U_OG // 2 + 1 + 2 * c + j // 2, j % 2)
            act.wait_ge(row_done, 1)
            for s in range(2):
                act.wait_ge(og_stored[s], 16 * TT)
            for g, dst in ((0, r_li), (1, r_lf)):
                act.activation(dst[:, 0:512], psum[0:4, 2 * g, :], ACT.Identity, bias=bgate[:, g:g + 1])
                m = act.activation(dst[:, 512:T], psum[0:4, 2 * g + 1, 0:P], ACT.Identity,
                                   bias=bgate[:, g:g + 1])
            m.then_inc(row_act, 1)
            act.wait_ge(tail_done, 1)
            act.activation(tail_out[:], psum[0:27, 6:8, :].rearrange("p b n -> p (b n)"),
                           ACT.Copy).then_inc(tail_ev, 1)
            act.wait_ge(s5_state_tr, 1)
            for r in range(2):
                act.activation(sst[:, r, :, PSTEPS::2].rearrange("p a b -> p b a"),
                               psum[:, 5, 256 * r:256 * (r + 1)].rearrange("p (b a) -> p b a", b=NB),
                               ACT.Copy).then_inc(s5_state_in, 1)
            act.wait_ge(row_dve, 1)
            act.activation(t_rows[1][:], t_rows[0][:], ACT.Exp, scale=-1.0).then_inc(row_act, 1)
            act.wait_ge(row_dve, 2)
            act.activation(r_g[:], t_rows[2][:], ACT.Ln).then_inc(row_act, 1)
            act.wait_ge(row_dve, 4)
            act.activation(r_g[:], t_rows[2][:], ACT.Exp).then_inc(row_act, 1)
            act.wait_ge(tail_ev, 1)
            act.dma_start(o["conv_p"].rearrange("o b j c -> (o b j) c"), tail_out[0:3, :]).then_inc(tail_stored, 16)
            act.dma_start(o["conv_s"].rearrange("o b j c -> (o b j) c"), tail_out[3:27, :]).then_inc(tail_stored, 16)
            act.dma_start(o["m_p"].rearrange("o b h -> h (o b)"), r_m[:, SEQ - 1:SEQ]).then_inc(out_stored, 16)
            with nc.allow_non_contiguous_dma(reason="32 words"):
                act.dma_start(o["m_s"].rearrange("o b h -> h (o b)"), r_m[:, SEQ + DSEQ - 1::DSEQ]
                              ).then_inc(out_stored, 16)
            for k in range(BLOCKS):
                pairs = slice(BP * k, BP * (k + 1))
                act.wait_ge(bwt_done, k + 1)
                if k:
                    act.wait_ge(v_done, k)
                act.activation(bwt[:].rearrange("p r q n -> p r (q n)"), psum[:, 6:8, :],
                               ACT.Copy).then_inc(bwt_ready, 1)
                act.wait_ge(v_done, k + 1)
                for r in range(2):
                    v = psum[:, 4 + r, 0:BP * STEPS].rearrange("p (q c) -> p q c", q=BP)
                    act.activation(sst[:, r, pairs, 1:PSTEPS], v[:, :, 0:PSTEPS - 1], ACT.Copy)
                    act.activation(fin[:, r, 0, pairs], v[:, :, PSTEPS - 1], ACT.Copy)
                    act.activation(sst[:, r, pairs, PSTEPS + 1::2], v[:, :, PSTEPS::2], ACT.Copy)
                    m = act.activation(fin[:, r, 1:, pairs].rearrange("p b a -> p a b"), v[:, :, PSTEPS + 1::2], ACT.Copy)
                m.then_inc(v_evac, 1)
            act.wait_ge(em_done, 1)
            act.activation(exp_neg_m[:].rearrange("p t h -> p (t h)"), psum[:, 7, 0:TT * H], ACT.Exp,
                           scale=-1.0).then_inc(em_ready, 1)
            for t in range(TT):
                act.wait_ge(arg_done, t + 1)
                act.activation(dt[:].rearrange("p h n -> p (h n)"), psum[:, 0, :], ACT.Exp).then_inc(dt_ready, 1)
                if t == SAMPLE:
                    act.wait_ge(kt_done, TT)
                    act.activation(ksb[:].rearrange("p h n -> p (h n)"), psum[:, 3, :],
                                   ACT.Copy).then_inc(ksb_ready, 1)
                    act.wait_ge(fin_tr, 1)
                    act.wait_ge(h_stored[1], 32)
                    act.activation(cp_out[:].rearrange("p (b n) d -> p b (n d)", b=2), psum[:, 0:2, :],
                                   ACT.Copy).then_inc(fin_ev, 1)
                    act.wait_ge(fin_tr, 2)
                    act.activation(np_out[:], psum[0:4, 6, 0:P], ACT.Copy).then_inc(fin_ev, 1)
                if t >= 2:
                    act.wait_ge(h_stored[t % 2], 16 * (t // 2))
                for h in range(H):
                    if t == SAMPLE:
                        for q in range(4):
                            act.wait_ge(ctr_done, 4 * h + q + 1)
                            act.activation(cts[:, 2 * q:2 * q + 2, 0:DV],
                                           psum[:, q, :].rearrange("p (b v) -> p b v", b=2),
                                           ACT.Copy).then_inc(cts_ready, 1)
                    act.wait_ge(num_done, H * t + h + 1)
                    act.activation(hraw[t % 2][:, h, :], psum[:, 4 + h % 2, 0:VA1], ACT.Copy).then_inc(num_evac, 1)
                act.wait_ge(num_evac, H * (t + 1))
                act.dma_start(oa_dram[P * t:P * (t + 1), :],
                              hraw[t % 2][:].rearrange("p h v -> p (h v)")).then_inc(h_stored[t % 2], 16)
            act.wait_ge(fin_ev, 2)
            act.dma_start(o["c_p"][0, 0].rearrange("h (v p) d -> p (h v) d", v=2), cp_out[:]).then_inc(out_stored, 16)
            act.dma_start(o["n_p"][0, 0], np_out[:]).then_inc(out_stored, 16)
            act.wait_ge(fin_tr, 3)
            act.activation(ns_out[:], psum[0:NB * H, 6, P:2 * P], ACT.Copy).then_inc(fin_ev, 1)
            act.wait_ge(fin_tr, 4)
            act.activation(s5p_out[:].rearrange("a r p -> a (r p)"), psum[0:PAIRS, 0, 0:2 * P],
                           ACT.Copy).then_inc(fin_ev, 1)
            act.wait_ge(fin_tr, 5)
            act.activation(s5_io[:].rearrange("x r q p -> x (r q p)"), psum[:, 1, :],
                           ACT.Copy).then_inc(fin_ev, 1)
            act.wait_ge(fin_ev, 5)
            act.dma_start(o["n_s"][0].rearrange("b h d -> (b h) d"), ns_out[:]).then_inc(out_stored, 16)
            for r in range(2):
                act.dma_start(o[("s5re_p", "s5im_p")[r]][0, 0].rearrange("(a g) p -> a (g p)", g=2),
                              s5p_out[:, r, :]).then_inc(out_stored, 16)
                act.dma_start(o[("s5re_s", "s5im_s")[r]][0].rearrange("b (a g) p -> (b a) (g p)", g=2)
                              .rearrange("(q x) p -> x q p", q=2), s5_io[:, r, :, :]).then_inc(out_stored, 16)
            for k in range(BLOCKS):
                banks = (2, 3) if k % 2 else (4, 5)
                act.wait_ge(y_done, k + 1)
                if k >= 2:
                    act.wait_ge(y_stored[k % 2], 16 * FR * (k // 2))
                for g in range(2):
                    act.activation(y_out[k % 2][:, :, g, :],
                                   psum[:, banks[g], 0:BP * STEPS].rearrange("p (q c) -> p q c", q=BP),
                                   ACT.Copy).then_inc(y_evac, 1)
            act.wait_ge(y_loaded, 16)
            for c in range(8):
                act.activation(z[:, c, :], z[:, c, :], ACT.Gelu_apprx_tanh).then_inc(z_ready, 1)
            for c in range(8):
                act.wait_ge(z_ready, c + 1)
                act.activation(z_hi[:, c, :], z[:, c, :], ACT.Copy).then_inc(z_hi_ready, 1)
            for j in range(2):
                act.wait_ge(raw_loaded[j], 16 * (U_GLU // 2 + 1))
                act.activation(w_hi[j][:], raw[j][:], ACT.Copy).then_inc(hi_ready, 1)

            def mlstm_tile(t):
                act.wait_ge(oa_loaded, 32 * (t + 1))
                for h in range(H):
                    m = act.activation(sq_out[:], oa[:, h, 0:DV], ACT.Square,
                                       accum_out=stat[:, 4, 4 * t + h:4 * t + h + 1])
                    if h < H - 1:
                        after(m)
                m.then_inc(oa_sums, 1)
                act.wait_ge(oa_mean, t + 1)
                act.activation(stat[:, 6, 4 * t:4 * t + 4], stat[:, 5, 4 * t:4 * t + 4],
                               ACT.Sqrt).then_inc(oa_root, 1)
                for q in range(2):
                    n = 2 * t + q
                    act.wait_ge(oat_done, n + 1)
                    for k in range(4):
                        m = act.activation(ot_hi[:, 4 * q + k, P * t:P * (t + 1)],
                                           psum[:, 4 + n % 4, P * k:P * (k + 1)], ACT.Copy,
                                           scale=chan[:, 4 * q + k, R_GMH:R_GMH + 1])
                    m.then_inc(oat_hi, 1)

            for j in range(4):
                for c in range(2):
                    n = 2 * j + c
                    act.wait_ge(pe_done, 5 * (U_GLU + j) + 2 + 3 * c)
                    act.activation(psum[:, 2 * c:2 * c + 2, 0:HALF], psum[:, 2 * c:2 * c + 2, 0:HALF],
                                   ACT.Sigmoid, bias=chan[:, n, R_BGLU:R_BGLU + 1]).then_inc(gate_ready, 1)
                    act.wait_ge(ob_ready, n + 1)
                    act.activation(ot_hi[:, 8 + n, :], ob[:], ACT.Copy).then_inc(ob_hi, 1)
                split((U_GLU + 2 + j) // 2, j % 2)
                mlstm_tile(j)
            mlstm_tile(TT - 1)
            with act.Fori(0, 4) as i:
                for j in range(4):
                    if j == 3:
                        for t in range(TT):
                            act.wait_ge(pe_done, 20 * i + (5 * (U_OUT + 3) + t + 1))
                            act.activation(mix[:, t, bass.ds(512 * i, 512)], psum[:, t, :],
                                           ACT.Copy).then_inc(tok_evac, 1)
                    split(2 * i + (U_OUT // 2 + 1 + j // 2), j % 2)
            act.wait_ge(tok_evac, 40)
            for t in range(TT):
                rms_sums(TT + 2 * t, mix[:, t, :], psum[:, 4:8, :])
                act.wait_ge(xr_ready, t + 1)
                rms_sums(TT + 2 * t + 1, xres[t % 2][:], psum[:, 4:8, :])
                act.dma_start(x_dram[P * t:P * (t + 1), :], xres[t % 2][:]).then_inc(xr_stored[t % 2], 16)
                tile_hi(ht_hi, t, 4 * TT + 4 * t)
            for s in range(2):
                act.wait_ge(xr_stored[s], 16 * (3 - s))
            def ffn_block(i, last=False):
                for j in range(12):
                    p = j // 2
                    bank = 4 * (p % 2)
                    if j < 8 and j % 2 == 0:
                        act.wait_ge(pe_done, 60 * i + (5 * (U_FFN + j) + 5))
                        if p:
                            act.wait_ge(hid_ready, 8 * i + 2 * p)
                        for h in range(2):
                            act.activation(sg[:, h, :], psum[:, bank + h, 0:HALF], ACT.Silu).then_inc(sg_ready, 1)
                    elif j < 8:
                        for h in range(2):
                            act.wait_ge(hid_ready, 8 * i + (2 * p + h + 1))
                            if p == 0 and h == 0:
                                act.wait_ge(pe_done, 60 * i + 5 * U_FFN)
                            act.activation(h_hi[:, p, HALF * h:HALF * (h + 1)], hid[:, h, :],
                                           ACT.Copy).then_inc(h_hi_ready, 1)
                    if not (last and j >= 10):
                        split(6 * i + ((U_FFN + 2 + j) // 2), j % 2)

            with act.Fori(0, NFB - 1) as i:
                ffn_block(i)
            ffn_block(NFB - 1, last=True)
            act.wait_ge(tok_evac, 40 + 20 * NFB)
            for t in range(TT):
                rms_sums(3 * TT + t, acc[:, t, :], psum[:, 4:8, :])

        @block.vector
        def _(dve):
            chained = [0]

            def after(ins):
                chained[0] += 1
                ins.then_inc(dve_chain, 1)
                dve.wait_ge(dve_chain, chained[0])

            def split(n, s):
                dve.wait_ge(hi_ready, n + 1)
                dve.tensor_tensor(w_lo[s][:], raw[s][:], w_hi[s][:].bitcast(F32),
                                  ALU.subtract).then_inc(lo_ready, 1)

            def rms_factor(n):
                dve.wait_ge(ssq_ready, n + 1)
                dve.tensor_scalar(stat[:, 1, n:n + 1], stat[:, 0, n:n + 1], 1.0 / D, EPS, ALU.mult,
                                  ALU.add).then_inc(mean_ready, 1)
                dve.wait_ge(root_ready, n + 1)
                after(dve.reciprocal(stat[:, 3, n:n + 1], stat[:, 2, n:n + 1]))
                return stat[:, 3, n:n + 1]

            def tile_lo(hi, lo, t, first):
                for q in range(4):
                    dve.wait_ge(tr_hi, first + q + 1)
                    cols = (slice(None), slice(4 * q, 4 * q + 4), slice(P * t, P * (t + 1)))
                    dve.tensor_tensor(lo[cols], psum[:, q, :].rearrange("p (k n) -> p k n", k=4),
                                      hi[cols].bitcast(F32), ALU.subtract).then_inc(tr_lo, 1)

            for s in range(2):
                split(s, s)
            for t in range(TT):
                f = rms_factor(t)
                if t == 0:
                    dve.wait_ge(g_loaded, 16)
                dve.scalar_tensor_tensor(out=xrow[t % 2][:], in0=xrow[t % 2][:], scalar=f, in1=gbc[:],
                                         op0=ALU.mult, op1=ALU.mult).then_inc(normed, 1)
                tile_lo(xt_hi, xt_lo, t, 4 * t)
            dve.wait_ge(dis_act, 1)
            dve.tensor_tensor(gate_w_lo[:], gate_w[:], gate_w_hi[:].bitcast(F32),
                              ALU.subtract).then_inc(gate_w_ready, 1)
            for s in range(2):
                dve.memset(conv_in[s][:, 0:HIST], 0.0).then_inc(conv_read, 1)
            dve.wait_ge(const_ready, 3)
            after(dve.tensor_reduce(diag16[:], ident[:].rearrange("p (g i) -> p i g", g=8), AX.X, ALU.add))

            def v(n):
                return dis[:, n, :]

            def tt(out, x, y, op):
                after(dve.tensor_tensor(v(out), v(x), v(y), op))

            LAM_RE, LAM_IM, EXPO, ANGLE, TURNS, COMP, MAG, SIN, COS, NR, DEN, T0 = range(4, 16)
            dve.wait_ge(dis_act, 2)
            step = ldt[:, 1, :].unsqueeze(2).to_broadcast([PAIRS, 2, NS])
            for dst, src in ((EXPO, LAM_RE), (ANGLE, LAM_IM)):
                after(dve.tensor_tensor(v(dst).rearrange("a (g p) -> a g p", g=2),
                                        v(src).rearrange("a (g p) -> a g p", g=2), step, ALU.mult))
            after(dve.tensor_scalar(v(TURNS), v(ANGLE), 1.0 / TWO_PI, ROUND, ALU.mult, ALU.add))
            after(dve.tensor_scalar(v(TURNS), v(TURNS), -ROUND, None, ALU.add))
            for part in (PI2_A, PI2_B, PI2_C):
                after(dve.scalar_tensor_tensor(out=v(ANGLE), in0=v(TURNS), scalar=-part, in1=v(ANGLE),
                                               op0=ALU.mult, op1=ALU.add))
            after(dve.tensor_scalar(v(ANGLE), v(ANGLE), 3.1415925, -3.1415925, ALU.min, ALU.max))
            after(dve.scalar_tensor_tensor(out=v(COMP), in0=v(ANGLE), scalar=-1.0, in1=v(ANGLE),
                                           op0=ALU.mult, op1=ALU.max))
            dve.tensor_scalar(v(COMP), v(COMP), -1.0, float(np.pi / 2), ALU.mult, ALU.add).then_inc(dis_dve, 1)
            dve.wait_ge(dis_act, 3)
            tt(0, MAG, COS, ALU.mult)
            tt(1, MAG, SIN, ALU.mult)
            after(dve.tensor_scalar(v(NR), v(0), -1.0, None, ALU.add))
            tt(DEN, LAM_RE, LAM_RE, ALU.mult)
            tt(T0, LAM_IM, LAM_IM, ALU.mult)
            tt(DEN, DEN, T0, ALU.add)
            after(dve.reciprocal(v(DEN), v(DEN)))
            tt(2, NR, LAM_RE, ALU.mult)
            tt(T0, 1, LAM_IM, ALU.mult)
            tt(2, 2, T0, ALU.add)
            tt(2, 2, DEN, ALU.mult)
            tt(3, 1, LAM_RE, ALU.mult)
            tt(T0, NR, LAM_IM, ALU.mult)
            tt(3, 3, T0, ALU.subtract)
            dve.tensor_tensor(v(3), v(3), v(DEN), ALU.mult).then_inc(dis_dve, 1)

            with dve.Fori(0, 4) as i:
                for j in range(2):
                    split(2 * i + (j + 2), j)
            dve.wait_ge(gates_done, 1)
            dve.tensor_copy(gate_tok[:].rearrange("p t g -> p (t g)"), psum[:, 5, 0:8 * TT]).then_inc(gate_tok_ready, 1)
            dve.wait_ge(small_tr, 3)
            for r in range(2):
                dve.tensor_copy(lbp[:, r, :, 1], psum[:, 6, PAIRS * r:PAIRS * (r + 1)])
            dve.tensor_copy(fct[:].rearrange("p r a -> p (r a)"), psum[:, 6, 2 * PAIRS:4 * PAIRS]).then_inc(small_ev, 1)
            dve.wait_ge(small_ev, 3)
            STEPS_CONV = 9
            with dve.Fori(0, 4) as i:
                for j in range(2):
                    n = 2 * i + j
                    split(2 * i + (U_QK + j + 2), j)
                    buf = conv_in[j]
                    dve.wait_ge(conv_filled, 4 * i + (2 * j + 2))
                    dve.wait_ge(bank_free, 2 * i + (U_QK + j + 1))
                    base_n = 2 * STEPS_CONV * i + STEPS_CONV * j
                    dve.tensor_copy(vec[:], chan[:, bass.ds(n, 1), :].rearrange("p o r -> p (o r)")
                                    ).then_inc(conv_step, 1)
                    dve.tensor_copy(conv_tail[:, bass.ds(n, 1), 0:HIST].rearrange("p o j -> p (o j)"),
                                    buf[:, SEQ:SEQ + HIST])
                    dve.tensor_copy(conv_tail[:, bass.ds(n, 1), HIST:].rearrange("p o (b j) -> p (o b) j", b=NB),
                                    streams(buf)[:, :, DSEQ:]).then_inc(conv_step, 1)
                    dve.wait_ge(conv_step, base_n + 2)
                    dve.tensor_copy(streams(buf)[:, :, 0:HIST],
                                    vec[:, R_HIST:].rearrange("p (b j) -> p b j", b=NB)).then_inc(conv_step, 1)
                    dve.wait_ge(conv_step, base_n + 3)
                    dve.wait_ge(silu_done, n)
                    for tap in range(CONV):
                        w = vec[:, tap:tap + 1]
                        for part in range(2):
                            if part == 0:
                                src, dst = buf[:, tap:tap + SEQ], conv_acc[:, 0:SEQ]
                            else:
                                src = streams(buf)[:, :, tap:tap + DSEQ]
                                dst = conv_acc[:, SEQ:].rearrange("p (b s) -> p b s", b=NB)
                            if tap == 0:
                                m = dve.tensor_scalar(dst, src, w, vec[:, R_BCONV:R_BCONV + 1], ALU.mult, ALU.add)
                            else:
                                m = dve.scalar_tensor_tensor(out=dst, in0=src, scalar=w, in1=dst,
                                                             op0=ALU.mult, op1=ALU.add)
                            if tap < CONV - 1:
                                m.then_inc(conv_step, 1)
                            elif part:
                                m.then_inc(conv_summed, 1)
                            else:
                                m.then_inc(conv_read, 1)
                        if tap < CONV - 1:
                            dve.wait_ge(conv_step, base_n + (3 + 2 * tap + 2))
            dve.wait_ge(s5_consts, 1)
            dve.wait_ge(gates_done, 1)
            dve.memset(va[:, :, :, DV:VA1].rearrange("p t h o -> p t (h o)"), 1.0).then_inc(ones_ready, 1)
            with dve.Fori(0, 3) as i:
                for j in range(4):
                    split(4 * i + (U_V + 2 + j), j % 2)
            for j in range(2):
                split(U_OG + 6 + j, j)
            t0, t1, t2, t3 = (t[:] for t in t_rows)
            dve.wait_ge(pe_done, 5 * U_GLU)
            dve.wait_ge(row_act, 1)
            dve.scalar_tensor_tensor(out=t0, in0=r_lf[:], scalar=-1.0, in1=r_lf[:], op0=ALU.mult,
                                     op1=ALU.max).then_inc(row_dve, 1)
            dve.wait_ge(row_act, 2)
            dve.tensor_scalar(t2, t1, 1.0, None, ALU.add).then_inc(row_dve, 1)
            dve.wait_ge(row_dve, 2)
            dve.scalar_tensor_tensor(out=t3, in0=t2, scalar=-1.0, in1=t1, op0=ALU.add, op1=ALU.subtract)
            after(dve.reciprocal(t0, t2))
            after(dve.tensor_tensor(t3, t3, t0, ALU.mult))
            dve.wait_ge(row_act, 3)
            after(dve.tensor_tensor(r_g[:], r_g[:], t3, ALU.subtract))
            after(dve.scalar_tensor_tensor(out=r_lf[:], in0=r_lf[:], scalar=0.0, in1=r_g[:], op0=ALU.min,
                                           op1=ALU.subtract))
            after(dve.memset(t1, 0.0))
            for c in range(SAMPLE):
                seg = slice(P * c, P * (c + 1))
                dve.tensor_tensor_scan(t0[:, seg], r_lf[:, seg], t1[:, seg], 0.0, ALU.add, ALU.add)
            dve.tensor_tensor_scan(r_m[:, 0:SEQ], r_lf[:, 0:SEQ], r_li[:, 0:SEQ], 0.0, ALU.add, ALU.max)
            for b in range(NB):
                seg = slice(SEQ + DSEQ * b, SEQ + DSEQ * (b + 1))
                dve.tensor_tensor_scan(t0[:, seg], r_lf[:, seg], t1[:, seg], 0.0, ALU.add, ALU.add)
                m = dve.tensor_tensor_scan(r_m[:, seg], r_lf[:, seg], r_li[:, seg], m0s[:, b:b + 1],
                                           ALU.add, ALU.max)
            after(m)
            after(dve.tensor_tensor(r_a[:], t0, r_m[:], ALU.subtract))
            dve.tensor_tensor(r_b[:], r_li[:], t0, ALU.subtract).then_inc(row_dve, 1)
            dve.tensor_copy(t2[:, 0:P], r_a[:, 0:P])
            for c in range(1, SAMPLE):
                seg = slice(P * c, P * (c + 1))
                dve.tensor_scalar(t2[:, seg], r_a[:, seg], r_m[:, P * c - 1:P * c], None, ALU.add)
            dve.tensor_tensor(t2[:, SEQ:].rearrange("p (b s) -> p b s", b=NB),
                              r_a[:, SEQ:].rearrange("p (b s) -> p b s", b=NB),
                              m0s[:].unsqueeze(2).to_broadcast([4, NB, DSEQ]), ALU.add).then_inc(row_dve, 1)
            dve.tensor_copy(lam8[:, 0, 0, :], lbp[:, 0, :, FR])
            dve.tensor_copy(lam8[:, 0, 1, :], lbp[:, 0, :, FR])
            dve.tensor_scalar(lam8[:, 1, 0, :], lbp[:, 1, :, FR], -1.0, None, ALU.mult)
            dve.tensor_copy(lam8[:, 1, 1, :], lbp[:, 1, :, FR])
            dve.memset(sst[:, :, :, 0:1].rearrange("p r a o -> p r (a o)"), 0.0)
            dve.memset(kpad[:, 0:7 * GI], 0.0)
            after(dve.memset(bdiag[:], 0.0))
            dve.memset(qgm[:], 0.0)
            after(dve.memset(ct[:], 0.0))
            dve.wait_ge(small_ev, 2)
            for k in range(BLOCKS):
                pairs = slice(BP * k, BP * (k + 1))
                if k:
                    dve.wait_ge(k_done, k)
                for g in range(2):
                    dve.tensor_copy(bdiag[64 * g:64 * g + 64, :, :, GI * g:GI * (g + 1)],
                                    bbar[64 * g:64 * g + 64, :, pairs, :]).then_inc(bdiag_ready, 1)
                if k:
                    dve.wait_ge(bwt_done, k)
                shape = [P, BP, FR, GI]
                lr, li = (lbp[:, r, pairs, 0:FR].unsqueeze(3).to_broadcast(shape) for r in range(2))
                br, bi = (bbar[:, r, pairs, :].unsqueeze(2).to_broadcast(shape) for r in range(2))
                dst = [bpw[:, r, :, :].rearrange("p q (k i) -> p q k i", k=FR) for r in range(2)]
                tmp = btmp[:].rearrange("p q (k i) -> p q k i", k=FR)
                if k:
                    dve.wait_ge(bpw_ready, k)
                dve.tensor_tensor(dst[0], lr, br, ALU.mult)
                after(dve.tensor_tensor(tmp, li, bi, ALU.mult))
                after(dve.tensor_tensor(dst[0], dst[0], tmp, ALU.subtract))
                dve.tensor_tensor(dst[1], lr, bi, ALU.mult)
                after(dve.tensor_tensor(tmp, li, br, ALU.mult))
                dve.tensor_tensor(dst[1], dst[1], tmp, ALU.add).then_inc(bpw_ready, 1)
                dve.wait_ge(k_done, k + 1)
                if k:
                    dve.wait_ge(k_stored, 16 * k)
                dve.scalar_tensor_tensor(out=kpad[:, 7 * GI:8 * GI], in0=diag16[:],
                                         scalar=chan[:, k, R_S5D:R_S5D + 1], in1=psum[:, 3, 0:GI],
                                         op0=ALU.mult, op1=ALU.add).then_inc(k_ready, 1)
                dve.tensor_copy(kpad[:, 8 * GI:], psum[:, 3, GI:P]).then_inc(k_ready, 1)
            scale = float(DQK) ** -0.5
            for t in range(TT):
                rows = slice(P * t, P * (t + 1))
                dve.wait_ge(s_done, t + 1)
                dve.wait_ge(dt_ready, t + 1)
                dve.scalar_tensor_tensor(out=pt[:].rearrange("p h n -> p (h n)"), in0=psum[:, 1, :],
                                         scalar=scale, in1=dt[:].rearrange("p h n -> p (h n)"),
                                         op0=ALU.mult, op1=ALU.mult).then_inc(pt_ready, 1)
                dve.wait_ge(gb_done, t + 1)
                gb = psum[:, 2, :].rearrange("p (h n) -> p h n", h=H)
                if t < SAMPLE:
                    after(dve.tensor_copy(decay[:, :, 0], gb[:, :, P - 1]))
                else:
                    after(dve.tensor_copy(decay[:], gb[:, :, DSEQ - 1::DSEQ]))
                dve.scalar_tensor_tensor(out=qg[:], in0=qk[:, 0:H, rows], scalar=scale, in1=gb,
                                         op0=ALU.mult, op1=ALU.mult).then_inc(qg_ready, 1)
                if t < SAMPLE:
                    dve.wait_ge(kt_done, t + 1)
                    dve.tensor_tensor(kw[:], psum[:, 3, :].rearrange("p (h n) -> p h n", h=H),
                                      dt[:, :, P - 1:P].to_broadcast([P, H, P]), ALU.mult).then_inc(kw_ready, 1)
                    for h in range(H):
                        dve.wait_ge(dc_done, H * t + h + 1)
                        dve.scalar_tensor_tensor(out=ct[:, h, :], in0=ct[:, h, :], scalar=decay[:, h, 0:1],
                                                 in1=psum[:, h, 0:VA1], op0=ALU.mult,
                                                 op1=ALU.add).then_inc(ct_ready, 1)
                    continue
                dve.wait_ge(qg_ready, TT)
                dve.wait_ge(ksb_ready, 1)
                for h in range(H):
                    if h:
                        dve.wait_ge(num_done, H * t + h)
                    dve.tensor_copy(qgm[:].rearrange("p (b s) -> p b s", b=NB)[:, :, 0:DSEQ],
                                    qg[:, h, :].rearrange("p (b s) -> p b s", b=NB)).then_inc(qgm_ready, 1)
                    dve.tensor_copy(cts[:, :, DV], n0[:, :, h]).then_inc(cts_ready, 1)
                    if h:
                        dve.wait_ge(un_done, 4 * h)
                    dve.tensor_tensor(kwall[:], ksb[:, h, :].unsqueeze(1).to_broadcast([P, NB, P]),
                                      dt[:, h, DSEQ - 1::DSEQ].unsqueeze(2).to_broadcast([P, NB, P]),
                                      ALU.mult).then_inc(kwall_ready, 1)
                    for v2 in range(2):
                        for q in range(2):
                            dve.wait_ge(un_done, 4 * h + 2 * v2 + q + 1)
                            for b in range(4 * q, 4 * q + 4):
                                c0 = c0n[h % 2][:, v2, b, :]
                                m = dve.scalar_tensor_tensor(out=c0, in0=c0, scalar=decay[:, h, b:b + 1],
                                                             in1=psum[:, 2 * v2 + q, P * (b % 4):P * (b % 4 + 1)],
                                                             op0=ALU.mult, op1=ALU.add)
                            m.then_inc(c_new, 1)
                    after(dve.tensor_tensor(n_new[:, :, h], n0[:, :, h], decay[:, h, :], ALU.mult))
                    dve.wait_ge(nn_done, h + 1)
                    dve.tensor_tensor(n_new[:, :, h], n_new[:, :, h], psum[:, 7, NB * h:NB * (h + 1)],
                                      ALU.add).then_inc(ct_ready, 1)
            for k in range(BLOCKS):
                if k >= 2:
                    dve.wait_ge(y_done, k - 1)
                dve.wait_ge(cpw_ready, BLOCKS + k)
                output_powers(dve, after, k).then_inc(cpw_ready, 1)
            for c in range(8):
                dve.wait_ge(z_hi_ready, c + 1)
                dve.tensor_tensor(z_lo[:, c, :], z[:, c, :], z_hi[:, c, :].bitcast(F32),
                                  ALU.subtract).then_inc(z_lo_ready, 1)
            for j in range(2):
                split(U_GLU + j, j)

            def mlstm_tile(t):
                f = stat[:, 7, 4 * t:4 * t + 4]
                mean = stat[:, 5, 4 * t:4 * t + 4]
                den = oa[:, :, DV]
                dve.wait_ge(oa_loaded, 32 * (t + 1))
                after(dve.scalar_tensor_tensor(out=f, in0=den, scalar=-1.0, in1=den, op0=ALU.mult, op1=ALU.max))
                after(dve.tensor_tensor(f, f, exp_neg_m[:, t, :], ALU.max))
                after(dve.reciprocal(f, f))
                dve.wait_ge(oa_sums, t + 1)
                after(dve.tensor_tensor(mean, stat[:, 4, 4 * t:4 * t + 4], f, ALU.mult))
                after(dve.tensor_tensor(mean, mean, f, ALU.mult))
                dve.tensor_scalar(mean, mean, 1.0 / DV, EPS, ALU.mult, ALU.add).then_inc(oa_mean, 1)
                dve.wait_ge(oa_root, t + 1)
                after(dve.reciprocal(stat[:, 6, 4 * t:4 * t + 4], stat[:, 6, 4 * t:4 * t + 4]))
                after(dve.tensor_tensor(f, f, stat[:, 6, 4 * t:4 * t + 4], ALU.mult))
                for h in range(H):
                    m = dve.scalar_tensor_tensor(out=og_in[:, h, :], in0=oa[:, h, 0:DV], scalar=f[:, h:h + 1],
                                                 in1=og_in[:, h, :], op0=ALU.mult, op1=ALU.mult)
                m.then_inc(oa_ready, 1)
                for q in range(2):
                    n = 2 * t + q
                    dve.wait_ge(oat_hi, n + 1)
                    for k in range(4):
                        kt = 4 * q + k
                        m = dve.scalar_tensor_tensor(
                            out=ot_lo[:, kt, P * t:P * (t + 1)], in0=psum[:, 4 + n % 4, P * k:P * (k + 1)],
                            scalar=chan[:, kt, R_GMH:R_GMH + 1],
                            in1=ot_hi[:, kt, P * t:P * (t + 1)].bitcast(F32), op0=ALU.mult, op1=ALU.subtract)
                    m.then_inc(oat_lo, 1)

            for j in range(4):
                for c in range(2):
                    n = 2 * j + c
                    dve.wait_ge(gate_ready, n + 1)
                    if n:
                        dve.wait_ge(ob_lo, n)
                    for h in range(2):
                        fr = slice(4 * h, 4 * h + 4)
                        m = dve.tensor_tensor(
                            ob[:].rearrange("p (c r) -> p r c", r=FR)[:, fr, :],
                            z[:, n, :].rearrange("p (r c) -> p r c", r=FR)[:, fr, :],
                            psum[:, 2 * c + h, 0:HALF].rearrange("p (r c) -> p r c", r=4), ALU.mult)
                        m.then_inc(ob_ready if h else ob_first, 1)
                    dve.wait_ge(ob_first, n + 1)
                    dve.wait_ge(ob_hi, n + 1)
                    dve.tensor_tensor(ot_lo[:, 8 + n, :], ob[:], ot_hi[:, 8 + n, :].bitcast(F32),
                                      ALU.subtract).then_inc(ob_lo, 1)
                split(U_GLU + 2 + j, j % 2)
                mlstm_tile(j)
            mlstm_tile(TT - 1)
            with dve.Fori(0, 4) as i:
                for j in range(4):
                    split(4 * i + (U_OUT + 2 + j), j % 2)
            dve.wait_ge(gp_loaded, 32)
            for t in range(TT):
                f = rms_factor(TT + 2 * t)
                after(dve.scalar_tensor_tensor(out=mix[:, t, :], in0=mix[:, t, :], scalar=f, in1=g_post[:],
                                               op0=ALU.mult, op1=ALU.mult))
                dve.wait_ge(xr_loaded[t % 2], 16 * (t // 2 + 1))
                dve.tensor_tensor(xres[t % 2][:], xres[t % 2][:], mix[:, t, :], ALU.add).then_inc(xr_ready, 1)
                f = rms_factor(TT + 2 * t + 1)
                dve.scalar_tensor_tensor(out=mix[:, t, :], in0=xres[t % 2][:], scalar=f, in1=g_ffn[:],
                                         op0=ALU.mult, op1=ALU.mult).then_inc(normed, 1)
                tile_lo(ht_hi, ht_lo, t, 4 * TT + 4 * t)
            def ffn_block(i, last=False):
                for j in range(12):
                    p = j // 2
                    bank = 4 * (p % 2)
                    if j < 8 and j % 2:
                        dve.wait_ge(pe_done, 60 * i + (5 * (U_FFN + j) + 5))
                        for h in range(2):
                            dve.wait_ge(sg_ready, 8 * i + (2 * p + h + 1))
                            if p:
                                dve.wait_ge(h_lo_ready, 8 * i + 2 * p)
                            dve.tensor_tensor(hid[:, h, :], sg[:, h, :], psum[:, bank + 2 + h, 0:HALF],
                                              ALU.mult).then_inc(hid_ready, 1)
                        for h in range(2):
                            dve.wait_ge(h_hi_ready, 8 * i + (2 * p + h + 1))
                            cols = (slice(None), p, slice(HALF * h, HALF * (h + 1)))
                            dve.tensor_tensor(h_lo[cols], hid[:, h, :], h_hi[cols].bitcast(F32),
                                              ALU.subtract).then_inc(h_lo_ready, 1)
                    if j >= 8:
                        for t in range(TT):
                            q = TT * (j - 8) + t
                            dve.wait_ge(pe_done, 60 * i + (5 * (U_FFN + j) + t + 1))
                            if q == 0:
                                dve.wait_ge(tok_evac, 20 * i + 40)
                            bank = q % 8 if q < 16 else q - 12
                            cols = slice(512 * (j - 8), 512 * (j - 7))
                            dve.tensor_tensor(acc[:, t, cols], acc[:, t, cols], psum[:, bank, :],
                                              ALU.add).then_inc(tok_evac, 1)
                    if not (last and j >= 10):
                        split(12 * i + (U_FFN + 2 + j), j % 2)

            dve.wait_ge(acc_zero, 1)
            with dve.Fori(0, NFB - 1) as i:
                ffn_block(i)
            ffn_block(NFB - 1, last=True)
            dve.wait_ge(gp_loaded, 48)
            for t in range(TT):
                f = rms_factor(3 * TT + t)
                after(dve.scalar_tensor_tensor(out=acc[:, t, :], in0=acc[:, t, :], scalar=f, in1=g_last[:],
                                               op0=ALU.mult, op1=ALU.mult))
                dve.wait_ge(last_loaded[t % 2], 16 * (t // 2 + 1))
                dve.tensor_tensor(xlast[t % 2][:], xlast[t % 2][:], acc[:, t, :], ALU.add).then_inc(y_ready, 1)

        @block.gpsimd
        def _(pool):
            chained = [0]

            def after(ins):
                chained[0] += 1
                ins.then_inc(pool_chain, 1)
                pool.wait_ge(pool_chain, chained[0])

            pool.memset(ident[:], 0.0)
            pool.memset(mask_prompt[:], 0.0)
            after(pool.memset(mask_sample[:], 0.0))
            pool.affine_select(out=ident[:], in_=ident[:], compare_op=ALU.not_equal, fill=1.0, base=0,
                               pattern=[[-1, P]], channel_multiplier=1).then_inc(const_ready, 1)
            pool.affine_select(out=mask_prompt[:], in_=mask_prompt[:], compare_op=ALU.is_ge, fill=MASKED,
                               base=0, pattern=[[1, P]], channel_multiplier=-1).then_inc(const_ready, 1)
            after(pool.affine_select(out=mask_sample[:], in_=mask_sample[:], compare_op=ALU.is_ge, fill=MASKED,
                                     base=0, pattern=[[1, P]], channel_multiplier=-1))
            per_stream = mask_sample[:].rearrange("p (b s) -> p b s", b=NB)
            pool.affine_select(out=per_stream, in_=per_stream, compare_op=ALU.is_ge, fill=MASKED, base=0,
                               pattern=[[-DSEQ, NB], [0, DSEQ]], channel_multiplier=1).then_inc(const_ready, 1)

            def cmul(dst, x, y, tmp):
                pool.tensor_tensor(dst[0], x[0], y[0], ALU.mult)
                after(pool.tensor_tensor(tmp, x[1], y[1], ALU.mult))
                after(pool.tensor_tensor(dst[0], dst[0], tmp, ALU.subtract))
                pool.tensor_tensor(dst[1], x[0], y[1], ALU.mult)
                after(pool.tensor_tensor(tmp, x[1], y[0], ALU.mult))
                after(pool.tensor_tensor(dst[1], dst[1], tmp, ALU.add))

            pool.wait_ge(small_ev, 3)
            pool.memset(lbp[:, 0, :, 0:1].rearrange("p a o -> p (a o)"), 1.0)
            after(pool.memset(lbp[:, 1, :, 0:1].rearrange("p a o -> p (a o)"), 0.0))
            lb = [lbp[:, r, :, 1] for r in range(2)]
            for k in range(2, FR + 1):
                cmul([lbp[:, r, :, k] for r in range(2)], [lbp[:, r, :, k - 1] for r in range(2)], lb,
                     stmp[:, 1, :, 0])
            cmul([bbar[:, r, :, :] for r in range(2)],
                 [fct[:, r, :].unsqueeze(2).to_broadcast([P, PAIRS, GI]) for r in range(2)],
                 [b_in[:, r, :, :] for r in range(2)], stmp[:, 0, :, :])
            pool.memset(stmp[:, 1, 0, 0:1], 0.0).then_inc(s5_consts, 1)
            pool.wait_ge(pe_done, 5 * U_GLU)
            after(pool.memset(sel[:], 0.0))
            pool.affine_select(out=sel[:], in_=sel[:], compare_op=ALU.not_equal, fill=1.0, base=0,
                               pattern=[[-1, 4], [0, P]], channel_multiplier=1).then_inc(sel_ready, 1)
            for k in range(BLOCKS):
                if k >= 2:
                    pool.wait_ge(k_done, k - 1)
                if k:
                    pool.wait_ge(cpw_ready, k)
                output_powers(pool, after, k).then_inc(cpw_ready, 1)
            pool.wait_ge(v_evac, BLOCKS)
            pool.wait_ge(s5_state_in, 2)

            def advance(dst, state, tmp, done):
                shape = list(state.shape)
                lam = [lam8[:, r, :, :] if len(shape) == 3 else
                       lam8[:, r, :, :].unsqueeze(3).to_broadcast(shape) for r in range(2)]
                pool.tensor_tensor(tmp[0], lam[0], state, ALU.mult).then_inc(scan_step, 1)
                pool.tensor_tensor(tmp[1], lam[1], state[:, ::-1], ALU.mult).then_inc(scan_step, 1)
                pool.wait_ge(scan_step, done + 1)
                pool.tensor_tensor(dst, dst, tmp[0], ALU.add).then_inc(scan_step, 1)
                pool.wait_ge(scan_step, done + 3)
                pool.tensor_tensor(dst, dst, tmp[1], ALU.add).then_inc(scan_step, 1)
                pool.wait_ge(scan_step, done + 4)

            one = [scan_tmp[:, r, :, :] for r in range(2)]
            for c in range(PSTEPS):
                advance(sst[:, :, :, c + 1] if c < PSTEPS - 1 else fin[:, :, 0, :], sst[:, :, :, c], one, 4 * c)
            many = [t[:] for t in stream_tmp]
            advance(sst[:, :, :, PSTEPS + 1::2], sst[:, :, :, PSTEPS::2], many, 4 * PSTEPS)
            advance(fin[:, :, 1:, :].rearrange("p r b a -> p r a b"), sst[:, :, :, PSTEPS + 1::2], many,
                    4 * PSTEPS + 4)
            pool.memset(scan_tmp[:, 0, 0, 0:1], 0.0).then_inc(scan_done, 1)
            pool.wait_ge(tr_done, 8 * TT)
            pool.memset(acc[:].rearrange("p t d -> p (t d)"), 0.0).then_inc(acc_zero, 1)


_INS = ["x_prompt", "x_sample", "state_conv", "state_mlstm_c", "state_mlstm_n", "state_mlstm_m",
        "state_s5_re", "state_s5_im", "g_pre_mix", "w_in", "w_conv", "b_conv", "b_igate", "b_fgate",
        "g_mh", "s5_lam_re", "s5_lam_im", "s5_log_dt", "s5_b_re", "s5_b_im", "s5_c_re", "s5_c_im",
        "s5_d", "w_glu", "b_glu", "w_out", "g_post_mix", "g_pre_ffn", "w_gate", "w_up", "w_down",
        "g_post_ffn"]
_OUTS = {"y_prompt": (1, SEQ, D), "y_sample": (NB, DSEQ, D),
         "conv_p": (1, 1, HIST, QK), "c_p": (1, 1, H, DV, DQK), "n_p": (1, 1, H, DQK), "m_p": (1, 1, H),
         "s5re_p": (1, 1, G, NS), "s5im_p": (1, 1, G, NS),
         "conv_s": (1, NB, HIST, QK), "c_s": (1, NB, H, DV, DQK), "n_s": (1, NB, H, DQK), "m_s": (1, NB, H),
         "s5re_s": (1, NB, G, NS), "s5im_s": (1, NB, G, NS)}


def kernel(**inputs):
    import concourse.bacc as bacc
    from concourse.bass_utils import run_bass_kernel_spmd

    nc = bacc.Bacc("TRN2", target_bir_lowering=False, num_devices=1)
    arrays, ins, outs = {}, {}, {}
    for name in _INS:
        x = np.ascontiguousarray(inputs[name])
        arrays[f"in_{name}"] = x
        ins[name] = nc.dram_tensor(f"in_{name}", x.shape, mybir.dt.from_np(x.dtype), kind="ExternalInput").ap()
    for name, shape in _OUTS.items():
        outs[name] = nc.dram_tensor(f"out_{name}", shape, F32, kind="ExternalOutput").ap()
    build(nc, ins, outs)
    r = run_bass_kernel_spmd(nc, [arrays], core_ids=[0])
    return tuple(r.results[0][f"out_{name}"] for name in _OUTS)
```

```python
from contextlib import ExitStack

import numpy as np

import concourse.bass as bass
from concourse import mybir
from concourse.alu_op_type import AluOpType as ALU

F32 = mybir.dt.float32
F32R = mybir.dt.float32r
ACT = mybir.ActivationFunctionType
AX = mybir.AxisListType

P = 128
D = 2048
KT = D // P
SEQ, NB, DSEQ = 512, 8, 16
TT = (SEQ + NB * DSEQ) // P
T = TT * P
HALF = T // 2
SAMPLE = SEQ // P
H, DV, DQK = 4, 256, 128
VA1 = DV + 1
QK = 2 * H * DQK
DA = H * DV
DB = D - DA
CONV = 4
HIST = CONV - 1
G, GI, NS = 64, 16, 64
PAIRS = G // 2
FR = P // GI
STEPS = T // FR
PSTEPS = SEQ // FR
BP = 4
BLOCKS = PAIRS // BP
DFF = 5632
FB = 512
NFB = DFF // FB
EPS = 1e-6
UNIT = 2048
U_S5, U_QK, U_V, U_OG = 0, 8, 16, 24
U_GLU, U_OUT, U_FFN = 32, 36, 52
N_UNITS = U_FFN + 12 * NFB
COL_V, COL_OG, COL_GATE, COL_U = QK, QK + DA, QK + 2 * DA, QK + 2 * DA + 2 * H
MASKED = -1.0e30
ROUND = 12582912.0
TWO_PI = 2.0 * np.pi
PI2_A = 6.28125
PI2_B = float(np.float32(np.floor((TWO_PI - PI2_A) * 2.0**20) / 2.0**20))
PI2_C = float(np.float32(TWO_PI - PI2_A - PI2_B))
KB = 1024
GP = 12
GW = GP * (KT - 1) + P

R_CONV, R_BCONV, R_BGLU, R_GMH, R_S5D, R_HIST = 0, 4, 5, 6, 7, 8
NROWS = R_HIST + NB * HIST


def build(nc, a, o):
    base = nc.sbuf_base + (-nc.sbuf_base) % 32
    CONST, RING, R1, R2 = 0, 7 * KB, 55 * KB, 135 * KB

    def at(name, shape, offset, dtype=F32):
        return nc.alloc_sbuf_tensor_at(name, shape, dtype, offset=base + offset)

    place = [CONST]

    def const(name, shape, dtype=F32):
        t = at(name, shape, place[0], dtype)
        place[0] += -(-int(np.prod(shape[1:])) * 4 // 32) * 32
        assert place[0] <= 7 * KB, place[0]
        return t

    ident = const("ident", [P, P])
    mask_prompt = const("mask_prompt", [P, P])
    mask_sample = const("mask_sample", [P, P])
    chan = const("chan", [P, 8, NROWS])
    conv_tail = const("conv_tail", [P, 8, 27])
    diag16 = const("diag16", [P, GI])
    n0 = const("n0", [P, NB, H])
    n_new = const("n_new", [P, NB, H])
    exp_neg_m = const("exp_neg_m", [P, TT, H])
    stat = const("stat", [P, 8, 20])
    bgate = const("bgate", [36, 1])
    m0s = const("m0s", [4, NB])
    decay = const("decay", [P, H, NB])
    vec = const("vec", [P, NROWS])

    raw = [at(f"raw{s}", [P, UNIT], RING + 8 * KB * s) for s in range(2)]
    w_hi = [at(f"w_hi{s}", [P, UNIT], RING + 16 * KB + 8 * KB * s, F32R) for s in range(2)]
    w_lo = [at(f"w_lo{s}", [P, UNIT], RING + 32 * KB + 8 * KB * s, F32R) for s in range(2)]

    xt_hi = at("xt_hi", [P, KT, T], R1, F32R)
    xt_lo = at("xt_lo", [P, KT, T], R1 + 40 * KB, F32R)
    qk = at("qk", [P, 8, T], R2)
    junk = at("junk", [P, D], R2)
    va = at("va", [P, TT, H, VA1], R2 + 20 * KB)
    xrow = [at(f"xrow{s}", [P, D], place) for s, place in
            enumerate((R2 + 41 * KB, R2 + 49 * KB, RING + 32 * KB, RING + 40 * KB))]
    gbc = at("gbc", [P, D], R2 + 57 * KB)
    cn = at("cn", [P, 2, 8, NS], R2 + 67 * KB + 512)
    rows_in = at("rows_in", [NROWS, QK], R2 + 20 * KB)
    dis = at("dis", [PAIRS, 16, P], R2 + 24 * KB)
    ldt = at("ldt", [PAIRS, 2, 2], R2 + 32 * KB)
    b_in = at("b_in", [P, 2, PAIRS, GI], R2 + 33 * KB)
    n_in = at("n_in", [NB * H, P], R2 + 37 * KB)
    fct = at("fct", [P, 2, PAIRS], R2 + 37 * KB + 512)
    gate_w = at("gate_w", [P, KT, 8], R2 + 38 * KB)
    gate_win = at("gate_win", [P, GW], R2 + 38 * KB + 512)
    gate_w_hi = at("gate_w_hi", [P, GW], R2 + 15 * KB, F32R)
    gate_w_lo = at("gate_w_lo", [P, GW], R2 + 17 * KB, F32R)
    gate_tmp = at("gate_tmp", [36, T], R2 + 12 * KB)
    stmp = at("stmp", [P, 2, PAIRS, GI], R2 + 8 * KB)
    u_out = [at(f"u_out{s}", [P, FR, STEPS], R2 + 41 * KB + 2560 * s) for s in range(2)]
    conv_in = [at(f"conv_in{s}", [P, HIST + SEQ + NB * (HIST + DSEQ)], R2 + 46 * KB + 2688 * s)
               for s in range(2)]
    og_out = [at(f"og_out{s}", [P, 512], R2 + 51 * KB + 512 + 2048 * s) for s in range(2)]
    bbar = at("bbar", [P, 2, PAIRS, GI], R2 + 57 * KB)
    c0t = at("c0t", [P, 2, PAIRS, GI], R2 + 61 * KB)
    lbp = at("lbp", [P, 2, PAIRS, FR + 1], R2 + 65 * KB)
    conv_acc = at("conv_acc", [P, T], R2 + 67 * KB + 512)

    u_in = at("u_in", [P, G, STEPS], R1)
    sst = at("sst", [P, 2, PAIRS, STEPS], R1 + 20 * KB)
    fin = at("fin", [P, 2, 1 + NB, PAIRS], R1 + 40 * KB)
    Q = R1 + 42 * KB + 256
    bpw = at("bpw", [P, 2, BP, P], Q)
    bwt = at("bwt", [P, 2, BP, P], Q + 4 * KB)
    cpw = [at(f"cpw{s}", [P, 2, BP, (FR + 1) * GI], Q + 8 * KB + 4608 * s) for s in range(2)]
    kpad = at("kpad", [P, 15 * GI], Q + 17 * KB)
    bdiag = at("bdiag", [P, 2, BP, 2 * GI], Q + 18 * KB)
    toep = [at(f"toep{s}", [P, 8, P], Q + place * KB) for s, place in enumerate((19, 23, 0, 4))]
    tail_out = at("tail_out", [27, QK], Q + 19 * KB)
    y_out = [at(f"y_out{s}", [P, BP, 2, STEPS], Q + 27 * KB + 2560 * s) for s in range(2)]
    stream_tmp = [at(f"stream_tmp{s}", [P, 2, PAIRS, NB], Q + 27 * KB + 2560 * s) for s in range(2)]
    ctmp = at("ctmp", [P, BP, (FR + 1) * GI], Q + 32 * KB)
    btmp = at("btmp", [P, BP, P], Q + 34 * KB + 256)
    scan_tmp = at("scan_tmp", [P, 2, 2, PAIRS], Q + 36 * KB + 256)
    lam8 = at("lam8", [P, 2, 2, PAIRS], Q + 36 * KB + 768)
    s5_io = at("s5_io", [P, 2, 2, P], RING + 46 * KB)
    s5p_out = at("s5p_out", [PAIRS, 2, P], R2 + 56 * KB)
    np_out = at("np_out", [H, P], RING + 45 * KB)
    ns_out = at("ns_out", [NB * H, P], RING + 45 * KB + 512)
    g_rows = [at(f"g_rows{s}", [4, T], R2 + 41 * KB + 2560 * s) for s in range(6)]
    r_li, r_lf, r_a, r_b, r_g, r_m = g_rows
    t_rows = [at(f"t_rows{s}", [4, T], RING + 30 * KB + 2560 * s) for s in range(4)]
    qgm = at("qgm", [P, 1152], R2 + 67 * KB + 384)
    ct = at("ct", [P, H, VA1], RING)
    hraw = [at(f"hraw{s}", [P, H, VA1], RING + 4128 * (s + 1)) for s in range(2)]
    dt = at("dt", [P, H, P], RING + 12 * KB + 512)
    pt = at("pt", [P, H, P], RING + 14 * KB + 512)
    qg = at("qg", [P, H, P], RING + 16 * KB + 512)
    kw = at("kw", [P, H, P], RING + 18 * KB + 512)
    ksb = at("ksb", [P, H, P], RING + 20 * KB + 512)
    sel = at("sel", [4, 4, P], RING + 22 * KB + 512)
    kwall = at("kwall", [P, NB, P], RING + 24 * KB + 512)
    cts = at("cts", [P, NB, VA1], RING + 28 * KB + 512)
    c0n = [at("c0n0", [P, 2, NB, P], Q), at("c0n1", [P, 2, NB, P], RING + 37 * KB)]
    cp_out = at("cp_out", [P, 2 * H, P], RING + 4128 * 2)

    ot_hi = at("ot_hi", [P, KT, T], R1, F32R)
    ot_lo = at("ot_lo", [P, KT, T], R1 + 40 * KB, F32R)
    z_hi = at("z_hi", [P, 8, T], R2, F32R)
    z_lo = at("z_lo", [P, 8, T], R2 + 20 * KB, F32R)
    z = at("z", [P, 8, T], R2 + 40 * KB)
    oa = at("oa", [P, H, VA1], R2 + 60 * KB)
    og_in = at("og_in", [P, H, DV], R2 + 60 * KB + 4128)
    ob = at("ob", [P, T], R2 + 68 * KB + 512)
    sq_out = at("sq_out", [P, DV], R2 + 71 * KB)
    mix = at("mix", [P, TT, D], R2)
    g_post = at("g_post", [P, D], R2 + 40 * KB)
    g_ffn = at("g_ffn", [P, D], R2 + 48 * KB)
    xres = [at(f"xres{s}", [P, D], place) for s, place in
            enumerate((R2 + 56 * KB, R2 + 64 * KB, RING + 32 * KB, RING + 40 * KB))]
    ht_hi = at("ht_hi", [P, KT, T], R1, F32R)
    ht_lo = at("ht_lo", [P, KT, T], R1 + 40 * KB, F32R)
    acc = at("acc", [P, TT, D], R2)
    h_hi = at("h_hi", [P, 4, T], R2 + 40 * KB, F32R)
    h_lo = at("h_lo", [P, 4, T], R2 + 50 * KB, F32R)
    sg = at("sg", [P, 2, HALF], R2 + 60 * KB)
    hid = at("hid", [P, 2, HALF], R2 + 62 * KB + 512)
    g_last = at("g_last", [P, D], R1 + 40 * KB)
    xlast = [at(f"xlast{t}", [P, D], R1 + 8 * t * KB) for t in range(TT)]

    def dram(name, shape):
        return nc.dram_tensor(name, shape, F32, kind="Internal").ap()

    u_dram = dram("u_dram", (DB, T))
    y_dram = dram("y_dram", (DB, T))
    gate_dram = dram("gate_dram", (2, H, T))
    og_dram = dram("og_dram", (T, DA))
    oa_dram = dram("oa_dram", (T, H * VA1))
    k_dram = dram("k_dram", (BLOCKS, P, 15 * GI))
    x_dram = dram("x_dram", (T, D))

    with ExitStack() as ctx:
        psum = ctx.enter_context(nc.psum_tensor("psum", [P, 8, 512], F32))

        def sem(name):
            return ctx.enter_context(nc.semaphore(name))

        raw_loaded = [sem(f"raw_loaded{s}") for s in range(2)]
        hi_ready, lo_ready = sem("hi_ready"), sem("lo_ready")
        pe_done = sem("pe_done")
        const_ready = sem("const_ready")
        x_loaded = [sem(f"x_loaded{s}") for s in range(4)]
        g_loaded, small_loaded = sem("g_loaded"), sem("small_loaded")
        ssq_ready, mean_ready, root_ready = sem("ssq_ready"), sem("mean_ready"), sem("root_ready")
        normed = sem("normed")
        tr_done, tr_hi, tr_lo = sem("tr_done"), sem("tr_hi"), sem("tr_lo")
        dve_chain, act_chain, pool_chain = sem("dve_chain"), sem("act_chain"), sem("pool_chain")
        dis_act, dis_dve = sem("dis_act"), sem("dis_dve")
        small_tr, small_ev = sem("small_tr"), sem("small_ev")
        gate_w_ready, gates_done, gates_evac, gates_stored, gates_loaded = (
            sem("gate_w_ready"), sem("gates_done"), sem("gates_evac"), sem("gates_stored"),
            sem("gates_loaded"))
        s5_consts = sem("s5_consts")
        bank_free = sem("bank_free")
        tok_evac = sem("tok_evac")
        u_evac, u_stored = sem("u_evac"), [sem(f"u_stored{s}") for s in range(2)]
        conv_filled = sem("conv_filled")
        conv_read = sem("conv_read")
        conv_step, conv_summed, silu_done = sem("conv_step"), sem("conv_summed"), sem("silu_done")
        og_stored = [sem(f"og_stored{s}") for s in range(2)]
        ones_ready = sem("ones_ready")
        u_loaded, s5_in = sem("u_loaded"), sem("s5_in")
        row_act, row_dve = sem("row_act"), sem("row_dve")
        tail_done, tail_ev, tail_stored = sem("tail_done"), sem("tail_ev"), sem("tail_stored")
        s5_state_tr, s5_state_in = sem("s5_state_tr"), sem("s5_state_in")
        bpw_ready, bwt_done, bwt_ready = sem("bpw_ready"), sem("bwt_done"), sem("bwt_ready")
        v_done, v_evac = sem("v_done"), sem("v_evac")
        cpw_ready, bdiag_ready = sem("cpw_ready"), sem("bdiag_ready")
        k_done, k_ready, k_stored = sem("k_done"), sem("k_ready"), sem("k_stored")
        scan_step, scan_done = sem("scan_step"), sem("scan_done")
        toep_loaded = [sem(f"toep_loaded{s}") for s in range(4)]
        y_done, y_evac = sem("y_done"), sem("y_evac")
        y_stored = [sem(f"y_stored{s}") for s in range(2)]
        sel_ready, em_done, em_ready = sem("sel_ready"), sem("em_done"), sem("em_ready")
        arg_done, s_done, gb_done, kt_done = (
            sem("arg_done"), sem("s_done"), sem("gb_done"), sem("kt_done"))
        dt_ready, pt_ready, qg_ready, kw_ready, ksb_ready = (
            sem("dt_ready"), sem("pt_ready"), sem("qg_ready"), sem("kw_ready"), sem("ksb_ready"))
        num_done, num_evac, dc_done, ct_ready = (
            sem("num_done"), sem("num_evac"), sem("dc_done"), sem("ct_ready"))
        h_stored = [sem(f"h_stored{s}") for s in range(2)]
        c0_loaded = [sem(f"c0_loaded{s}") for s in range(2)]
        c0_stored = [sem(f"c0_stored{s}") for s in range(2)]
        ctr_done, cts_ready, un_done, c_new = (
            sem("ctr_done"), sem("cts_ready"), sem("un_done"), sem("c_new"))
        qgm_ready, kwall_ready, nn_done = sem("qgm_ready"), sem("kwall_ready"), sem("nn_done")
        fin_tr, fin_ev, out_stored = sem("fin_tr"), sem("fin_ev"), sem("out_stored")
        z_loaded, z_ready, z_hi_ready, z_lo_ready = (
            [sem(f"z_loaded{s}") for s in range(2)], sem("z_ready"), sem("z_hi_ready"), sem("z_lo_ready"))
        oa_loaded, oa_sums, oa_mean, oa_root, oa_ready = (
            sem("oa_loaded"), sem("oa_sums"), sem("oa_mean"), sem("oa_root"), sem("oa_ready"))
        oat_done, oat_hi, oat_lo = sem("oat_done"), sem("oat_hi"), sem("oat_lo")
        gate_ready, ob_first, ob_ready, ob_hi, ob_lo = (
            sem("gate_ready"), sem("ob_first"), sem("ob_ready"), sem("ob_hi"), sem("ob_lo"))
        gp_loaded, xr_loaded = sem("gp_loaded"), [sem(f"xr_loaded{s}") for s in range(4)]
        mix_normed, xr_ready, xr_stored = (
            sem("mix_normed"), sem("xr_ready"), [sem(f"xr_stored{s}") for s in range(4)])
        acc_zero, sg_ready, hid_ready, h_hi_ready, h_lo_ready = (
            sem("acc_zero"), sem("sg_ready"), sem("hid_ready"), sem("h_hi_ready"), sem("h_lo_ready"))
        last_loaded = [sem(f"last_loaded{t}") for t in range(TT)]
        ff_normed, y_ready = sem("ff_normed"), [sem(f"y_ready{t}") for t in range(TT)]
        res_stored = sem("res_stored")
        def step_slices(tile):
            if tile < SAMPLE:
                return a["x_prompt"][0, P * tile:P * (tile + 1), :]
            return a["x_sample"].rearrange("b t d -> (b t) d")

        w_in, w_glu, w_out = a["w_in"][0], a["w_glu"][0], a["w_out"][0]
        w_gate, w_up, w_down = a["w_gate"][0], a["w_up"][0], a["w_down"][0]

        def cols_of(w, col, width=P):
            return w[:, bass.ds(col, width)].rearrange("(k p) n -> p k n", p=P)

        def rows_of(w, row, col):
            return w[bass.ds(row, 4 * P), bass.ds(col, 512)].rearrange("(k p) n -> p k n", p=P)

        def as_unit(t, k):
            return t[:].rearrange("p (k n) -> p k n", k=k)

        def streams(t):
            return t[:, HIST + SEQ:].rearrange("p (b s) -> p b s", b=NB)

        def output_powers(eng, after, k):
            pairs = slice(BP * k, BP * (k + 1))
            shape = [P, BP, FR + 1, GI]
            lr, li = (lbp[:, r, pairs, :].unsqueeze(3).to_broadcast(shape) for r in range(2))
            cr, ci = (c0t[:, r, pairs, :].unsqueeze(2).to_broadcast(shape) for r in range(2))
            dst = [cpw[k % 2][:, r, :, :].rearrange("p q (k i) -> p q k i", i=GI) for r in range(2)]
            tmp = ctmp[:].rearrange("p q (k i) -> p q k i", i=GI)
            eng.tensor_tensor(dst[0], lr, cr, ALU.mult)
            after(eng.tensor_tensor(tmp, li, ci, ALU.mult))
            after(eng.tensor_tensor(dst[0], dst[0], tmp, ALU.add))
            eng.tensor_tensor(dst[1], lr, ci, ALU.mult)
            after(eng.tensor_tensor(tmp, li, cr, ALU.mult))
            return eng.tensor_tensor(dst[1], dst[1], tmp, ALU.subtract)

        PIPE = [(stage, k - lag) for k in range(TT + 2) for stage, lag in (("sums", 0), ("split", 1))
                if 0 <= k - lag < TT]
        PIPE2 = [(stage, k - lag) for k in range(TT + 2)
                 for stage, lag in (("mix", 0), ("hidden", 1), ("split", 2)) if 0 <= k - lag < TT]

        s5_c = {0: a["s5_c_re"], 1: a["s5_c_im"]}
        s5_b = {0: a["s5_b_re"], 1: a["s5_b_im"]}
        s5_state = {0: a["state_s5_re"], 1: a["state_s5_im"]}
        ON_POOL = (0, 2)
        N_SMALL = 18
        block = ctx.enter_context(nc.Block())

        OUT_SMALL = 9

        def store_y(sp, t):
            dst = (o["y_prompt"][0, P * t:P * (t + 1), :] if t < SAMPLE else
                   o["y_sample"].rearrange("b t d -> (b t) d"))
            sp.wait_ge(y_ready[t], 1)
            sp.dma_start(dst, xlast[t][:]).then_inc(res_stored, 16)

        @block.sync
        def _(sp):
            def load(n, s, src, k):
                sp.wait_ge(lo_ready, n - 1)
                sp.dma_start(as_unit(raw[s], k), src).then_inc(raw_loaded[s], 16)

            for t in (1, 3):
                sp.dma_start(xrow[t][:], step_slices(t)).then_inc(x_loaded[t], 16)
            for s in range(2):
                sp.dma_start(as_unit(raw[s], KT), cols_of(w_in, COL_U + P * s)).then_inc(raw_loaded[s], 16)
            with sp.Fori(1, 4) as i:
                for j in range(2):
                    load(2 * i + j, j, cols_of(w_in, 2 * P * i + (COL_U + P * j)), KT)
            with sp.Fori(0, 4) as i:
                for j in range(2):
                    load(2 * i + (U_QK + j), j, cols_of(w_in, 2 * P * i + P * j), KT)
            with sp.Fori(0, 4) as i:
                for j in range(4):
                    load(4 * i + (U_V + j), j % 2, rows_of(w_in, 4 * P * j, 512 * i + COL_V), 4)
            sp.wait_ge(gates_stored, 32)
            for s in range(2):
                sp.wait_ge(u_stored[s], 16 * 5)
            for g in range(2):
                sp.dma_start((r_li, r_lf)[g][:], gate_dram[g]).then_inc(gates_loaded, 16)
            sp.wait_ge(pe_done, 5 * U_GLU)
            for r in range(FR):
                sp.dma_start(u_in[GI * (7 - r):GI * (8 - r), :, :],
                             u_dram[:, STEPS * r:STEPS * (r + 1)].rearrange("(g i) c -> i g c", i=GI)
                             ).then_inc(u_loaded, 16)
            for r in range(2):
                sp.dma_start(s5_io[:, r, :, :],
                             s5_state[r][0].rearrange("b (a g) p -> (b a) (g p)", g=2)
                             .rearrange("(q x) p -> x q p", q=2)).then_inc(s5_in, 16)
            for k in range(BLOCKS):
                sp.wait_ge(k_ready, 2 * k + 2)
                sp.dma_start(k_dram[k], kpad[:]).then_inc(k_stored, 16)

            def head_state(x, h, v):
                return x[0, :, h].rearrange("b (v p) d -> v p b d", v=2)[v]

            def load_c0(h):
                for v in range(2):
                    sp.dma_start(c0n[h % 2][:, v, :, :], head_state(a["state_mlstm_c"], h, v)
                                 ).then_inc(c0_loaded[h % 2], 16)

            def load_toep(k):
                sp.wait_ge(k_stored, 16 * (k + 1))
                for r in range(FR):
                    sp.dma_start(toep[k % 4][GI * r:GI * (r + 1), :, :],
                                 k_dram[k].rearrange("(g j) c -> j g c", j=GI)[:, :, GI * r:GI * r + P]
                                 ).then_inc(toep_loaded[k % 4], 16)

            sp.wait_ge(v_done, BLOCKS)
            sp.wait_ge(row_act, 3)
            load_c0(0)
            load_c0(1)
            sp.wait_ge(tail_stored, 32)
            load_toep(0)
            load_toep(1)
            for h in range(H):
                sp.wait_ge(c_new, 4 * (h + 1))
                for v in range(2):
                    sp.dma_start(head_state(o["c_s"], h, v), c0n[h % 2][:, v, :, :]
                                 ).then_inc(c0_stored[h % 2], 16)
                if h + 2 < H:
                    sp.wait_ge(c0_stored[h % 2], 32)
                    load_c0(h + 2)
            sp.wait_ge(ct_ready, H * TT)
            for s in range(2):
                sp.wait_ge(c0_stored[s], 64)
                sp.wait_ge(h_stored[s], 16 * (3 - s))
            load_toep(2)
            load_toep(3)
            sp.wait_ge(out_stored, 16 * OUT_SMALL)
            for j in range(2):
                load(U_GLU + j, j, cols_of(w_glu, 256 * j, 256), 8)

            def load_z(k):
                sp.wait_ge(y_stored[k % 2], 16 * FR * (k // 2 + 1))
                if k >= 2:
                    sp.wait_ge(z_loaded[k % 2], 16 * (k // 2))
                sp.dma_start(z[:, k, :], y_dram[P * k:P * (k + 1), :]).then_inc(z_loaded[k % 2], 16)

            for k in range(BLOCKS):
                sp.wait_ge(y_evac, 2 * k + 2)
                for t in range(FR):
                    sp.dma_start(
                        y_dram[P * k:P * (k + 1), STEPS * t:STEPS * (t + 1)].rearrange("(g i) c -> i g c", i=GI),
                        y_out[k % 2][GI * t:GI * (t + 1), :, :, :].rearrange("i q g c -> i (q g) c")
                    ).then_inc(y_stored[k % 2], 16)
                if k + 4 < BLOCKS:
                    sp.wait_ge(y_done, k + 1)
                    load_toep(k + 4)
                if k:
                    load_z(k - 1)
            load_z(BLOCKS - 1)
            sp.wait_ge(cpw_ready, 2 * BLOCKS)

            def load_oa(t):
                rows = slice(P * t, P * (t + 1))
                sp.dma_start(oa[:].rearrange("p h v -> p (h v)"), oa_dram[rows, :]).then_inc(oa_loaded, 16)
                sp.dma_start(og_in[:].rearrange("p h v -> p (h v)"), og_dram[rows, :]).then_inc(oa_loaded, 16)

            for s in range(2):
                sp.wait_ge(og_stored[s], 16 * TT)
            load_oa(0)
            for t in range(1, TT):
                if t < 3:
                    load(U_GLU + 1 + t, (t - 1) % 2, cols_of(w_glu, 256 * (t + 1), 256), 8)
                else:
                    load(U_OUT + t - 3, (t - 1) % 2, rows_of(w_out, 4 * P * (t - 3), 0), 4)
                sp.wait_ge(oat_done, 2 * t)
                load_oa(t)
            for j in range(2, 4):
                load(U_OUT + j, j % 2, rows_of(w_out, 4 * P * j, 0), 4)
            with sp.Fori(1, 4) as i:
                for j in range(4):
                    load(4 * i + (U_OUT + j), j % 2, rows_of(w_out, 4 * P * j, 512 * i), 4)
            for s in range(2):
                sp.dma_start((g_post, g_ffn)[s][:], a[("g_post_mix", "g_pre_ffn")[s]].broadcast_to((P, D))
                             ).then_inc(gp_loaded, 16)
            for t in range(TT):
                if t == 2:
                    load(U_FFN, 0, cols_of(w_gate, 0), KT)
                    load(U_FFN + 1, 1, cols_of(w_up, 0), KT)
                if t == 2:
                    sp.wait_ge(pe_done, 5 * U_FFN)
                if t < 4:
                    sp.dma_start(xres[t][:], step_slices(t)).then_inc(xr_loaded[t], 16)
            for t in range(TT):
                sp.wait_ge(xr_ready, t + 1)
                sp.dma_start(x_dram[P * t:P * (t + 1), :], xres[t % 4][:]).then_inc(xr_stored[t % 4], 16)
                if t == 0:
                    sp.wait_ge(normed, TT + 1)
                    sp.wait_ge(xr_stored[0], 16)
                    sp.dma_start(xres[0][:], step_slices(4)).then_inc(xr_loaded[0], 16)
            for j in range(2, 8):
                load(U_FFN + j, j % 2, cols_of((w_gate, w_up)[j % 2], P * (j // 2)), KT)
            for j in range(4):
                load(U_FFN + 8 + j, j % 2, rows_of(w_down, 0, 512 * j), 4)
            with sp.Fori(1, NFB) as i:
                for j in range(4):
                    load(12 * i + (U_FFN + 2 * j), 0, cols_of(w_gate, FB * i + P * j), KT)
                    load(12 * i + (U_FFN + 2 * j + 1), 1, cols_of(w_up, FB * i + P * j), KT)
                for j in range(4):
                    load(12 * i + (U_FFN + 8 + j), j % 2, rows_of(w_down, FB * i, 512 * j), 4)
            sp.wait_ge(pe_done, 5 * (N_UNITS - 4))
            sp.dma_start(g_last[:], a["g_post_ffn"].broadcast_to((P, D))).then_inc(gp_loaded, 16)
            for s in range(4):
                sp.wait_ge(xr_stored[s], 32 if s == 0 else 16)
            for t in range(TT):
                sp.dma_start(xlast[t][:], x_dram[P * t:P * (t + 1), :]).then_inc(last_loaded[t], 16)
            for t in range(TT):
                store_y(sp, t)
            sp.wait_ge(res_stored, 16 * TT)

        @block.tensor
        def _(pe):
            PARTS = ((0, 0), (0, 1), (1, 0))

            def transpose_rows(src, first):
                for q in range(4):
                    n = first + q
                    if n >= 4:
                        pe.wait_ge(tr_lo, n - 3)
                    for k in range(4):
                        m = pe.transpose(psum[:, q, P * k:P * (k + 1)],
                                         src[:, P * (4 * q + k):P * (4 * q + k + 1)], ident[:])
                    m.then_inc(tr_done, 1)

            def channel_unit(slot, bank, rows, kts=KT, part=0):
                w = (w_hi[slot], w_lo[slot])
                width = UNIT // kts
                for k in range(kts):
                    for wp in range(2):
                        lhs = w[wp][:, width * k + P * part:width * k + P * (part + 1)]
                        for rp in range(2 - wp):
                            for h in range(2):
                                m = pe.matmul(psum[:, bank + h, 0:HALF], lhs,
                                              rows[rp][:, k, HALF * h:HALF * (h + 1)],
                                              start=(k == 0 and wp == 0 and rp == 0),
                                              stop=(k == kts - 1 and wp == 1))
                return m

            def row_unit(slot, rows, k0, first, last):
                w = (w_hi[slot], w_lo[slot])
                for t in range(TT):
                    for k in range(4):
                        for wp, rp in PARTS:
                            m = pe.matmul(psum[:, t, :], rows[rp][:, k0 + k, P * t:P * (t + 1)],
                                          w[wp][:, 512 * k:512 * (k + 1)],
                                          start=(first and k == 0 and wp == 0 and rp == 0),
                                          stop=(last and k == 3 and wp == 1))
                    m.then_inc(pe_done, 1)

            xt = (xt_hi, xt_lo)
            pe.wait_ge(const_ready, 3)
            for t in range(TT):
                pe.wait_ge(normed, t + 1)
                transpose_rows(xrow[t % 4], 4 * t)
            pe.wait_ge(small_loaded, 16 * N_SMALL)
            for c in range(8):
                pe.transpose(psum[:, 4, NROWS * c:NROWS * (c + 1)],
                             rows_in[:, P * c:P * (c + 1)], ident[0:NROWS, 0:NROWS])
            pe.transpose(psum[:, 4, 320:320 + NB * H], n_in[:], ident[0:NB * H, 0:NB * H]
                         ).then_inc(small_tr, 1)
            for r in range(2):
                for k in range(8):
                    for g in range(2):
                        m = pe.matmul(psum[64 * g:64 * g + 64, 5 + r, 64 * k:64 * (k + 1)], cn[:, r, k, :],
                                      ident[:].rearrange("p (a g i) -> p g a i", g=2, i=GI)[:, g],
                                      start=True, stop=True)
            m.then_inc(small_tr, 1)
            pe.wait_ge(tr_lo, 4 * TT)
            for j in range(2):
                pe.wait_ge(lo_ready, j + 1)
                channel_unit(j, 2 * j, xt).then_inc(pe_done, 5)
            with pe.Fori(1, 4) as i:
                for j in range(2):
                    pe.wait_ge(lo_ready, 2 * i + (j + 1))
                    pe.wait_ge(bank_free, 2 * i + (j - 1))
                    channel_unit(j, 2 * j, xt).then_inc(pe_done, 5)
            pe.wait_ge(gate_w_ready, 2)
            pe.wait_ge(small_ev, 2)
            for k in range(KT):
                for wp, rp in PARTS:
                    for h in range(2):
                        m = pe.matmul(psum[:, 4 + h, 0:HALF], (gate_w_hi, gate_w_lo)[wp][:, GP * k:GP * k + P],
                                      xt[rp][:, k, HALF * h:HALF * (h + 1)],
                                      start=(k == 0 and wp == 0 and rp == 0),
                                      stop=(k == KT - 1 and wp == 1))
            m.then_inc(gates_done, 1)
            pe.wait_ge(dis_dve, 2)
            for r in range(4):
                m = pe.transpose(psum[:, 6, PAIRS * r:PAIRS * (r + 1)], dis[:, r, :],
                                 ident[0:PAIRS, 0:PAIRS])
            m.then_inc(small_tr, 1)
            with pe.Fori(0, 4) as i:
                for j in range(2):
                    pe.wait_ge(lo_ready, 2 * i + (U_QK + j + 1))
                    pe.wait_ge(bank_free, 2 * i + (U_QK + j - 1))
                    channel_unit(j, 2 * j, xt).then_inc(pe_done, 5)
            pe.wait_ge(bank_free, 16)
            for j in range(4):
                pe.wait_ge(lo_ready, U_V + j + 1)
                row_unit(j % 2, xt, 4 * j, j == 0, j == 3)
            with pe.Fori(1, 4) as i:
                pe.wait_ge(tok_evac, 5 * i)
                for j in range(4):
                    pe.wait_ge(lo_ready, 4 * i + (U_V + j + 1))
                    row_unit(j % 2, xt, 4 * j, j == 0, j == 3)
            pe.wait_ge(small_ev, 3)
            for c in range(8):
                m = pe.transpose(psum[0:27, 6 + c // 4, P * (c % 4):P * (c % 4 + 1)],
                                 conv_tail[:, c, :], ident[:])
            m.then_inc(tail_done, 1)
            pe.wait_ge(s5_in, 32)
            for r in range(2):
                for q in range(2):
                    m = pe.transpose(psum[:, 5, P * (2 * r + q):P * (2 * r + q + 1)], s5_io[:, r, q, :],
                                     ident[:])
            m.then_inc(s5_state_tr, 1)
            pe.wait_ge(u_loaded, 16 * FR)
            pe.wait_ge(tail_ev, 1)
            pe.wait_ge(tok_evac, 20)
            pe.wait_ge(s5_state_in, 2)
            for k in range(BLOCKS):
                pe.wait_ge(bpw_ready, k + 1)
                if k:
                    pe.wait_ge(bwt_ready, k)
                for r in range(2):
                    for q in range(BP):
                        m = pe.transpose(psum[:, 6 + r, P * q:P * (q + 1)], bpw[:, r, q, :], ident[:])
                m.then_inc(bwt_done, 1)
                pe.wait_ge(cpw_ready, k + 1)
                pe.wait_ge(bdiag_ready, 2 * k + 2)
                if k:
                    pe.wait_ge(k_ready, 2 * k)
                for q in range(BP):
                    for r in range(2):
                        m = pe.matmul(psum[32 * q:32 * q + 32, 3, 0:P], bdiag[:, r, q, :],
                                      cpw[k % 2][:, r, q, 0:P], start=(r == 0), stop=(r == 1))
                m.then_inc(k_done, 1)
                pe.wait_ge(bwt_ready, k + 1)
                if k:
                    pe.wait_ge(v_evac, k)
                for r in range(2):
                    for q in range(BP):
                        for g in range(2):
                            m = pe.matmul(psum[64 * g:64 * g + 64, 4 + r, STEPS * q:STEPS * (q + 1)],
                                          bwt[:, r, q, 64 * g:64 * g + 64],
                                          u_in[:, 2 * (BP * k + q) + g, :], start=True, stop=True)
                m.then_inc(v_done, 1)
            pe.wait_ge(v_evac, BLOCKS)
            pe.wait_ge(k_ready, 2 * BLOCKS)
            pe.wait_ge(ones_ready, 1)
            pe.wait_ge(sel_ready, 1)
            pe.wait_ge(row_dve, 3)
            for t in range(TT):
                m = pe.matmul(psum[:, 7, 4 * t:4 * t + 4], r_m[:, P * t:P * (t + 1)], ident[0:4, 0:4],
                              start=True, stop=True)
            m.then_inc(em_done, 1)
            pe.wait_ge(row_act, 3)
            pe.wait_ge(silu_done, 9)
            for t in range(TT):
                rows = slice(P * t, P * (t + 1))
                mask = mask_prompt if t < SAMPLE else mask_sample
                if t:
                    pe.wait_ge(ct_ready, H * t)
                for h in range(H):
                    cols = slice(P * h, P * (h + 1))
                    pe.matmul(psum[:, 0, cols], sel[:, h, :], r_a[:, rows], start=True, stop=False)
                    pe.matmul(psum[:, 0, cols], r_b[:, rows], sel[:, h, :], start=False, stop=False)
                    m = pe.matmul(psum[:, 0, cols], ident[:], mask[:], start=False, stop=True)
                m.then_inc(arg_done, 1)
                for h in range(H):
                    m = pe.matmul(psum[:, 1, P * h:P * (h + 1)], qk[:, H + h, rows], qk[:, h, rows],
                                  start=True, stop=True)
                m.then_inc(s_done, 1)
                for h in range(H):
                    m = pe.matmul(psum[:, 2, P * h:P * (h + 1)], sel[:, h, :], r_g[:, rows],
                                  start=True, stop=True)
                m.then_inc(gb_done, 1)
                for h in range(H):
                    m = pe.transpose(psum[:, 3, P * h:P * (h + 1)], qk[:, H + h, rows], ident[:])
                m.then_inc(kt_done, 1)
                pe.wait_ge(pt_ready, t + 1)
                pe.wait_ge(qg_ready, t + 1)
                if t < SAMPLE:
                    pe.wait_ge(kw_ready, t + 1)
                    pe.wait_ge(ct_ready, max(H * t, 0))
                    for h in range(H):
                        n = H * t + h
                        if n >= 2:
                            pe.wait_ge(num_evac, n - 1)
                        pe.matmul(psum[:, 4 + h % 2, 0:VA1], pt[:, h, :], va[:, t, h, :],
                                  start=True, stop=False)
                        pe.matmul(psum[:, 4 + h % 2, 0:VA1], qg[:, h, :], ct[:, h, :],
                                  start=False, stop=True).then_inc(num_done, 1)
                        pe.matmul(psum[:, h, 0:VA1], kw[:, h, :], va[:, t, h, :],
                                  start=True, stop=True).then_inc(dc_done, 1)
                    continue
                pe.wait_ge(ksb_ready, 1)
                for h in range(H):
                    for v in range(2):
                        m = pe.transpose(psum[:, h // 2, P * (2 * (h % 2) + v):P * (2 * (h % 2) + v + 1)],
                                         ct[:, h, P * v:P * (v + 1)], ident[:])
                m.then_inc(fin_tr, 1)
                pe.transpose(psum[0:4, 6, 0:P], ct[:, :, DV], ident[:]).then_inc(fin_tr, 1)
                pe.wait_ge(em_ready, 1)
                for h in range(H):
                    c0 = c0n[h % 2]
                    pe.wait_ge(c0_loaded[h % 2], 32 * (h // 2 + 1))
                    if h == 0:
                        pe.wait_ge(fin_ev, 1)
                    else:
                        pe.wait_ge(c_new, 4 * h)
                    for b in range(NB):
                        for v in range(2):
                            m = pe.transpose(
                                psum[:, b // 2, P * (2 * (b % 2) + v):P * (2 * (b % 2) + v + 1)],
                                c0[:, v, b, :], ident[:])
                        if b % 2:
                            m.then_inc(ctr_done, 1)
                    pe.wait_ge(num_evac, H * t + h - 1)
                    pe.matmul(psum[:, 4 + h % 2, 0:VA1], pt[:, h, :], va[:, t, h, :],
                              start=True, stop=False)
                    pe.wait_ge(qgm_ready, h + 1)
                    pe.wait_ge(cts_ready, 5 * (h + 1))
                    for b in range(NB):
                        m = pe.matmul(psum[:, 4 + h % 2, 0:VA1], qgm[:, P * b:P * (b + 1)],
                                      cts[:, b, :], start=False, stop=(b == NB - 1))
                    m.then_inc(num_done, 1)
                    pe.wait_ge(kwall_ready, h + 1)
                    for v in range(2):
                        for q in range(2):
                            pe.matmul(psum[:, 2 * v + q, :], va[:, t, h, P * v:P * (v + 1)],
                                      kwall[:, 4 * q:4 * q + 4, :], start=True,
                                      stop=True).then_inc(un_done, 1)
                    if h:
                        pe.wait_ge(ct_ready, H * t + h)
                    pe.matmul(psum[:, 7, NB * h:NB * (h + 1)], ksb[:, h, :],
                              dt[:, h, DSEQ - 1::DSEQ], start=True, stop=True).then_inc(nn_done, 1)
            pe.wait_ge(ct_ready, H * TT)
            pe.wait_ge(fin_ev, 2)
            pe.transpose(psum[0:NB * H, 6, P:2 * P], n_new[:].rearrange("p b h -> p (b h)"),
                         ident[:]).then_inc(fin_tr, 1)
            pe.wait_ge(scan_done, 1)
            pe.wait_ge(c_new, 4 * H)
            for r in range(2):
                m = pe.transpose(psum[0:PAIRS, 0, P * r:P * (r + 1)], fin[:, r, 0, :], ident[:])
            m.then_inc(fin_tr, 1)
            for r in range(2):
                for q in range(2):
                    m = pe.transpose(
                        psum[:, 1, P * (2 * r + q):P * (2 * r + q + 1)],
                        fin[:, r, 1 + 4 * q:5 + 4 * q, :].rearrange("p b a -> p (b a)"), ident[:])
            m.then_inc(fin_tr, 1)
            pe.wait_ge(num_evac, H * TT)
            for k in range(BLOCKS):
                pe.wait_ge(cpw_ready, BLOCKS + k + 1)
                pe.wait_ge(toep_loaded[k % 4], 16 * FR * (k // 4 + 1))
                banks = (2, 3) if k % 2 else (4, 5)
                if k >= 2:
                    pe.wait_ge(y_evac, 2 * (k - 1))
                for q in range(BP):
                    for g in range(2):
                        out = psum[:, banks[g], STEPS * q:STEPS * (q + 1)]
                        states = slice(64 * g, 64 * g + 64)
                        pe.matmul(out, toep[k % 4][:, 2 * q + g, :], u_in[:, 2 * (BP * k + q) + g, :],
                                  start=True, stop=False)
                        for r in range(2):
                            m = pe.matmul(out, cpw[k % 2][states, r, q, GI:],
                                          sst[states, r, BP * k + q, :], start=False, stop=(r == 1))
                m.then_inc(y_done, 1)
            def mlstm_to_channels(t):
                pe.wait_ge(oa_ready, t + 1)
                for q in range(2):
                    n = 2 * t + q
                    if n >= 4:
                        pe.wait_ge(oat_lo, n - 3)
                    for k in range(4):
                        m = pe.transpose(psum[:, 4 + n % 4, P * k:P * (k + 1)],
                                         og_in[:, 2 * q + k // 2, P * (k % 2):P * (k % 2 + 1)], ident[:])
                    m.then_inc(oat_done, 1)

            pe.wait_ge(z_lo_ready, 8)
            pe.wait_ge(y_evac, 2 * BLOCKS)
            pe.wait_ge(fin_ev, 5)
            for j in range(4):
                pe.wait_ge(lo_ready, U_GLU + j + 1)
                for c in range(2):
                    if 2 * j + c >= 2:
                        pe.wait_ge(ob_ready, 2 * j + c - 1)
                    channel_unit(j % 2, 2 * c, (z_hi, z_lo), 8, c).then_inc(pe_done, 2 + c)
                mlstm_to_channels(j)
            mlstm_to_channels(TT - 1)
            pe.wait_ge(ob_lo, 8)
            pe.wait_ge(oat_lo, 2 * TT)
            with pe.Fori(0, 4) as i:
                pe.wait_ge(tok_evac, 5 * i + 20)
                for j in range(4):
                    pe.wait_ge(lo_ready, 4 * i + (U_OUT + j + 1))
                    row_unit(j % 2, (ot_hi, ot_lo), 4 * j, j == 0, j == 3)
            pe.wait_ge(tok_evac, 40)
            for t in range(TT):
                pe.wait_ge(normed, TT + t + 1)
                transpose_rows(mix[:, t, :], 4 * TT + 4 * t)
            pe.wait_ge(tr_lo, 8 * TT)
            BANKS = [q % 8 if q < 16 else q - 12 for q in range(20)]
            with pe.Fori(0, NFB) as i:
                for p in range(4):
                    if p == 0:
                        pe.wait_ge(tok_evac, 20 * i + 32)
                    elif p == 1:
                        pe.wait_ge(tok_evac, 20 * i + 40)
                    else:
                        pe.wait_ge(hid_ready, 8 * i + 2 * (p - 1))
                    for j in range(2):
                        pe.wait_ge(lo_ready, 12 * i + (U_FFN + 2 * p + j + 1))
                        channel_unit(j, 4 * (p % 2) + 2 * j, (ht_hi, ht_lo)).then_inc(pe_done, 5)
                for j in range(4):
                    pe.wait_ge(lo_ready, 12 * i + (U_FFN + 8 + j + 1))
                    w = (w_hi[j % 2], w_lo[j % 2])
                    for t in range(TT):
                        q = TT * j + t
                        if q == 0:
                            pe.wait_ge(h_lo_ready, 8 * i + 6)
                        elif q == 4:
                            pe.wait_ge(hid_ready, 8 * i + 8)
                        elif q >= 8:
                            pe.wait_ge(tok_evac, 20 * i + (40 + (q - 8 if q < 16 else q - 4) + 1))
                        for k in range(4):
                            if j == 0 and k == 3 and t == 0:
                                pe.wait_ge(h_lo_ready, 8 * i + 7)
                            if j == 0 and k == 3 and t == 2:
                                pe.wait_ge(h_lo_ready, 8 * i + 8)
                            for wp, rp in PARTS:
                                m = pe.matmul(psum[:, BANKS[q], :],
                                              (h_hi, h_lo)[rp][:, k, P * t:P * (t + 1)],
                                              w[wp][:, 512 * k:512 * (k + 1)],
                                              start=(k == 0 and wp == 0 and rp == 0),
                                              stop=(k == 3 and wp == 1))
                        m.then_inc(pe_done, 1)

        @block.scalar
        def _(act):
            chained = [0]

            def after(ins):
                chained[0] += 1
                ins.then_inc(act_chain, 1)
                act.wait_ge(act_chain, chained[0])

            def split(half, s):
                act.wait_ge(raw_loaded[s], 16 * half + 16)
                act.wait_ge(pe_done, 10 * half + (5 * s - 5))
                act.activation(w_hi[s][:], raw[s][:], ACT.Copy).then_inc(hi_ready, 1)

            act.dma_start(xrow[0][:], step_slices(0)).then_inc(x_loaded[0], 16)
            act.dma_start(gbc[:], a["g_pre_mix"].broadcast_to((P, D))).then_inc(g_loaded, 16)
            act.dma_start(xrow[2][:], step_slices(2)).then_inc(x_loaded[2], 16)
            n_small = [0]

            def small(dst, src):
                n_small[0] += 1
                act.dma_start(dst, src).then_inc(small_loaded, 16)

            small(rows_in[R_CONV:R_CONV + 4, :], a["w_conv"][0])
            for r, name in ((R_BCONV, "b_conv"), (R_BGLU, "b_glu"), (R_GMH, "g_mh"), (R_S5D, "s5_d")):
                small(rows_in[r:r + 1, :], a[name])
            small(rows_in[R_HIST:NROWS, :], a["state_conv"][0].rearrange("b j c -> (b j) c"))
            for r, name in ((4, "s5_lam_re"), (5, "s5_lam_im")):
                small(dis[:, r, :], a[name][0].rearrange("(a g) p -> a (g p)", g=2))
            small(ldt[:, 0, :], a["s5_log_dt"][0].rearrange("(a g) -> a g", g=2))
            for r in range(2):
                small(b_in[:, r, :, :], s5_b[r][0].rearrange("(a g) p i -> (g p) a i", g=2))
                small(cn[:, r, :, :], s5_c[r][0].rearrange("(k q) i p -> (q i) k p", q=8))
            small(bgate[0:4, :], a["b_igate"].rearrange("o h -> h o"))
            small(bgate[32:36, :], a["b_fgate"].rearrange("o h -> h o"))
            with nc.allow_non_contiguous_dma(reason="32 words"):
                small(m0s[:], a["state_mlstm_m"][0].rearrange("b h -> h b"))
            small(n_in[:], a["state_mlstm_n"][0].rearrange("b h d -> (b h) d"))
            small(gate_w[:], cols_of(w_in, COL_GATE, 8))
            assert n_small[0] == N_SMALL, n_small

            def rms_sums(n, src, scratch):
                act.activation(scratch, src, ACT.Square, accum_out=stat[:, 0, n:n + 1]).then_inc(ssq_ready, 1)
                act.wait_ge(mean_ready, n + 1)
                act.activation(stat[:, 2, n:n + 1], stat[:, 1, n:n + 1], ACT.Sqrt).then_inc(root_ready, 1)

            def tile_hi(dst, t, first):
                for q in range(4):
                    act.wait_ge(tr_done, first + q + 1)
                    act.activation(dst[:, 4 * q:4 * q + 4, P * t:P * (t + 1)],
                                   psum[:, q, :].rearrange("p (k n) -> p k n", k=4),
                                   ACT.Copy).then_inc(tr_hi, 1)

            for stage, t in PIPE:
                if stage == "sums":
                    act.wait_ge(x_loaded[t % 4], 16 * (t // 4 + 1))
                    rms_sums(t, xrow[t % 4][:], junk[:])
                    continue
                tile_hi(xt_hi, t, 4 * t)
                if t == 0:
                    act.dma_start(xrow[0][:], step_slices(4)).then_inc(x_loaded[0], 16)
                if t in (2, 3):
                    act.wait_ge(raw_loaded[t - 2], 16)
                    act.activation(w_hi[t - 2][:], raw[t - 2][:], ACT.Copy).then_inc(hi_ready, 1)
            act.wait_ge(small_tr, 1)
            act.activation(chan[:].rearrange("p c r -> p (c r)"), psum[:, 4, 0:8 * NROWS], ACT.Copy)
            act.activation(n0[:].rearrange("p b h -> p (b h)"), psum[:, 4, 320:320 + NB * H],
                           ACT.Copy).then_inc(small_ev, 1)
            act.wait_ge(small_tr, 2)
            act.wait_ge(normed, TT)
            act.activation(c0t[:, 0, :, :].rearrange("p a i -> p (a i)"), psum[:, 5, :],
                           ACT.Copy).then_inc(u_stored[1], 16)
            act.activation(c0t[:, 1, :, :].rearrange("p a i -> p (a i)"), psum[:, 6, :],
                           ACT.Copy, scale=-1.0).then_inc(small_ev, 1)
            act.wait_ge(gate_w_ready, 1)
            act.activation(gate_w_hi[:], gate_win[:], ACT.Copy).then_inc(dis_act, 1)
            act.activation(ldt[:, 1, :], ldt[:, 0, :], ACT.Exp).then_inc(dis_act, 1)
            act.wait_ge(dis_dve, 1)
            act.activation(dis[:, 10, :], dis[:, 6, :], ACT.Exp).then_inc(silu_done, 1)
            act.activation(dis[:, 11, :], dis[:, 7, :], ACT.Sin).then_inc(u_stored[0], 16)
            act.activation(dis[:, 12, :], dis[:, 9, :], ACT.Sin).then_inc(dis_act, 1)

            with act.Fori(0, 4) as i:
                for j in range(2):
                    act.wait_ge(pe_done, 10 * i + (5 * j + 5))
                    act.wait_ge(u_stored[j], 16 * i + 16)
                    act.activation(u_out[j][:, :, 0:40],
                                   psum[:, 2 * j, 0:HALF].rearrange("p (c r) -> p r c", r=FR),
                                   ACT.Copy).then_inc(u_evac, 1)
                    act.activation(u_out[j][:, :, 40:80],
                                   psum[:, 2 * j + 1, 0:HALF].rearrange("p (c r) -> p r c", r=FR),
                                   ACT.Copy).then_inc(bank_free, 1)
                    split(i + 1, j)
                    act.wait_ge(u_evac, 2 * i + (j + 1))
                    act.wait_ge(bank_free, 2 * i + (j + 1))
                    act.dma_start(u_dram[bass.ds(2 * P * i + P * j, P), :],
                                  u_out[j][:].rearrange("p r c -> p (r c)")).then_inc(u_stored[j], 16)
            act.wait_ge(gates_done, 1)
            for g in range(2):
                part = slice(32 * g, 32 * g + 4)
                for h in range(2):
                    m = act.activation(gate_tmp[part, HALF * h:HALF * (h + 1)], psum[part, 4 + h, 0:HALF],
                                       ACT.Identity, bias=bgate[part, :])
            m.then_inc(gates_evac, 1)
            act.wait_ge(gates_evac, 1)
            for g in range(2):
                act.dma_start(gate_dram[g], gate_tmp[32 * g:32 * g + 4, :]).then_inc(gates_stored, 16)
            act.wait_ge(s5_consts, 1)
            act.wait_ge(gates_stored, 32)
            with act.Fori(0, 4) as i:
                for j in range(2):
                    act.wait_ge(pe_done, 10 * i + (5 * (U_QK + j) + 5))
                    act.wait_ge(conv_read, 2 * i + (j + 1))
                    buf = conv_in[j]
                    act.activation(buf[:, HIST:HIST + HALF], psum[:, 2 * j, 0:HALF],
                                   ACT.Copy).then_inc(conv_filled, 1)
                    act.activation(buf[:, HIST + HALF:HIST + SEQ], psum[:, 2 * j + 1, 0:SEQ - HALF],
                                   ACT.Copy).then_inc(conv_filled, 1)
                    act.activation(streams(buf)[:, :, HIST:],
                                   psum[:, 2 * j + 1, SEQ - HALF:HALF].rearrange("p (b s) -> p b s", b=NB),
                                   ACT.Copy).then_inc(bank_free, 1)
                    split(i + (U_QK // 2 + 1), j)
                    act.wait_ge(conv_summed, 2 * i + (j + 1))
                    act.activation(qk[:, bass.ds(2 * i + j, 1), :], conv_acc[:].unsqueeze(1),
                                   ACT.Silu).then_inc(silu_done, 1)
            act.wait_ge(ones_ready, 1)
            with act.Fori(0, 2) as i:
                for j in range(4):
                    if j == 3:
                        for t in range(TT):
                            act.wait_ge(pe_done, 20 * i + (5 * (U_V + 3) + t + 1))
                            act.activation(va[:, t, bass.ds(2 * i, 2), 0:DV],
                                           psum[:, t, :].rearrange("p (h v) -> p h v", h=2),
                                           ACT.Copy).then_inc(tok_evac, 1)
                    split(2 * i + (U_V // 2 + 1 + j // 2), j % 2)
            for c in range(2):
                for j in range(4):
                    if j == 3:
                        for t in range(TT):
                            n = TT * c + t
                            act.wait_ge(pe_done, 5 * (U_OG + 4 * c + 3) + t + 1)
                            if n >= 2:
                                act.wait_ge(og_stored[n % 2], 16 * (n // 2))
                            act.activation(og_out[n % 2][:], psum[:, t, :], ACT.Sigmoid).then_inc(tok_evac, 1)
                            act.wait_ge(tok_evac, 10 + n + 1)
                            act.dma_start(og_dram[P * t:P * (t + 1), 512 * c:512 * (c + 1)],
                                          og_out[n % 2][:]).then_inc(og_stored[n % 2], 16)
                    if c == 0 or j < 2:
                        split(U_OG // 2 + 1 + 2 * c + j // 2, j % 2)
            act.wait_ge(tail_done, 1)
            act.activation(tail_out[:], psum[0:27, 6:8, :].rearrange("p b n -> p (b n)"),
                           ACT.Copy).then_inc(tail_ev, 1)
            act.wait_ge(s5_state_tr, 1)
            for r in range(2):
                act.activation(sst[:, r, :, PSTEPS::2].rearrange("p a b -> p b a"),
                               psum[:, 5, 256 * r:256 * (r + 1)].rearrange("p (b a) -> p b a", b=NB),
                               ACT.Copy).then_inc(s5_state_in, 1)
            for s in range(2):
                act.wait_ge(og_stored[s], 16 * TT)
            act.wait_ge(row_dve, 1)
            act.activation(t_rows[1][:], t_rows[0][:], ACT.Exp, scale=-1.0).then_inc(row_act, 1)
            act.wait_ge(row_dve, 2)
            act.activation(r_g[:], t_rows[2][:], ACT.Ln).then_inc(row_act, 1)
            act.wait_ge(row_dve, 4)
            act.activation(r_g[:], t_rows[2][:], ACT.Exp).then_inc(row_act, 1)
            act.wait_ge(tail_ev, 1)
            act.dma_start(o["conv_p"].rearrange("o b j c -> (o b j) c"), tail_out[0:3, :]).then_inc(tail_stored, 16)
            act.dma_start(o["conv_s"].rearrange("o b j c -> (o b j) c"), tail_out[3:27, :]).then_inc(tail_stored, 16)
            act.dma_start(o["m_p"].rearrange("o b h -> h (o b)"), r_m[:, SEQ - 1:SEQ]).then_inc(out_stored, 16)
            with nc.allow_non_contiguous_dma(reason="32 words"):
                act.dma_start(o["m_s"].rearrange("o b h -> h (o b)"), r_m[:, SEQ + DSEQ - 1::DSEQ]
                              ).then_inc(out_stored, 16)
            for k in range(BLOCKS):
                pairs = slice(BP * k, BP * (k + 1))
                act.wait_ge(bwt_done, k + 1)
                if k:
                    act.wait_ge(v_done, k)
                act.activation(bwt[:].rearrange("p r q n -> p r (q n)"), psum[:, 6:8, :],
                               ACT.Copy).then_inc(bwt_ready, 1)
                act.wait_ge(v_done, k + 1)
                for r in range(2):
                    v = psum[:, 4 + r, 0:BP * STEPS].rearrange("p (q c) -> p q c", q=BP)
                    act.activation(sst[:, r, pairs, 1:PSTEPS], v[:, :, 0:PSTEPS - 1], ACT.Copy)
                    act.activation(fin[:, r, 0, pairs], v[:, :, PSTEPS - 1], ACT.Copy)
                    act.activation(sst[:, r, pairs, PSTEPS + 1::2], v[:, :, PSTEPS::2], ACT.Copy)
                    m = act.activation(fin[:, r, 1:, pairs].rearrange("p b a -> p a b"), v[:, :, PSTEPS + 1::2], ACT.Copy)
                m.then_inc(v_evac, 1)
            act.wait_ge(em_done, 1)
            act.activation(exp_neg_m[:].rearrange("p t h -> p (t h)"), psum[:, 7, 0:TT * H], ACT.Exp,
                           scale=-1.0).then_inc(em_ready, 1)
            for t in range(TT):
                act.wait_ge(arg_done, t + 1)
                act.activation(dt[:].rearrange("p h n -> p (h n)"), psum[:, 0, :], ACT.Exp).then_inc(dt_ready, 1)
                if t == SAMPLE:
                    act.wait_ge(kt_done, TT)
                    act.activation(ksb[:].rearrange("p h n -> p (h n)"), psum[:, 3, :],
                                   ACT.Copy).then_inc(ksb_ready, 1)
                    act.wait_ge(fin_tr, 1)
                    act.wait_ge(h_stored[1], 32)
                    act.activation(cp_out[:].rearrange("p (b n) d -> p b (n d)", b=2), psum[:, 0:2, :],
                                   ACT.Copy).then_inc(fin_ev, 1)
                    act.wait_ge(fin_tr, 2)
                    act.activation(np_out[:], psum[0:4, 6, 0:P], ACT.Copy).then_inc(fin_ev, 1)
                if t >= 2:
                    act.wait_ge(h_stored[t % 2], 16 * (t // 2))
                for h in range(H):
                    if t == SAMPLE:
                        for q in range(4):
                            act.wait_ge(ctr_done, 4 * h + q + 1)
                            act.activation(cts[:, 2 * q:2 * q + 2, 0:DV],
                                           psum[:, q, :].rearrange("p (b v) -> p b v", b=2),
                                           ACT.Copy).then_inc(cts_ready, 1)
                    act.wait_ge(num_done, H * t + h + 1)
                    act.activation(hraw[t % 2][:, h, :], psum[:, 4 + h % 2, 0:VA1], ACT.Copy).then_inc(num_evac, 1)
                act.wait_ge(num_evac, H * (t + 1))
                act.dma_start(oa_dram[P * t:P * (t + 1), :],
                              hraw[t % 2][:].rearrange("p h v -> p (h v)")).then_inc(h_stored[t % 2], 16)
            act.wait_ge(fin_ev, 2)
            act.dma_start(o["c_p"][0, 0].rearrange("h (v p) d -> p (h v) d", v=2), cp_out[:]).then_inc(out_stored, 16)
            act.dma_start(o["n_p"][0, 0], np_out[:]).then_inc(out_stored, 16)
            act.wait_ge(fin_tr, 3)
            act.activation(ns_out[:], psum[0:NB * H, 6, P:2 * P], ACT.Copy).then_inc(fin_ev, 1)
            act.wait_ge(fin_tr, 4)
            act.activation(s5p_out[:].rearrange("a r p -> a (r p)"), psum[0:PAIRS, 0, 0:2 * P],
                           ACT.Copy).then_inc(fin_ev, 1)
            act.wait_ge(fin_tr, 5)
            act.activation(s5_io[:].rearrange("x r q p -> x (r q p)"), psum[:, 1, :],
                           ACT.Copy).then_inc(fin_ev, 1)
            act.wait_ge(fin_ev, 5)
            act.dma_start(o["n_s"][0].rearrange("b h d -> (b h) d"), ns_out[:]).then_inc(out_stored, 16)
            for r in range(2):
                act.dma_start(o[("s5re_p", "s5im_p")[r]][0, 0].rearrange("(a g) p -> a (g p)", g=2),
                              s5p_out[:, r, :]).then_inc(out_stored, 16)
                act.dma_start(o[("s5re_s", "s5im_s")[r]][0].rearrange("b (a g) p -> (b a) (g p)", g=2)
                              .rearrange("(q x) p -> x q p", q=2), s5_io[:, r, :, :]).then_inc(out_stored, 16)
            def z_part(c):
                if 0 <= c < BLOCKS:
                    act.wait_ge(z_loaded[c % 2], 16 * (c // 2 + 1))
                    act.activation(z[:, c, :], z[:, c, :], ACT.Gelu_apprx_tanh).then_inc(z_ready, 1)
                if c >= 1:
                    act.wait_ge(z_ready, c)
                    act.activation(z_hi[:, c - 1, :], z[:, c - 1, :], ACT.Copy).then_inc(z_hi_ready, 1)

            for k in range(BLOCKS):
                banks = (2, 3) if k % 2 else (4, 5)
                act.wait_ge(y_done, k + 1)
                if k >= 2:
                    act.wait_ge(y_stored[k % 2], 16 * FR * (k // 2))
                for g in range(2):
                    act.activation(y_out[k % 2][:, :, g, :],
                                   psum[:, banks[g], 0:BP * STEPS].rearrange("p (q c) -> p q c", q=BP),
                                   ACT.Copy).then_inc(y_evac, 1)
                if k < 2:
                    act.wait_ge(raw_loaded[k], 16 * (U_GLU // 2 + 1))
                    act.activation(w_hi[k][:], raw[k][:], ACT.Copy).then_inc(hi_ready, 1)
                z_part(k - 3)
            for c in range(BLOCKS - 3, BLOCKS + 1):
                z_part(c)

            def mlstm_tile(t):
                act.wait_ge(oa_loaded, 32 * (t + 1))
                for h in range(H):
                    m = act.activation(sq_out[:], oa[:, h, 0:DV], ACT.Square,
                                       accum_out=stat[:, 4, 4 * t + h:4 * t + h + 1])
                    if h < H - 1:
                        after(m)
                m.then_inc(oa_sums, 1)
                act.wait_ge(oa_mean, t + 1)
                act.activation(stat[:, 6, 4 * t:4 * t + 4], stat[:, 5, 4 * t:4 * t + 4],
                               ACT.Sqrt).then_inc(oa_root, 1)
                for q in range(2):
                    n = 2 * t + q
                    act.wait_ge(oat_done, n + 1)
                    for k in range(4):
                        m = act.activation(ot_hi[:, 4 * q + k, P * t:P * (t + 1)],
                                           psum[:, 4 + n % 4, P * k:P * (k + 1)], ACT.Copy,
                                           scale=chan[:, 4 * q + k, R_GMH:R_GMH + 1])
                    m.then_inc(oat_hi, 1)

            for j in range(4):
                for c in range(2):
                    n = 2 * j + c
                    act.wait_ge(pe_done, 5 * (U_GLU + j) + 2 + 3 * c)
                    act.activation(psum[:, 2 * c:2 * c + 2, 0:HALF], psum[:, 2 * c:2 * c + 2, 0:HALF],
                                   ACT.Sigmoid, bias=chan[:, n, R_BGLU:R_BGLU + 1]).then_inc(gate_ready, 1)
                    act.wait_ge(ob_ready, n + 1)
                    act.activation(ot_hi[:, 8 + n, :], ob[:], ACT.Copy).then_inc(ob_hi, 1)
                split((U_GLU + 2 + j) // 2, j % 2)
                mlstm_tile(j)
            mlstm_tile(TT - 1)
            def out_chunk(i, last=False):
                for j in range(4):
                    if j == 3:
                        for t in range(TT):
                            act.wait_ge(pe_done, 20 * i + (5 * (U_OUT + 3) + t + 1))
                            act.activation(mix[:, t, bass.ds(512 * i, 512)], psum[:, t, :],
                                           ACT.Copy).then_inc(tok_evac, 1)
                    if not (last and j >= 2):
                        split(2 * i + (U_OUT // 2 + 1 + j // 2), j % 2)

            with act.Fori(0, 3) as i:
                out_chunk(i)
            out_chunk(3, last=True)
            act.wait_ge(tok_evac, 40)
            n = TT
            for stage, t in PIPE2:
                if stage == "mix":
                    rms_sums(n, mix[:, t, :], psum[:, 4:8, :])
                elif stage == "hidden":
                    act.wait_ge(xr_ready, t + 1)
                    rms_sums(n, xres[t % 4][:], psum[:, 4:8, :])
                else:
                    tile_hi(ht_hi, t, 4 * TT + 4 * t)
                    if t >= 3:
                        split(U_FFN // 2, t - 3)
                n += stage != "split"
            for s in range(2):
                act.wait_ge(xr_stored[s], 16 * (2 - s))

            def ffn_block(i, last=False):
                for j in range(12):
                    p = j // 2
                    bank = 4 * (p % 2)
                    if j < 8 and j % 2 == 0:
                        act.wait_ge(pe_done, 60 * i + (5 * (U_FFN + j) + 5))
                        if p:
                            act.wait_ge(hid_ready, 8 * i + 2 * p)
                        for h in range(2):
                            act.activation(sg[:, h, :], psum[:, bank + h, 0:HALF], ACT.Silu).then_inc(sg_ready, 1)
                    elif j < 8:
                        for h in range(2):
                            act.wait_ge(hid_ready, 8 * i + (2 * p + h + 1))
                            if p == 0 and h == 0:
                                act.wait_ge(pe_done, 60 * i + 5 * U_FFN)
                            act.activation(h_hi[:, p, HALF * h:HALF * (h + 1)], hid[:, h, :],
                                           ACT.Copy).then_inc(h_hi_ready, 1)
                    if not (last and j >= 10):
                        split(6 * i + ((U_FFN + 2 + j) // 2), j % 2)

            with act.Fori(0, NFB - 1) as i:
                ffn_block(i)
            ffn_block(NFB - 1, last=True)
            for t in range(TT):
                act.wait_ge(tok_evac, 40 + 20 * NFB - TT + t + 1)
                rms_sums(3 * TT + t, acc[:, t, :], psum[:, 0:4, :])

        @block.vector
        def _(dve):
            chained = [0]

            def after(ins):
                chained[0] += 1
                ins.then_inc(dve_chain, 1)
                dve.wait_ge(dve_chain, chained[0])

            def split(n, s):
                dve.wait_ge(hi_ready, n + 1)
                dve.tensor_tensor(w_lo[s][:], raw[s][:], w_hi[s][:].bitcast(F32),
                                  ALU.subtract).then_inc(lo_ready, 1)

            def rms_factor(n):
                dve.wait_ge(ssq_ready, n + 1)
                dve.tensor_scalar(stat[:, 1, n:n + 1], stat[:, 0, n:n + 1], 1.0 / D, EPS, ALU.mult,
                                  ALU.add).then_inc(mean_ready, 1)
                dve.wait_ge(root_ready, n + 1)
                after(dve.reciprocal(stat[:, 3, n:n + 1], stat[:, 2, n:n + 1]))
                return stat[:, 3, n:n + 1]

            def tile_lo(hi, lo, t, first):
                for q in range(4):
                    dve.wait_ge(tr_hi, first + q + 1)
                    cols = (slice(None), slice(4 * q, 4 * q + 4), slice(P * t, P * (t + 1)))
                    dve.tensor_tensor(lo[cols], psum[:, q, :].rearrange("p (k n) -> p k n", k=4),
                                      hi[cols].bitcast(F32), ALU.subtract).then_inc(tr_lo, 1)

            for stage, t in PIPE:
                if stage == "sums":
                    f = rms_factor(t)
                    if t == 0:
                        dve.wait_ge(g_loaded, 16)
                    dve.scalar_tensor_tensor(out=xrow[t % 4][:], in0=xrow[t % 4][:], scalar=f, in1=gbc[:],
                                             op0=ALU.mult, op1=ALU.mult).then_inc(normed, 1)
                    continue
                tile_lo(xt_hi, xt_lo, t, 4 * t)
                if t in (2, 3):
                    split(t - 2, t - 2)
            after(dve.memset(gate_win[:], 0.0))
            dve.wait_ge(small_loaded, 16 * N_SMALL)
            for g in range(2):
                m = dve.tensor_copy(gate_win[:, 32 * g:32 * g + GP * KT].rearrange("p (k c) -> p k c", c=GP)[:, :, 0:4],
                                    gate_w[:, :, 4 * g:4 * g + 4])
            m.then_inc(gate_w_ready, 1)
            dve.wait_ge(dis_act, 1)
            dve.tensor_tensor(gate_w_lo[:], gate_win[:], gate_w_hi[:].bitcast(F32),
                              ALU.subtract).then_inc(gate_w_ready, 1)
            for s in range(2):
                dve.memset(conv_in[s][:, 0:HIST], 0.0).then_inc(conv_read, 1)
            dve.wait_ge(const_ready, 3)
            after(dve.tensor_reduce(diag16[:], ident[:].rearrange("p (g i) -> p i g", g=8), AX.X, ALU.add))

            def v(n):
                return dis[:, n, :]

            def tt(out, x, y, op):
                after(dve.tensor_tensor(v(out), v(x), v(y), op))

            LAM_RE, LAM_IM, EXPO, ANGLE, TURNS, COMP, MAG, SIN, COS, NR, DEN, T0 = range(4, 16)
            dve.wait_ge(dis_act, 2)
            step = ldt[:, 1, :].unsqueeze(2).to_broadcast([PAIRS, 2, NS])
            for dst, src in ((EXPO, LAM_RE), (ANGLE, LAM_IM)):
                after(dve.tensor_tensor(v(dst).rearrange("a (g p) -> a g p", g=2),
                                        v(src).rearrange("a (g p) -> a g p", g=2), step, ALU.mult))
            after(dve.tensor_scalar(v(TURNS), v(ANGLE), 1.0 / TWO_PI, ROUND, ALU.mult, ALU.add))
            after(dve.tensor_scalar(v(TURNS), v(TURNS), -ROUND, None, ALU.add))
            for part in (PI2_A, PI2_B, PI2_C):
                after(dve.scalar_tensor_tensor(out=v(ANGLE), in0=v(TURNS), scalar=-part, in1=v(ANGLE),
                                               op0=ALU.mult, op1=ALU.add))
            after(dve.tensor_scalar(v(ANGLE), v(ANGLE), 3.1415925, -3.1415925, ALU.min, ALU.max))
            after(dve.scalar_tensor_tensor(out=v(COMP), in0=v(ANGLE), scalar=-1.0, in1=v(ANGLE),
                                           op0=ALU.mult, op1=ALU.max))
            dve.tensor_scalar(v(COMP), v(COMP), -1.0, float(np.pi / 2), ALU.mult, ALU.add).then_inc(dis_dve, 1)
            dve.wait_ge(dis_act, 3)
            tt(0, MAG, COS, ALU.mult)
            tt(1, MAG, SIN, ALU.mult)
            after(dve.tensor_scalar(v(NR), v(0), -1.0, None, ALU.add))
            tt(DEN, LAM_RE, LAM_RE, ALU.mult)
            tt(T0, LAM_IM, LAM_IM, ALU.mult)
            tt(DEN, DEN, T0, ALU.add)
            after(dve.reciprocal(v(DEN), v(DEN)))
            tt(2, NR, LAM_RE, ALU.mult)
            tt(T0, 1, LAM_IM, ALU.mult)
            tt(2, 2, T0, ALU.add)
            tt(2, 2, DEN, ALU.mult)
            tt(3, 1, LAM_RE, ALU.mult)
            tt(T0, NR, LAM_IM, ALU.mult)
            tt(3, 3, T0, ALU.subtract)
            dve.tensor_tensor(v(3), v(3), v(DEN), ALU.mult).then_inc(dis_dve, 1)

            with dve.Fori(0, 4) as i:
                for j in range(2):
                    split(2 * i + (j + 2), j)
            dve.wait_ge(small_tr, 3)
            for r in range(2):
                dve.tensor_copy(lbp[:, r, :, 1], psum[:, 6, PAIRS * r:PAIRS * (r + 1)])
            dve.tensor_copy(fct[:].rearrange("p r a -> p (r a)"), psum[:, 6, 2 * PAIRS:4 * PAIRS]).then_inc(small_ev, 1)
            dve.wait_ge(small_ev, 3)
            STEPS_CONV = 9
            with dve.Fori(0, 4) as i:
                for j in range(2):
                    n = 2 * i + j
                    split(2 * i + (U_QK + j + 2), j)
                    buf = conv_in[j]
                    dve.wait_ge(conv_filled, 4 * i + (2 * j + 2))
                    dve.wait_ge(bank_free, 2 * i + (U_QK + j + 1))
                    base_n = 2 * STEPS_CONV * i + STEPS_CONV * j
                    dve.tensor_copy(vec[:], chan[:, bass.ds(n, 1), :].rearrange("p o r -> p (o r)")
                                    ).then_inc(conv_step, 1)
                    dve.tensor_copy(conv_tail[:, bass.ds(n, 1), 0:HIST].rearrange("p o j -> p (o j)"),
                                    buf[:, SEQ:SEQ + HIST])
                    dve.tensor_copy(conv_tail[:, bass.ds(n, 1), HIST:].rearrange("p o (b j) -> p (o b) j", b=NB),
                                    streams(buf)[:, :, DSEQ:]).then_inc(conv_step, 1)
                    dve.wait_ge(conv_step, base_n + 2)
                    dve.tensor_copy(streams(buf)[:, :, 0:HIST],
                                    vec[:, R_HIST:].rearrange("p (b j) -> p b j", b=NB)).then_inc(conv_step, 1)
                    dve.wait_ge(conv_step, base_n + 3)
                    dve.wait_ge(silu_done, n + 1)
                    for tap in range(CONV):
                        w = vec[:, tap:tap + 1]
                        for part in range(2):
                            if part == 0:
                                src, dst = buf[:, tap:tap + SEQ], conv_acc[:, 0:SEQ]
                            else:
                                src = streams(buf)[:, :, tap:tap + DSEQ]
                                dst = conv_acc[:, SEQ:].rearrange("p (b s) -> p b s", b=NB)
                            if tap == 0:
                                m = dve.tensor_scalar(dst, src, w, vec[:, R_BCONV:R_BCONV + 1], ALU.mult, ALU.add)
                            else:
                                m = dve.scalar_tensor_tensor(out=dst, in0=src, scalar=w, in1=dst,
                                                             op0=ALU.mult, op1=ALU.add)
                            if tap < CONV - 1:
                                m.then_inc(conv_step, 1)
                            elif part:
                                m.then_inc(conv_summed, 1)
                            else:
                                m.then_inc(conv_read, 1)
                        if tap < CONV - 1:
                            dve.wait_ge(conv_step, base_n + (3 + 2 * tap + 2))
            dve.wait_ge(s5_consts, 1)
            dve.wait_ge(gates_done, 1)
            dve.memset(va[:, :, :, DV:VA1].rearrange("p t h o -> p t (h o)"), 1.0).then_inc(ones_ready, 1)
            with dve.Fori(0, 3) as i:
                for j in range(4):
                    split(4 * i + (U_V + 2 + j), j % 2)
            for j in range(2):
                split(U_OG + 6 + j, j)
            t0, t1, t2, t3 = (t[:] for t in t_rows)
            dve.wait_ge(pe_done, 5 * U_GLU)
            dve.wait_ge(gates_loaded, 32)
            dve.scalar_tensor_tensor(out=t0, in0=r_lf[:], scalar=-1.0, in1=r_lf[:], op0=ALU.mult,
                                     op1=ALU.max).then_inc(row_dve, 1)
            dve.wait_ge(row_act, 1)
            dve.tensor_scalar(t2, t1, 1.0, None, ALU.add).then_inc(row_dve, 1)
            dve.wait_ge(row_dve, 2)
            dve.scalar_tensor_tensor(out=t3, in0=t2, scalar=-1.0, in1=t1, op0=ALU.add, op1=ALU.subtract)
            after(dve.reciprocal(t0, t2))
            after(dve.tensor_tensor(t3, t3, t0, ALU.mult))
            dve.wait_ge(row_act, 2)
            after(dve.tensor_tensor(r_g[:], r_g[:], t3, ALU.subtract))
            after(dve.scalar_tensor_tensor(out=r_lf[:], in0=r_lf[:], scalar=0.0, in1=r_g[:], op0=ALU.min,
                                           op1=ALU.subtract))
            after(dve.memset(t1, 0.0))
            for c in range(SAMPLE):
                seg = slice(P * c, P * (c + 1))
                dve.tensor_tensor_scan(t0[:, seg], r_lf[:, seg], t1[:, seg], 0.0, ALU.add, ALU.add)
            dve.tensor_tensor_scan(r_m[:, 0:SEQ], r_lf[:, 0:SEQ], r_li[:, 0:SEQ], 0.0, ALU.add, ALU.max)
            for b in range(NB):
                seg = slice(SEQ + DSEQ * b, SEQ + DSEQ * (b + 1))
                dve.tensor_tensor_scan(t0[:, seg], r_lf[:, seg], t1[:, seg], 0.0, ALU.add, ALU.add)
                m = dve.tensor_tensor_scan(r_m[:, seg], r_lf[:, seg], r_li[:, seg], m0s[:, b:b + 1],
                                           ALU.add, ALU.max)
            after(m)
            after(dve.tensor_tensor(r_a[:], t0, r_m[:], ALU.subtract))
            dve.tensor_tensor(r_b[:], r_li[:], t0, ALU.subtract).then_inc(row_dve, 1)
            dve.tensor_copy(t2[:, 0:P], r_a[:, 0:P])
            for c in range(1, SAMPLE):
                seg = slice(P * c, P * (c + 1))
                dve.tensor_scalar(t2[:, seg], r_a[:, seg], r_m[:, P * c - 1:P * c], None, ALU.add)
            dve.tensor_tensor(t2[:, SEQ:].rearrange("p (b s) -> p b s", b=NB),
                              r_a[:, SEQ:].rearrange("p (b s) -> p b s", b=NB),
                              m0s[:].unsqueeze(2).to_broadcast([4, NB, DSEQ]), ALU.add).then_inc(row_dve, 1)
            dve.tensor_copy(lam8[:, 0, 0, :], lbp[:, 0, :, FR])
            dve.tensor_copy(lam8[:, 0, 1, :], lbp[:, 0, :, FR])
            dve.tensor_scalar(lam8[:, 1, 0, :], lbp[:, 1, :, FR], -1.0, None, ALU.mult)
            dve.tensor_copy(lam8[:, 1, 1, :], lbp[:, 1, :, FR])
            dve.memset(sst[:, :, :, 0:1].rearrange("p r a o -> p r (a o)"), 0.0)
            dve.memset(kpad[:, 0:7 * GI], 0.0)
            after(dve.memset(bdiag[:], 0.0))
            dve.memset(qgm[:], 0.0)
            after(dve.memset(ct[:], 0.0))
            dve.wait_ge(small_ev, 2)
            for k in range(BLOCKS):
                pairs = slice(BP * k, BP * (k + 1))
                if k:
                    dve.wait_ge(k_done, k)
                for g in range(2):
                    dve.tensor_copy(bdiag[64 * g:64 * g + 64, :, :, GI * g:GI * (g + 1)],
                                    bbar[64 * g:64 * g + 64, :, pairs, :]).then_inc(bdiag_ready, 1)
                if k:
                    dve.wait_ge(bwt_done, k)
                shape = [P, BP, FR, GI]
                lr, li = (lbp[:, r, pairs, 0:FR].unsqueeze(3).to_broadcast(shape) for r in range(2))
                br, bi = (bbar[:, r, pairs, :].unsqueeze(2).to_broadcast(shape) for r in range(2))
                dst = [bpw[:, r, :, :].rearrange("p q (k i) -> p q k i", k=FR) for r in range(2)]
                tmp = btmp[:].rearrange("p q (k i) -> p q k i", k=FR)
                if k:
                    dve.wait_ge(bpw_ready, k)
                dve.tensor_tensor(dst[0], lr, br, ALU.mult)
                after(dve.tensor_tensor(tmp, li, bi, ALU.mult))
                after(dve.tensor_tensor(dst[0], dst[0], tmp, ALU.subtract))
                dve.tensor_tensor(dst[1], lr, bi, ALU.mult)
                after(dve.tensor_tensor(tmp, li, br, ALU.mult))
                dve.tensor_tensor(dst[1], dst[1], tmp, ALU.add).then_inc(bpw_ready, 1)
                dve.wait_ge(k_done, k + 1)
                if k:
                    dve.wait_ge(k_stored, 16 * k)
                dve.scalar_tensor_tensor(out=kpad[:, 7 * GI:8 * GI], in0=diag16[:],
                                         scalar=chan[:, k, R_S5D:R_S5D + 1], in1=psum[:, 3, 0:GI],
                                         op0=ALU.mult, op1=ALU.add).then_inc(k_ready, 1)
                dve.tensor_copy(kpad[:, 8 * GI:], psum[:, 3, GI:P]).then_inc(k_ready, 1)
            scale = float(DQK) ** -0.5
            for t in range(TT):
                rows = slice(P * t, P * (t + 1))
                dve.wait_ge(s_done, t + 1)
                dve.wait_ge(dt_ready, t + 1)
                dve.scalar_tensor_tensor(out=pt[:].rearrange("p h n -> p (h n)"), in0=psum[:, 1, :],
                                         scalar=scale, in1=dt[:].rearrange("p h n -> p (h n)"),
                                         op0=ALU.mult, op1=ALU.mult).then_inc(pt_ready, 1)
                dve.wait_ge(gb_done, t + 1)
                gb = psum[:, 2, :].rearrange("p (h n) -> p h n", h=H)
                if t < SAMPLE:
                    after(dve.tensor_copy(decay[:, :, 0], gb[:, :, P - 1]))
                else:
                    after(dve.tensor_copy(decay[:], gb[:, :, DSEQ - 1::DSEQ]))
                dve.scalar_tensor_tensor(out=qg[:], in0=qk[:, 0:H, rows], scalar=scale, in1=gb,
                                         op0=ALU.mult, op1=ALU.mult).then_inc(qg_ready, 1)
                if t < SAMPLE:
                    dve.wait_ge(kt_done, t + 1)
                    dve.tensor_tensor(kw[:], psum[:, 3, :].rearrange("p (h n) -> p h n", h=H),
                                      dt[:, :, P - 1:P].to_broadcast([P, H, P]), ALU.mult).then_inc(kw_ready, 1)
                    for h in range(H):
                        dve.wait_ge(dc_done, H * t + h + 1)
                        dve.scalar_tensor_tensor(out=ct[:, h, :], in0=ct[:, h, :], scalar=decay[:, h, 0:1],
                                                 in1=psum[:, h, 0:VA1], op0=ALU.mult,
                                                 op1=ALU.add).then_inc(ct_ready, 1)
                    continue
                dve.wait_ge(qg_ready, TT)
                dve.wait_ge(ksb_ready, 1)
                for h in range(H):
                    if h:
                        dve.wait_ge(num_done, H * t + h)
                    dve.tensor_copy(qgm[:].rearrange("p (b s) -> p b s", b=NB)[:, :, 0:DSEQ],
                                    qg[:, h, :].rearrange("p (b s) -> p b s", b=NB)).then_inc(qgm_ready, 1)
                    dve.tensor_copy(cts[:, :, DV], n0[:, :, h]).then_inc(cts_ready, 1)
                    if h:
                        dve.wait_ge(un_done, 4 * h)
                    dve.tensor_tensor(kwall[:], ksb[:, h, :].unsqueeze(1).to_broadcast([P, NB, P]),
                                      dt[:, h, DSEQ - 1::DSEQ].unsqueeze(2).to_broadcast([P, NB, P]),
                                      ALU.mult).then_inc(kwall_ready, 1)
                    for v2 in range(2):
                        for q in range(2):
                            dve.wait_ge(un_done, 4 * h + 2 * v2 + q + 1)
                            for b in range(4 * q, 4 * q + 4):
                                c0 = c0n[h % 2][:, v2, b, :]
                                m = dve.scalar_tensor_tensor(out=c0, in0=c0, scalar=decay[:, h, b:b + 1],
                                                             in1=psum[:, 2 * v2 + q, P * (b % 4):P * (b % 4 + 1)],
                                                             op0=ALU.mult, op1=ALU.add)
                            m.then_inc(c_new, 1)
                    after(dve.tensor_tensor(n_new[:, :, h], n0[:, :, h], decay[:, h, :], ALU.mult))
                    dve.wait_ge(nn_done, h + 1)
                    dve.tensor_tensor(n_new[:, :, h], n_new[:, :, h], psum[:, 7, NB * h:NB * (h + 1)],
                                      ALU.add).then_inc(ct_ready, 1)
            def z_lo_part(c):
                dve.wait_ge(z_hi_ready, c + 1)
                dve.tensor_tensor(z_lo[:, c, :], z[:, c, :], z_hi[:, c, :].bitcast(F32),
                                  ALU.subtract).then_inc(z_lo_ready, 1)

            for k in range(BLOCKS):
                if k >= 2:
                    dve.wait_ge(y_done, k - 1)
                dve.wait_ge(cpw_ready, BLOCKS + k)
                output_powers(dve, after, k).then_inc(cpw_ready, 1)
                if k in (3, 4):
                    split(U_GLU + k - 3, k - 3)
                if k >= 5:
                    z_lo_part(k - 5)
            for c in range(BLOCKS - 5, BLOCKS):
                z_lo_part(c)

            def mlstm_tile(t):
                f = stat[:, 7, 4 * t:4 * t + 4]
                mean = stat[:, 5, 4 * t:4 * t + 4]
                den = oa[:, :, DV]
                dve.wait_ge(oa_loaded, 32 * (t + 1))
                after(dve.scalar_tensor_tensor(out=f, in0=den, scalar=-1.0, in1=den, op0=ALU.mult, op1=ALU.max))
                after(dve.tensor_tensor(f, f, exp_neg_m[:, t, :], ALU.max))
                after(dve.reciprocal(f, f))
                dve.wait_ge(oa_sums, t + 1)
                after(dve.tensor_tensor(mean, stat[:, 4, 4 * t:4 * t + 4], f, ALU.mult))
                after(dve.tensor_tensor(mean, mean, f, ALU.mult))
                dve.tensor_scalar(mean, mean, 1.0 / DV, EPS, ALU.mult, ALU.add).then_inc(oa_mean, 1)
                dve.wait_ge(oa_root, t + 1)
                after(dve.reciprocal(stat[:, 6, 4 * t:4 * t + 4], stat[:, 6, 4 * t:4 * t + 4]))
                after(dve.tensor_tensor(f, f, stat[:, 6, 4 * t:4 * t + 4], ALU.mult))
                for h in range(H):
                    m = dve.scalar_tensor_tensor(out=og_in[:, h, :], in0=oa[:, h, 0:DV], scalar=f[:, h:h + 1],
                                                 in1=og_in[:, h, :], op0=ALU.mult, op1=ALU.mult)
                m.then_inc(oa_ready, 1)
                for q in range(2):
                    n = 2 * t + q
                    dve.wait_ge(oat_hi, n + 1)
                    for k in range(4):
                        kt = 4 * q + k
                        m = dve.scalar_tensor_tensor(
                            out=ot_lo[:, kt, P * t:P * (t + 1)], in0=psum[:, 4 + n % 4, P * k:P * (k + 1)],
                            scalar=chan[:, kt, R_GMH:R_GMH + 1],
                            in1=ot_hi[:, kt, P * t:P * (t + 1)].bitcast(F32), op0=ALU.mult, op1=ALU.subtract)
                    m.then_inc(oat_lo, 1)

            for j in range(4):
                for c in range(2):
                    n = 2 * j + c
                    dve.wait_ge(gate_ready, n + 1)
                    if n:
                        dve.wait_ge(ob_lo, n)
                    for h in range(2):
                        fr = slice(4 * h, 4 * h + 4)
                        m = dve.tensor_tensor(
                            ob[:].rearrange("p (c r) -> p r c", r=FR)[:, fr, :],
                            z[:, n, :].rearrange("p (r c) -> p r c", r=FR)[:, fr, :],
                            psum[:, 2 * c + h, 0:HALF].rearrange("p (r c) -> p r c", r=4), ALU.mult)
                        m.then_inc(ob_ready if h else ob_first, 1)
                    dve.wait_ge(ob_first, n + 1)
                    dve.wait_ge(ob_hi, n + 1)
                    dve.tensor_tensor(ot_lo[:, 8 + n, :], ob[:], ot_hi[:, 8 + n, :].bitcast(F32),
                                      ALU.subtract).then_inc(ob_lo, 1)
                split(U_GLU + 2 + j, j % 2)
                mlstm_tile(j)
            mlstm_tile(TT - 1)
            with dve.Fori(0, 3) as i:
                for j in range(4):
                    split(4 * i + (U_OUT + 2 + j), j % 2)
            for j in range(2):
                split(U_FFN - 2 + j, j)
            dve.wait_ge(gp_loaded, 32)
            n = TT
            for stage, t in PIPE2:
                if stage == "mix":
                    f = rms_factor(n)
                    dve.scalar_tensor_tensor(out=mix[:, t, :], in0=mix[:, t, :], scalar=f, in1=g_post[:],
                                             op0=ALU.mult, op1=ALU.mult).then_inc(mix_normed, 1)
                elif stage == "hidden":
                    f = rms_factor(n)
                    dve.scalar_tensor_tensor(out=mix[:, t, :], in0=xres[t % 4][:], scalar=f, in1=g_ffn[:],
                                             op0=ALU.mult, op1=ALU.mult).then_inc(normed, 1)
                else:
                    tile_lo(ht_hi, ht_lo, t, 4 * TT + 4 * t)
                    if t >= 3:
                        dve.wait_ge(xr_stored[t - 1], 16)
                        split(U_FFN + t - 3, t - 3)
                n += stage != "split"
            def ffn_block(i, last=False):
                for j in range(12):
                    p = j // 2
                    bank = 4 * (p % 2)
                    if j < 8 and j % 2:
                        dve.wait_ge(pe_done, 60 * i + (5 * (U_FFN + j) + 5))
                        for h in range(2):
                            dve.wait_ge(sg_ready, 8 * i + (2 * p + h + 1))
                            if p:
                                dve.wait_ge(h_lo_ready, 8 * i + 2 * p)
                            dve.tensor_tensor(hid[:, h, :], sg[:, h, :], psum[:, bank + 2 + h, 0:HALF],
                                              ALU.mult).then_inc(hid_ready, 1)
                        for h in range(2):
                            dve.wait_ge(h_hi_ready, 8 * i + (2 * p + h + 1))
                            cols = (slice(None), p, slice(HALF * h, HALF * (h + 1)))
                            dve.tensor_tensor(h_lo[cols], hid[:, h, :], h_hi[cols].bitcast(F32),
                                              ALU.subtract).then_inc(h_lo_ready, 1)
                    if j >= 8:
                        for t in range(TT):
                            q = TT * (j - 8) + t
                            if last and j == 11 and t >= 2:
                                finish(t - 2)
                            dve.wait_ge(pe_done, 60 * i + (5 * (U_FFN + j) + t + 1))
                            if q == 0:
                                dve.wait_ge(tok_evac, 20 * i + 40)
                            bank = q % 8 if q < 16 else q - 12
                            cols = slice(512 * (j - 8), 512 * (j - 7))
                            dve.tensor_tensor(acc[:, t, cols], acc[:, t, cols], psum[:, bank, :],
                                              ALU.add).then_inc(tok_evac, 1)
                    if not (last and j >= 10):
                        split(12 * i + (U_FFN + 2 + j), j % 2)

            def finish(t):
                f = rms_factor(3 * TT + t)
                if t == 0:
                    dve.wait_ge(gp_loaded, 48)
                m = dve.scalar_tensor_tensor(out=acc[:, t, :], in0=acc[:, t, :], scalar=f, in1=g_last[:],
                                             op0=ALU.mult, op1=ALU.mult)
                if t in ON_POOL:
                    m.then_inc(ff_normed, 1)
                    return
                after(m)
                dve.wait_ge(last_loaded[t], 16)
                dve.tensor_tensor(xlast[t][:], xlast[t][:], acc[:, t, :], ALU.add).then_inc(y_ready[t], 1)

            dve.wait_ge(acc_zero, 1)
            with dve.Fori(0, NFB - 1) as i:
                ffn_block(i)
            ffn_block(NFB - 1, last=True)
            for t in range(TT - 2, TT):
                finish(t)

        @block.gpsimd
        def _(pool):
            chained = [0]

            def after(ins):
                chained[0] += 1
                ins.then_inc(pool_chain, 1)
                pool.wait_ge(pool_chain, chained[0])

            pool.memset(ident[:], 0.0)
            pool.memset(mask_prompt[:], 0.0)
            after(pool.memset(mask_sample[:], 0.0))
            pool.affine_select(out=ident[:], in_=ident[:], compare_op=ALU.not_equal, fill=1.0, base=0,
                               pattern=[[-1, P]], channel_multiplier=1).then_inc(const_ready, 1)
            pool.affine_select(out=mask_prompt[:], in_=mask_prompt[:], compare_op=ALU.is_ge, fill=MASKED,
                               base=0, pattern=[[1, P]], channel_multiplier=-1).then_inc(const_ready, 1)
            after(pool.affine_select(out=mask_sample[:], in_=mask_sample[:], compare_op=ALU.is_ge, fill=MASKED,
                                     base=0, pattern=[[1, P]], channel_multiplier=-1))
            per_stream = mask_sample[:].rearrange("p (b s) -> p b s", b=NB)
            pool.affine_select(out=per_stream, in_=per_stream, compare_op=ALU.is_ge, fill=MASKED, base=0,
                               pattern=[[-DSEQ, NB], [0, DSEQ]], channel_multiplier=1).then_inc(const_ready, 1)

            def cmul(dst, x, y, tmp):
                pool.tensor_tensor(dst[0], x[0], y[0], ALU.mult)
                after(pool.tensor_tensor(tmp, x[1], y[1], ALU.mult))
                after(pool.tensor_tensor(dst[0], dst[0], tmp, ALU.subtract))
                pool.tensor_tensor(dst[1], x[0], y[1], ALU.mult)
                after(pool.tensor_tensor(tmp, x[1], y[0], ALU.mult))
                after(pool.tensor_tensor(dst[1], dst[1], tmp, ALU.add))

            pool.wait_ge(small_ev, 3)
            pool.memset(lbp[:, 0, :, 0:1].rearrange("p a o -> p (a o)"), 1.0)
            after(pool.memset(lbp[:, 1, :, 0:1].rearrange("p a o -> p (a o)"), 0.0))
            lb = [lbp[:, r, :, 1] for r in range(2)]
            for k in range(2, FR + 1):
                cmul([lbp[:, r, :, k] for r in range(2)], [lbp[:, r, :, k - 1] for r in range(2)], lb,
                     stmp[:, 1, :, 0])
            cmul([bbar[:, r, :, :] for r in range(2)],
                 [fct[:, r, :].unsqueeze(2).to_broadcast([P, PAIRS, GI]) for r in range(2)],
                 [b_in[:, r, :, :] for r in range(2)], stmp[:, 0, :, :])
            pool.memset(stmp[:, 1, 0, 0:1], 0.0).then_inc(s5_consts, 1)
            pool.wait_ge(pe_done, 5 * U_GLU)
            after(pool.memset(sel[:], 0.0))
            pool.affine_select(out=sel[:], in_=sel[:], compare_op=ALU.not_equal, fill=1.0, base=0,
                               pattern=[[-1, 4], [0, P]], channel_multiplier=1).then_inc(sel_ready, 1)
            for k in range(BLOCKS):
                if k >= 2:
                    pool.wait_ge(k_done, k - 1)
                if k:
                    pool.wait_ge(cpw_ready, k)
                output_powers(pool, after, k).then_inc(cpw_ready, 1)
            pool.wait_ge(v_evac, BLOCKS)
            pool.wait_ge(s5_state_in, 2)

            def advance(dst, state, tmp, done):
                shape = list(state.shape)
                lam = [lam8[:, r, :, :] if len(shape) == 3 else
                       lam8[:, r, :, :].unsqueeze(3).to_broadcast(shape) for r in range(2)]
                pool.tensor_tensor(tmp[0], lam[0], state, ALU.mult).then_inc(scan_step, 1)
                pool.tensor_tensor(tmp[1], lam[1], state[:, ::-1], ALU.mult).then_inc(scan_step, 1)
                pool.wait_ge(scan_step, done + 1)
                pool.tensor_tensor(dst, dst, tmp[0], ALU.add).then_inc(scan_step, 1)
                pool.wait_ge(scan_step, done + 3)
                pool.tensor_tensor(dst, dst, tmp[1], ALU.add).then_inc(scan_step, 1)
                pool.wait_ge(scan_step, done + 4)

            one = [scan_tmp[:, r, :, :] for r in range(2)]
            for c in range(PSTEPS):
                advance(sst[:, :, :, c + 1] if c < PSTEPS - 1 else fin[:, :, 0, :], sst[:, :, :, c], one, 4 * c)
            many = [t[:] for t in stream_tmp]
            advance(sst[:, :, :, PSTEPS + 1::2], sst[:, :, :, PSTEPS::2], many, 4 * PSTEPS)
            advance(fin[:, :, 1:, :].rearrange("p r b a -> p r a b"), sst[:, :, :, PSTEPS + 1::2], many,
                    4 * PSTEPS + 4)
            pool.memset(scan_tmp[:, 0, 0, 0:1], 0.0).then_inc(scan_done, 1)
            for t in range(TT):
                pool.wait_ge(mix_normed, t + 1)
                pool.wait_ge(xr_loaded[t % 4], 16 * (t // 4 + 1))
                pool.tensor_tensor(xres[t % 4][:], xres[t % 4][:], mix[:, t, :], ALU.add).then_inc(xr_ready, 1)
            pool.wait_ge(tr_done, 8 * TT)
            pool.memset(acc[:].rearrange("p t d -> p (t d)"), 0.0).then_inc(acc_zero, 1)
            for n, t in enumerate(ON_POOL):
                pool.wait_ge(ff_normed, n + 1)
                pool.wait_ge(last_loaded[t], 16)
                pool.tensor_tensor(xlast[t][:], xlast[t][:], acc[:, t, :], ALU.add).then_inc(y_ready[t], 1)


_INS = ["x_prompt", "x_sample", "state_conv", "state_mlstm_c", "state_mlstm_n", "state_mlstm_m",
        "state_s5_re", "state_s5_im", "g_pre_mix", "w_in", "w_conv", "b_conv", "b_igate", "b_fgate",
        "g_mh", "s5_lam_re", "s5_lam_im", "s5_log_dt", "s5_b_re", "s5_b_im", "s5_c_re", "s5_c_im",
        "s5_d", "w_glu", "b_glu", "w_out", "g_post_mix", "g_pre_ffn", "w_gate", "w_up", "w_down",
        "g_post_ffn"]
_OUTS = {"y_prompt": (1, SEQ, D), "y_sample": (NB, DSEQ, D),
         "conv_p": (1, 1, HIST, QK), "c_p": (1, 1, H, DV, DQK), "n_p": (1, 1, H, DQK), "m_p": (1, 1, H),
         "s5re_p": (1, 1, G, NS), "s5im_p": (1, 1, G, NS),
         "conv_s": (1, NB, HIST, QK), "c_s": (1, NB, H, DV, DQK), "n_s": (1, NB, H, DQK), "m_s": (1, NB, H),
         "s5re_s": (1, NB, G, NS), "s5im_s": (1, NB, G, NS)}


def kernel(**inputs):
    import concourse.bacc as bacc
    from concourse.bass_utils import run_bass_kernel_spmd

    nc = bacc.Bacc("TRN2", target_bir_lowering=False, num_devices=1)
    arrays, ins, outs = {}, {}, {}
    for name in _INS:
        x = np.ascontiguousarray(inputs[name])
        arrays[f"in_{name}"] = x
        ins[name] = nc.dram_tensor(f"in_{name}", x.shape, mybir.dt.from_np(x.dtype), kind="ExternalInput").ap()
    for name, shape in _OUTS.items():
        outs[name] = nc.dram_tensor(f"out_{name}", shape, F32, kind="ExternalOutput").ap()
    build(nc, ins, outs)
    r = run_bass_kernel_spmd(nc, [arrays], core_ids=[0])
    return tuple(r.results[0][f"out_{name}"] for name in _OUTS)
```

```python
from contextlib import ExitStack

import numpy as np

import concourse.bass as bass
from concourse import mybir
from concourse.alu_op_type import AluOpType as ALU

F32 = mybir.dt.float32
F32R = mybir.dt.float32r
ACT = mybir.ActivationFunctionType
AX = mybir.AxisListType

P = 128
D = 2048
KT = D // P
SEQ, NB, DSEQ = 512, 8, 16
TT = (SEQ + NB * DSEQ) // P
T = TT * P
HALF = T // 2
SAMPLE = SEQ // P
H, DV, DQK = 4, 256, 128
VA1 = DV + 1
QK = 2 * H * DQK
DA = H * DV
DB = D - DA
CONV = 4
HIST = CONV - 1
G, GI, NS = 64, 16, 64
PAIRS = G // 2
FR = P // GI
STEPS = T // FR
PSTEPS = SEQ // FR
BP = 4
BLOCKS = PAIRS // BP
DFF = 5632
FB = 512
NFB = DFF // FB
EPS = 1e-6
UNIT = 2048
U_S5, U_QK, U_V, U_OG = 0, 8, 16, 24
U_GLU, U_OUT, U_FFN = 32, 36, 52
N_UNITS = U_FFN + 12 * NFB
COL_V, COL_OG, COL_GATE, COL_U = QK, QK + DA, QK + 2 * DA, QK + 2 * DA + 2 * H
MASKED = -1.0e30
ROUND = 12582912.0
TWO_PI = 2.0 * np.pi
PI2_A = 6.28125
PI2_B = float(np.float32(np.floor((TWO_PI - PI2_A) * 2.0**20) / 2.0**20))
PI2_C = float(np.float32(TWO_PI - PI2_A - PI2_B))
KB = 1024
GP = 12
GW = GP * (KT - 1) + P

R_CONV, R_BCONV, R_BGLU, R_GMH, R_S5D, R_HIST = 0, 4, 5, 6, 7, 8
NROWS = R_HIST + NB * HIST


def build(nc, a, o):
    base = nc.sbuf_base + (-nc.sbuf_base) % 32
    CONST, RING, R1, R2 = 0, 7 * KB, 55 * KB, 135 * KB

    def at(name, shape, offset, dtype=F32):
        return nc.alloc_sbuf_tensor_at(name, shape, dtype, offset=base + offset)

    place = [CONST]

    def const(name, shape, dtype=F32):
        t = at(name, shape, place[0], dtype)
        place[0] += -(-int(np.prod(shape[1:])) * 4 // 32) * 32
        assert place[0] <= 7 * KB, place[0]
        return t

    ident = const("ident", [P, P])
    mask_prompt = const("mask_prompt", [P, P])
    mask_sample = const("mask_sample", [P, P])
    chan = const("chan", [P, 8, NROWS])
    conv_tail = const("conv_tail", [P, 8, 27])
    diag16 = const("diag16", [P, GI])
    n0 = const("n0", [P, NB, H])
    n_new = const("n_new", [P, NB, H])
    exp_neg_m = const("exp_neg_m", [P, TT, H])
    stat = const("stat", [P, 8, 20])
    mix_sq = const("mix_sq", [P, 4, TT])
    bgate = const("bgate", [36, 1])
    m0s = const("m0s", [4, NB])
    decay = const("decay", [P, H, NB])
    vec = const("vec", [P, NROWS])

    raw = [at(f"raw{s}", [P, UNIT], RING + 8 * KB * s) for s in range(2)]
    w_hi = [at(f"w_hi{s}", [P, UNIT], RING + 16 * KB + 8 * KB * s, F32R) for s in range(2)]
    w_lo = [at(f"w_lo{s}", [P, UNIT], RING + 32 * KB + 8 * KB * s, F32R) for s in range(2)]

    xt_hi = at("xt_hi", [P, KT, T], R1, F32R)
    xt_lo = at("xt_lo", [P, KT, T], R1 + 40 * KB, F32R)
    qk = at("qk", [P, 8, T], R2)
    junk = at("junk", [P, D], R2)
    va = at("va", [P, TT, H, VA1], R2 + 20 * KB)
    xrow = [at(f"xrow{s}", [P, D], place) for s, place in
            enumerate((R2 + 41 * KB, R2 + 49 * KB, RING + 32 * KB, RING + 40 * KB, RING + 24 * KB))]
    gbc = at("gbc", [P, D], R2 + 57 * KB)
    cn = at("cn", [P, 2, 8, NS], R2 + 67 * KB + 512)
    rows_in = at("rows_in", [NROWS, QK], R2 + 20 * KB)
    dis = at("dis", [PAIRS, 16, P], R2 + 24 * KB)
    ldt = at("ldt", [PAIRS, 2, 2], R2 + 32 * KB)
    b_in = at("b_in", [P, 2, PAIRS, GI], R2 + 33 * KB)
    n_in = at("n_in", [NB * H, P], R2 + 37 * KB)
    fct = at("fct", [P, 2, PAIRS], R2 + 37 * KB + 512)
    gate_w = at("gate_w", [P, KT, 8], R2 + 38 * KB)
    gate_win = at("gate_win", [P, GW], R2 + 38 * KB + 512)
    gate_w_hi = at("gate_w_hi", [P, GW], R2 + 15 * KB, F32R)
    gate_w_lo = at("gate_w_lo", [P, GW], R2 + 17 * KB, F32R)
    gate_tmp = at("gate_tmp", [36, T], R2 + 12 * KB)
    stmp = at("stmp", [P, 2, PAIRS, GI], R2 + 8 * KB)
    u_out = [at(f"u_out{s}", [P, FR, STEPS], R2 + 41 * KB + 2560 * s) for s in range(2)]
    conv_in = [at(f"conv_in{s}", [P, HIST + SEQ + NB * (HIST + DSEQ)], R2 + 46 * KB + 2688 * s)
               for s in range(2)]
    og_out = [at(f"og_out{s}", [P, 512], R2 + 53 * KB + 2048 * s) for s in range(2)]
    cpw_out = at("cpw_out", [P, 2, 2, P], R2 + 51 * KB)
    cpw_tmp = at("cpw_tmp", [P, 2, P], R2 + 70 * KB)
    bbar = at("bbar", [P, 2, PAIRS, GI], R2 + 57 * KB)
    c0t = at("c0t", [P, 2, PAIRS, GI], R2 + 61 * KB)
    lbp = at("lbp", [P, 2, PAIRS, FR + 1], R2 + 65 * KB)
    conv_acc = at("conv_acc", [P, T], R2 + 67 * KB + 512)

    u_in = at("u_in", [P, G, STEPS], R1)
    sst = at("sst", [P, 2, PAIRS, STEPS], R1 + 20 * KB)
    fin = at("fin", [P, 2, 1 + NB, PAIRS], R1 + 40 * KB)
    Q = R1 + 42 * KB + 256
    bpw = [at(f"bpw{s}", [P, 2, BP, P], Q + 23 * KB * s) for s in range(2)]
    bwt = [at(f"bwt{s}", [P, 2, BP, P], Q + (4 + 23 * s) * KB) for s in range(2)]
    cpw = [at(f"cpw{s}", [P, 2, BP, P], Q + (8 + 4 * s) * KB) for s in range(2)]
    cpy = [at(f"cpy{s}", [P, 2 * BP, P], Q + (8 + 4 * s) * KB) for s in range(2)]
    sty = [at(f"sty{s}", [P, 2 * BP, STEPS], Q + 16 * (1 + s) * KB) for s in range(2)]
    kpad = [at(f"kpad{s}", [P, 15 * GI], Q + (16 + s) * KB) for s in range(2)]
    bdiag = [at(f"bdiag{s}", [P, 2, BP, 2 * GI], Q + (18 + 13 * s) * KB) for s in range(2)]
    toep = [at(f"toep{s}", [P, 8, P], Q + place * KB) for s, place in enumerate((19, 23, 0, 4))]
    tail_out = at("tail_out", [27, QK], Q + 19 * KB)
    y_out = [at(f"y_out{s}", [P, BP, 2, STEPS], Q + 27 * KB + 2560 * s) for s in range(2)]
    stream_tmp = [at(f"stream_tmp{s}", [P, 2, PAIRS, NB], Q + 27 * KB + 2560 * s) for s in range(2)]
    btmp = [at(f"btmp{s}", [P, BP, P], Q + (32 + 2 * s) * KB) for s in range(2)]
    scan_tmp = at("scan_tmp", [P, 2, 2, PAIRS], Q + 36 * KB + 256)
    lam8 = at("lam8", [P, 2, 2, PAIRS], Q + 36 * KB + 768)
    s5_io = at("s5_io", [P, 2, 2, P], RING + 46 * KB)
    s5p_out = at("s5p_out", [PAIRS, 2, P], R2 + 56 * KB)
    np_out = at("np_out", [H, P], RING + 45 * KB)
    ns_out = at("ns_out", [NB * H, P], RING + 45 * KB + 512)
    r_li, r_lf, r_x, r_y = (at(f"rows{s}", [4, T], R2 + 41 * KB + 2560 * s) for s in range(4))
    r_z = at("rows4", [4, T], R2 + 67 * KB + 512)
    r_g, r_b, r_a, r_m = r_li, r_lf, r_x, r_y
    qgm = at("qgm", [P, 1152], R2 + 67 * KB + 384)
    ct = at("ct", [P, H, VA1], RING)
    hraw = [at(f"hraw{s}", [P, H, VA1], RING + 4128 * (s + 1)) for s in range(2)]
    dt = at("dt", [P, H, P], RING + 12 * KB + 512)
    pt = at("pt", [P, H, P], RING + 14 * KB + 512)
    qg = at("qg", [P, H, P], RING + 16 * KB + 512)
    kw = at("kw", [P, H, P], RING + 18 * KB + 512)
    ksb = at("ksb", [P, H, P], RING + 20 * KB + 512)
    sel = at("sel", [4, 4, P], RING + 22 * KB + 512)
    kwall = at("kwall", [P, NB, P], RING + 24 * KB + 512)
    cts = at("cts", [P, NB, VA1], RING + 28 * KB + 512)
    c0n = [at("c0n0", [P, 2, NB, P], Q), at("c0n1", [P, 2, NB, P], RING + 37 * KB)]
    cp_out = at("cp_out", [P, 2 * H, P], RING + 4128 * 2)

    ot_hi = at("ot_hi", [P, KT, T], R1, F32R)
    ot_lo = at("ot_lo", [P, KT, T], R1 + 40 * KB, F32R)
    z_hi = at("z_hi", [P, 8, T], R2, F32R)
    z_lo = at("z_lo", [P, 8, T], R2 + 20 * KB, F32R)
    z = at("z", [P, 8, T], R2 + 40 * KB)
    og_in = [at(f"og_in{s}", [P, H, DV], R2 + (57 + 4 * s) * KB) for s in range(2)]
    hrow = [at(f"hrow{s}", [P, DA], R2 + (60 + 4 * s) * KB) for s in range(2)]
    ob = at("ob", [P, T], R2 + 68 * KB + 512)
    sq_out = at("sq_out", [P, DV], R2 + 65 * KB)
    mix = at("mix", [P, TT, D], R2)
    g_post = at("g_post", [P, D], R2 + 40 * KB)
    g_ffn = at("g_ffn", [P, D], R2 + 48 * KB)
    xres = [at(f"xres{s}", [P, D], place) for s, place in
            enumerate((R2 + 56 * KB, R2 + 64 * KB, RING + 32 * KB, RING + 40 * KB))]
    ht_hi = at("ht_hi", [P, KT, T], R1, F32R)
    ht_lo = at("ht_lo", [P, KT, T], R1 + 40 * KB, F32R)
    acc = at("acc", [P, TT, D], R2)
    h_hi = at("h_hi", [P, 4, T], R2 + 40 * KB, F32R)
    h_lo = at("h_lo", [P, 4, T], R2 + 50 * KB, F32R)
    sg = at("sg", [P, 2, HALF], R2 + 60 * KB)
    hid = at("hid", [P, 2, HALF], R2 + 62 * KB + 512)
    g_last = at("g_last", [P, D], R1 + 40 * KB)
    xlast = [at(f"xlast{t}", [P, D], R1 + 8 * t * KB) for t in range(TT)]

    def dram(name, shape):
        return nc.dram_tensor(name, shape, F32, kind="Internal").ap()

    u_dram = dram("u_dram", (DB, T))
    y_dram = dram("y_dram", (DB, T))
    gate_dram = dram("gate_dram", (2, H, T))
    og_dram = dram("og_dram", (T, DA))
    k_dram = dram("k_dram", (BLOCKS, P, 15 * GI))
    cpw_dram = dram("cpw_dram", (BLOCKS, P, 2, BP, P))
    ha_dram = dram("ha_dram", (T, DA))
    x_dram = dram("x_dram", (T, D))

    with ExitStack() as ctx:
        psum = ctx.enter_context(nc.psum_tensor("psum", [P, 8, 512], F32))

        def sem(name):
            return ctx.enter_context(nc.semaphore(name))

        raw_loaded = [sem(f"raw_loaded{s}") for s in range(2)]
        hi_ready, lo_ready = sem("hi_ready"), sem("lo_ready")
        pe_done = sem("pe_done")
        const_ready = sem("const_ready")
        rows_loaded = [sem(f"rows_loaded{s}") for s in range(5)]
        g_loaded, small_loaded = sem("g_loaded"), sem("small_loaded")
        ssq_ready, mean_ready, root_ready = sem("ssq_ready"), sem("mean_ready"), sem("root_ready")
        normed = sem("normed")
        tr_done, tr_hi, tr_lo = sem("tr_done"), sem("tr_hi"), sem("tr_lo")
        dve_chain, act_chain, pool_chain = sem("dve_chain"), sem("act_chain"), sem("pool_chain")
        dis_act, dis_dve = sem("dis_act"), sem("dis_dve")
        small_tr, small_ev = sem("small_tr"), sem("small_ev")
        gate_w_ready, gates_done, gates_evac, gates_stored, gates_loaded = (
            sem("gate_w_ready"), sem("gates_done"), sem("gates_evac"), sem("gates_stored"),
            sem("gates_loaded"))
        s5_consts = sem("s5_consts")
        bank_free = sem("bank_free")
        tok_evac = sem("tok_evac")
        u_evac, u_stored = sem("u_evac"), [sem(f"u_stored{s}") for s in range(2)]
        conv_filled = sem("conv_filled")
        conv_read = sem("conv_read")
        conv_step, conv_summed, silu_done = sem("conv_step"), sem("conv_summed"), sem("silu_done")
        og_stored = [sem(f"og_stored{s}") for s in range(2)]
        ones_ready = sem("ones_ready")
        u_loaded, s5_in = [sem(f"u_loaded{s}") for s in range(2)], sem("s5_in")
        row_act, row_dve = sem("row_act"), sem("row_dve")
        tail_done, tail_ev, tail_stored = sem("tail_done"), sem("tail_ev"), sem("tail_stored")
        s5_state_tr, s5_state_in = sem("s5_state_tr"), sem("s5_state_in")
        bpw_ready = [sem(f"bpw_ready{s}") for s in range(2)]
        bwt_done, bwt_ready = sem("bwt_done"), sem("bwt_ready")
        v_done, v_evac = sem("v_done"), sem("v_evac")
        cpw_ready, cpw_stored = sem("cpw_ready"), sem("cpw_stored")
        cpw_loaded = [sem(f"cpw_loaded{s}") for s in range(2)]
        bdiag_ready = sem("bdiag_ready")
        k_done, k_ready, k_stored = sem("k_done"), sem("k_ready"), [sem(f"k_stored{s}") for s in range(2)]
        cpy_loaded = [sem(f"cpy_loaded{s}") for s in range(2)]
        sty_ready = sem("sty_ready")
        scan_step, scan_done = sem("scan_step"), sem("scan_done")
        toep_loaded = [sem(f"toep_loaded{s}") for s in range(4)]
        y_done, y_evac = sem("y_done"), sem("y_evac")
        y_stored = [sem(f"y_stored{s}") for s in range(2)]
        sel_ready, em_done, em_ready = sem("sel_ready"), sem("em_done"), sem("em_ready")
        arg_done, s_done, gb_done, kt_done = (
            sem("arg_done"), sem("s_done"), sem("gb_done"), sem("kt_done"))
        dt_ready, pt_ready, qg_ready, kw_ready, ksb_ready = (
            sem("dt_ready"), sem("pt_ready"), sem("qg_ready"), sem("kw_ready"), sem("ksb_ready"))
        num_done, num_evac, dc_done, ct_ready = (
            sem("num_done"), sem("num_evac"), sem("dc_done"), sem("ct_ready"))
        c0_loaded = [sem(f"c0_loaded{s}") for s in range(2)]
        c0_stored = [sem(f"c0_stored{s}") for s in range(2)]
        ctr_done, cts_ready, un_done, c_new = (
            sem("ctr_done"), sem("cts_ready"), sem("un_done"), sem("c_new"))
        qgm_ready, kwall_ready, nn_done = sem("qgm_ready"), sem("kwall_ready"), sem("nn_done")
        fin_tr, fin_ev, out_stored = sem("fin_tr"), sem("fin_ev"), sem("out_stored")
        z_loaded, z_ready, z_hi_ready, z_lo_ready = (
            [sem(f"z_loaded{s}") for s in range(2)], sem("z_ready"), sem("z_hi_ready"), sem("z_lo_ready"))
        og_loaded, oa_sums, oa_mean, oa_root, oa_ready = (
            [sem(f"og_loaded{s}") for s in range(2)], sem("oa_sums"), sem("oa_mean"), sem("oa_root"), sem("oa_ready"))
        ha_stored, hrow_loaded = ([sem(f"ha_stored{s}") for s in range(2)],
                                  [sem(f"hrow_loaded{s}") for s in range(2)])
        oat_done, oat_hi, oat_lo = sem("oat_done"), sem("oat_hi"), sem("oat_lo")
        gate_ready, ob_first, ob_ready, ob_hi, ob_lo = (
            sem("gate_ready"), sem("ob_first"), sem("ob_ready"), sem("ob_hi"), sem("ob_lo"))
        gp_loaded = sem("gp_loaded")
        mix_copied = sem("mix_copied")
        mix_normed, xr_ready, xr_stored = (
            sem("mix_normed"), sem("xr_ready"), [sem(f"xr_stored{s}") for s in range(4)])
        acc_zero, sg_ready, hid_ready, h_hi_ready, h_lo_ready = (
            sem("acc_zero"), sem("sg_ready"), sem("hid_ready"), sem("h_hi_ready"), sem("h_lo_ready"))
        last_loaded, ff_normed = sem("last_loaded"), sem("ff_normed")
        y_by_pool, y_by_dve = sem("y_by_pool"), sem("y_by_dve")
        res_stored = sem("res_stored")
        def step_slices(tile):
            if tile < SAMPLE:
                return a["x_prompt"][0, P * tile:P * (tile + 1), :]
            return a["x_sample"].rearrange("b t d -> (b t) d")

        w_in, w_glu, w_out = a["w_in"][0], a["w_glu"][0], a["w_out"][0]
        w_gate, w_up, w_down = a["w_gate"][0], a["w_up"][0], a["w_down"][0]

        def cols_of(w, col, width=P):
            return w[:, bass.ds(col, width)].rearrange("(k p) n -> p k n", p=P)

        def rows_of(w, row, col):
            return w[bass.ds(row, 4 * P), bass.ds(col, 512)].rearrange("(k p) n -> p k n", p=P)

        def as_unit(t, k):
            return t[:].rearrange("p (k n) -> p k n", k=k)

        def streams(t):
            return t[:, HIST + SEQ:].rearrange("p (b s) -> p b s", b=NB)

        def powers(eng, after, dst, tmp, first, matrix, pairs, sign):
            n = pairs.stop - pairs.start
            shape = [P, n, FR, GI]
            lr, li = (lbp[:, r, pairs, first:first + FR].unsqueeze(3).to_broadcast(shape) for r in range(2))
            xr, xi = (matrix[:, r, pairs, :].unsqueeze(2).to_broadcast(shape) for r in range(2))
            re, im = (dst[:, r, :, :].rearrange("p q (k i) -> p q k i", k=FR) for r in range(2))
            t = tmp[:].rearrange("p q (k i) -> p q k i", k=FR)
            add, sub = (ALU.add, ALU.subtract) if sign > 0 else (ALU.subtract, ALU.add)
            eng.tensor_tensor(re, lr, xr, ALU.mult)
            after(eng.tensor_tensor(t, li, xi, ALU.mult))
            after(eng.tensor_tensor(re, re, t, add))
            eng.tensor_tensor(im, lr, xi, ALU.mult)
            after(eng.tensor_tensor(t, li, xr, ALU.mult))
            return eng.tensor_tensor(im, im, t, sub)

        def input_powers(eng, after, k):
            return powers(eng, after, bpw[k % 2], btmp[k % 2], 0, bbar, slice(BP * k, BP * (k + 1)), -1)

        def load_toep(eng, k):
            eng.wait_ge(k_stored[k % 2], 16 * (k // 2 + 1))
            for r in range(FR):
                eng.dma_start(toep[k % 4][GI * r:GI * (r + 1), :, :],
                             k_dram[k].rearrange("(g j) c -> j g c", j=GI)[:, :, GI * r:GI * r + P]
                             ).then_inc(toep_loaded[k % 4], 16)

        def load_cpy(eng, k, signal):
            for r in range(2):
                for g in range(2):
                    eng.dma_start(cpy[k % 2][64 * r:64 * r + 64, g::2, :],
                                 cpw_dram[k][64 * g:64 * g + 64, r]).then_inc(signal[k % 2], 16)

        PIPE = [(stage, k - lag) for k in range(TT + 2) for stage, lag in (("sums", 0), ("split", 1))
                if 0 <= k - lag < TT]
        PIPE2 = [("mix", 0), ("mix", 1), ("mix", 2), ("hidden", 0), ("mix", 3), ("hidden", 1), ("split", 0),
                 ("mix", 4), ("hidden", 2), ("split", 1), ("hidden", 3), ("split", 2), ("hidden", 4),
                 ("split", 3), ("split", 4)]
        NORMS = [step for step in PIPE2 if step[0] != "split"]

        s5_c = {0: a["s5_c_re"], 1: a["s5_c_im"]}
        s5_b = {0: a["s5_b_re"], 1: a["s5_b_im"]}
        s5_state = {0: a["state_s5_re"], 1: a["state_s5_im"]}
        ON_POOL, ON_DVE = (0, 2), (1, 3, 4)
        N_SMALL = 18
        block = ctx.enter_context(nc.Block())

        OUT_SMALL = 9

        def store_y(sp, t):
            dst = (o["y_prompt"][0, P * t:P * (t + 1), :] if t < SAMPLE else
                   o["y_sample"].rearrange("b t d -> (b t) d"))
            if t in ON_POOL:
                sp.wait_ge(y_by_pool, ON_POOL.index(t) + 1)
            else:
                sp.wait_ge(y_by_dve, ON_DVE.index(t) + 1)
            sp.dma_start(dst, xlast[t][:]).then_inc(res_stored, 16)

        @block.sync
        def _(sp):
            def load(n, s, src, k):
                sp.wait_ge(lo_ready, n - 1)
                sp.dma_start(as_unit(raw[s], k), src).then_inc(raw_loaded[s], 16)

            for t in (1, 3):
                sp.dma_start(xrow[t][:], step_slices(t)).then_inc(rows_loaded[t], 16)
            for s in range(2):
                sp.dma_start(as_unit(raw[s], KT), cols_of(w_in, COL_U + P * s)).then_inc(raw_loaded[s], 16)
            n_small = [0]

            def small(dst, src):
                n_small[0] += 1
                sp.dma_start(dst, src).then_inc(small_loaded, 16)

            small(rows_in[R_CONV:R_CONV + 4, :], a["w_conv"][0])
            for r, name in ((R_BCONV, "b_conv"), (R_BGLU, "b_glu"), (R_GMH, "g_mh"), (R_S5D, "s5_d")):
                small(rows_in[r:r + 1, :], a[name])
            small(rows_in[R_HIST:NROWS, :], a["state_conv"][0].rearrange("b j c -> (b j) c"))
            for r, name in ((4, "s5_lam_re"), (5, "s5_lam_im")):
                small(dis[:, r, :], a[name][0].rearrange("(a g) p -> a (g p)", g=2))
            small(ldt[:, 0, :], a["s5_log_dt"][0].rearrange("(a g) -> a g", g=2))
            for r in range(2):
                small(b_in[:, r, :, :], s5_b[r][0].rearrange("(a g) p i -> (g p) a i", g=2))
                small(cn[:, r, :, :], s5_c[r][0].rearrange("(k q) i p -> (q i) k p", q=8))
            small(bgate[0:4, :], a["b_igate"].rearrange("o h -> h o"))
            small(bgate[32:36, :], a["b_fgate"].rearrange("o h -> h o"))
            with nc.allow_non_contiguous_dma(reason="32 words"):
                small(m0s[:], a["state_mlstm_m"][0].rearrange("b h -> h b"))
            small(n_in[:], a["state_mlstm_n"][0].rearrange("b h d -> (b h) d"))
            small(gate_w[:], cols_of(w_in, COL_GATE, 8))
            assert n_small[0] == N_SMALL, n_small
            with sp.Fori(1, 4) as i:
                for j in range(2):
                    load(2 * i + j, j, cols_of(w_in, 2 * P * i + (COL_U + P * j)), KT)
            with sp.Fori(0, 4) as i:
                for j in range(2):
                    load(2 * i + (U_QK + j), j, cols_of(w_in, 2 * P * i + P * j), KT)
            sp.wait_ge(gates_stored, 32)
            for s in range(2):
                sp.wait_ge(u_stored[s], 16 * 5)
            for g in range(2):
                sp.dma_start((r_li, r_lf)[g][:], gate_dram[g]).then_inc(gates_loaded, 16)
            with sp.Fori(0, 4) as i:
                for j in range(4):
                    load(4 * i + (U_V + j), j % 2, rows_of(w_in, 4 * P * j, 512 * i + COL_V), 4)
            def load_cpw(k):
                sp.dma_start(cpw[k % 2][:], cpw_dram[k]).then_inc(cpw_loaded[k % 2], 16)

            sp.wait_ge(cpw_stored, 16 * 2 * BLOCKS)
            sp.wait_ge(pe_done, 5 * U_GLU)
            for r in range(2):
                sp.dma_start(s5_io[:, r, :, :],
                             s5_state[r][0].rearrange("b (a g) p -> (b a) (g p)", g=2)
                             .rearrange("(q x) p -> x q p", q=2)).then_inc(s5_in, 16)
            load_cpw(0)
            for h in range(2):
                for r in range(FR):
                    sp.dma_start(u_in[GI * (7 - r):GI * (8 - r), G // 2 * h:G // 2 * (h + 1), :],
                                 u_dram[DB // 2 * h:DB // 2 * (h + 1), STEPS * r:STEPS * (r + 1)]
                                 .rearrange("(g i) c -> i g c", i=GI)).then_inc(u_loaded[h], 16)
            load_cpw(1)
            for k in range(BLOCKS):
                if k + 2 < BLOCKS:
                    sp.wait_ge(k_done, k + 1)
                    load_cpw(k + 2)
                sp.wait_ge(k_ready, 2 * k + 2)
                sp.dma_start(k_dram[k], kpad[k % 2][:]).then_inc(k_stored[k % 2], 16)

            def head_state(x, h, v):
                return x[0, :, h].rearrange("b (v p) d -> v p b d", v=2)[v]

            def load_c0(h):
                for v in range(2):
                    sp.dma_start(c0n[h % 2][:, v, :, :], head_state(a["state_mlstm_c"], h, v)
                                 ).then_inc(c0_loaded[h % 2], 16)

            def load_og(t):
                sp.dma_start(og_in[t % 2][:].rearrange("p h v -> p (h v)"), og_dram[P * t:P * (t + 1), :]
                             ).then_inc(og_loaded[t % 2], 16)

            sp.wait_ge(v_done, BLOCKS)
            for s in range(2):
                sp.wait_ge(og_stored[s], 16 * TT)
            load_og(0)
            load_og(1)
            load_cpy(sp, 0, cpw_loaded)
            load_cpy(sp, 1, cpw_loaded)
            load_c0(0)
            load_c0(1)
            sp.wait_ge(tail_stored, 32)
            load_toep(sp, 0)
            load_toep(sp, 1)
            for t in range(2, TT):
                sp.wait_ge(ha_stored[t % 2], 16 * (t // 2))
                load_og(t)
            for h in range(H):
                sp.wait_ge(c_new, 4 * (h + 1))
                for v in range(2):
                    sp.dma_start(head_state(o["c_s"], h, v), c0n[h % 2][:, v, :, :]
                                 ).then_inc(c0_stored[h % 2], 16)
                if h + 2 < H:
                    sp.wait_ge(c0_stored[h % 2], 32)
                    load_c0(h + 2)
            sp.wait_ge(ct_ready, H * TT)
            for s in range(2):
                sp.wait_ge(c0_stored[s], 64)
            load_toep(sp, 2)
            load_toep(sp, 3)

            def load_hrow(t):
                sp.dma_start(hrow[t % 2][:], ha_dram[P * t:P * (t + 1), :]).then_inc(hrow_loaded[t % 2], 16)

            def load_z(k):
                sp.wait_ge(y_stored[k % 2], 16 * FR * (k // 2 + 1))
                if k >= 2:
                    sp.wait_ge(z_loaded[k % 2], 16 * (k // 2))
                sp.dma_start(z[:, k, :], y_dram[P * k:P * (k + 1), :]).then_inc(z_loaded[k % 2], 16)

            for k in range(BLOCKS):
                sp.wait_ge(y_evac, 2 * k + 2)
                for t in range(FR):
                    sp.dma_start(
                        y_dram[P * k:P * (k + 1), STEPS * t:STEPS * (t + 1)].rearrange("(g i) c -> i g c", i=GI),
                        y_out[k % 2][GI * t:GI * (t + 1), :, :, :].rearrange("i q g c -> i (q g) c")
                    ).then_inc(y_stored[k % 2], 16)
                if k:
                    load_z(k - 1)
                if k + 4 < BLOCKS:
                    sp.wait_ge(y_done, k + 1)
                    load_toep(sp, k + 4)
                if k == 0:
                    sp.wait_ge(out_stored, 16 * OUT_SMALL)
                    for s in range(2):
                        sp.wait_ge(ha_stored[s], 16 * (3 - s))
                if k in (0, 1):
                    load(U_GLU + k, k, cols_of(w_glu, 256 * k, 256), 8)
                if k == 2:
                    load_hrow(0)
                    load_hrow(1)
            load_z(BLOCKS - 1)
            for t in range(4):
                if t + 2 < TT and t < 2:
                    sp.wait_ge(oat_done, 2 * t + 2)
                    load_hrow(t + 2)
                if t == 1:
                    sp.wait_ge(oat_done, 6)
                    load_hrow(4)
                if t < 2:
                    load(U_GLU + 2 + t, t % 2, cols_of(w_glu, 256 * (t + 2), 256), 8)
                else:
                    load(U_OUT + t - 2, t % 2, rows_of(w_out, 4 * P * (t - 2), 0), 4)
            for j in range(2, 4):
                load(U_OUT + j, j % 2, rows_of(w_out, 4 * P * j, 0), 4)
            sp.wait_ge(ob_lo, 8)
            sp.wait_ge(oat_done, 2 * TT)
            for s in range(2):
                sp.dma_start((g_post, g_ffn)[s][:], a[("g_post_mix", "g_pre_ffn")[s]].broadcast_to((P, D))
                             ).then_inc(gp_loaded, 16)
            for t in range(2):
                sp.dma_start(xres[t][:], step_slices(t)).then_inc(rows_loaded[t], 16)
            with sp.Fori(1, 4) as i:
                for j in range(4):
                    load(4 * i + (U_OUT + j), j % 2, rows_of(w_out, 4 * P * j, 512 * i), 4)
            load(U_FFN, 0, cols_of(w_gate, 0), KT)
            load(U_FFN + 1, 1, cols_of(w_up, 0), KT)
            sp.wait_ge(pe_done, 5 * U_FFN)
            for t in range(2, 4):
                sp.dma_start(xres[t][:], step_slices(t)).then_inc(rows_loaded[t], 16)
            for t in range(TT):
                sp.wait_ge(xr_ready, t + 1)
                sp.dma_start(x_dram[P * t:P * (t + 1), :], xres[t % 4][:]).then_inc(xr_stored[t % 4], 16)
                if t == 0:
                    sp.wait_ge(normed, TT + 1)
                    sp.wait_ge(xr_stored[0], 16)
                    sp.dma_start(xres[0][:], step_slices(4)).then_inc(rows_loaded[0], 16)
            for j in range(2, 8):
                load(U_FFN + j, j % 2, cols_of((w_gate, w_up)[j % 2], P * (j // 2)), KT)
            for j in range(4):
                load(U_FFN + 8 + j, j % 2, rows_of(w_down, 0, 512 * j), 4)
            with sp.Fori(1, NFB) as i:
                for j in range(4):
                    load(12 * i + (U_FFN + 2 * j), 0, cols_of(w_gate, FB * i + P * j), KT)
                    load(12 * i + (U_FFN + 2 * j + 1), 1, cols_of(w_up, FB * i + P * j), KT)
                for j in range(4):
                    load(12 * i + (U_FFN + 8 + j), j % 2, rows_of(w_down, FB * i, 512 * j), 4)
            sp.wait_ge(pe_done, 5 * (N_UNITS - 4))
            sp.dma_start(g_last[:], a["g_post_ffn"].broadcast_to((P, D))).then_inc(gp_loaded, 16)
            for s in range(4):
                sp.wait_ge(xr_stored[s], 32 if s == 0 else 16)
            for t in range(TT):
                sp.dma_start(xlast[t][:], x_dram[P * t:P * (t + 1), :]).then_inc(last_loaded, 16)
            for t in range(TT):
                store_y(sp, t)
            sp.wait_ge(res_stored, 16 * TT)

        @block.tensor
        def _(pe):
            PARTS = ((0, 0), (0, 1), (1, 0))

            def transpose_rows(src, first):
                for q in range(4):
                    n = first + q
                    if n >= 4:
                        pe.wait_ge(tr_lo, n - 3)
                    for k in range(4):
                        m = pe.transpose(psum[:, q, P * k:P * (k + 1)],
                                         src[:, P * (4 * q + k):P * (4 * q + k + 1)], ident[:])
                    m.then_inc(tr_done, 1)

            def channel_unit(slot, bank, rows, kts=KT, part=0, rows_ready=None):
                w = (w_hi[slot], w_lo[slot])
                width = UNIT // kts
                for k in range(kts):
                    if rows_ready is not None:
                        pe.wait_ge(rows_ready, k + 1)
                    for wp in range(2):
                        lhs = w[wp][:, width * k + P * part:width * k + P * (part + 1)]
                        for rp in range(2 - wp):
                            for h in range(2):
                                m = pe.matmul(psum[:, bank + h, 0:HALF], lhs,
                                              rows[rp][:, k, HALF * h:HALF * (h + 1)],
                                              start=(k == 0 and wp == 0 and rp == 0),
                                              stop=(k == kts - 1 and wp == 1))
                return m

            def row_unit(slot, rows, k0, first, last, evacuated=None):
                w = (w_hi[slot], w_lo[slot])
                for t in range(TT):
                    if evacuated is not None:
                        pe.wait_ge(tok_evac, evacuated + t)
                    for k in range(4):
                        for wp, rp in PARTS:
                            m = pe.matmul(psum[:, t, :], rows[rp][:, k0 + k, P * t:P * (t + 1)],
                                          w[wp][:, 512 * k:512 * (k + 1)],
                                          start=(first and k == 0 and wp == 0 and rp == 0),
                                          stop=(last and k == 3 and wp == 1))
                    m.then_inc(pe_done, 1)

            xt = (xt_hi, xt_lo)
            pe.wait_ge(const_ready, 3)
            for t in range(TT):
                pe.wait_ge(normed, t + 1)
                transpose_rows(xrow[t], 4 * t)
            pe.wait_ge(small_loaded, 16 * N_SMALL)
            for c in range(8):
                pe.transpose(psum[:, 4, NROWS * c:NROWS * (c + 1)],
                             rows_in[:, P * c:P * (c + 1)], ident[0:NROWS, 0:NROWS])
            pe.transpose(psum[:, 4, 320:320 + NB * H], n_in[:], ident[0:NB * H, 0:NB * H]
                         ).then_inc(small_tr, 1)
            for r in range(2):
                for k in range(8):
                    for g in range(2):
                        m = pe.matmul(psum[64 * g:64 * g + 64, 5 + r, 64 * k:64 * (k + 1)], cn[:, r, k, :],
                                      ident[:].rearrange("p (a g i) -> p g a i", g=2, i=GI)[:, g],
                                      start=True, stop=True)
            m.then_inc(small_tr, 1)
            pe.wait_ge(tr_lo, 4 * TT)
            for j in range(2):
                pe.wait_ge(lo_ready, j + 1)
                channel_unit(j, 2 * j, xt).then_inc(pe_done, 5)
            with pe.Fori(1, 4) as i:
                for j in range(2):
                    pe.wait_ge(lo_ready, 2 * i + (j + 1))
                    pe.wait_ge(bank_free, 2 * i + (j - 1))
                    channel_unit(j, 2 * j, xt).then_inc(pe_done, 5)
            pe.wait_ge(gate_w_ready, 2)
            pe.wait_ge(small_ev, 2)
            for k in range(KT):
                for wp, rp in PARTS:
                    for h in range(2):
                        m = pe.matmul(psum[:, 4 + h, 0:HALF], (gate_w_hi, gate_w_lo)[wp][:, GP * k:GP * k + P],
                                      xt[rp][:, k, HALF * h:HALF * (h + 1)],
                                      start=(k == 0 and wp == 0 and rp == 0),
                                      stop=(k == KT - 1 and wp == 1))
            m.then_inc(gates_done, 1)
            pe.wait_ge(dis_dve, 2)
            for r in range(4):
                m = pe.transpose(psum[:, 6, PAIRS * r:PAIRS * (r + 1)], dis[:, r, :],
                                 ident[0:PAIRS, 0:PAIRS])
            m.then_inc(small_tr, 1)
            with pe.Fori(0, 4) as i:
                for j in range(2):
                    pe.wait_ge(lo_ready, 2 * i + (U_QK + j + 1))
                    pe.wait_ge(bank_free, 2 * i + (U_QK + j - 1))
                    channel_unit(j, 2 * j, xt).then_inc(pe_done, 5)
            pe.wait_ge(bank_free, 16)
            for j in range(4):
                pe.wait_ge(lo_ready, U_V + j + 1)
                row_unit(j % 2, xt, 4 * j, j == 0, j == 3)
            with pe.Fori(1, 4) as i:
                for j in range(4):
                    pe.wait_ge(lo_ready, 4 * i + (U_V + j + 1))
                    row_unit(j % 2, xt, 4 * j, j == 0, j == 3, 5 * i - 4 if j == 0 else None)
            pe.wait_ge(small_ev, 3)
            for c in range(8):
                m = pe.transpose(psum[0:27, 6 + c // 4, P * (c % 4):P * (c % 4 + 1)],
                                 conv_tail[:, c, :], ident[:])
            m.then_inc(tail_done, 1)
            pe.wait_ge(s5_in, 32)
            for r in range(2):
                for q in range(2):
                    m = pe.transpose(psum[:, 5, P * (2 * r + q):P * (2 * r + q + 1)], s5_io[:, r, q, :],
                                     ident[:])
            m.then_inc(s5_state_tr, 1)
            pe.wait_ge(tail_ev, 1)
            pe.wait_ge(tok_evac, 20)
            pe.wait_ge(s5_state_in, 2)
            def transpose_input(k):
                pe.wait_ge(bpw_ready[k % 2], k // 2 + 1)
                if k:
                    pe.wait_ge(bwt_ready, k)
                for r in range(2):
                    for q in range(BP):
                        m = pe.transpose(psum[:, 6 + r, P * q:P * (q + 1)], bpw[k % 2][:, r, q, :], ident[:])
                m.then_inc(bwt_done, 1)

            transpose_input(0)
            for k in range(BLOCKS):
                pe.wait_ge(cpw_loaded[k % 2], 16 * (k // 2 + 1))
                pe.wait_ge(bdiag_ready, 2 * k + 2)
                if k:
                    pe.wait_ge(k_ready, 2 * k)
                for q in range(BP):
                    for cols, right in ((slice(0, GI), lambda r: c0t[:, r, BP * k + q, :]),
                                        (slice(GI, P), lambda r: cpw[k % 2][:, r, q, 0:P - GI])):
                        for r in range(2):
                            m = pe.matmul(psum[32 * q:32 * q + 32, 3, cols], bdiag[k % 2][:, r, q, :],
                                          right(r), start=(r == 0), stop=(r == 1))
                m.then_inc(k_done, 1)
                if k + 1 < BLOCKS:
                    transpose_input(k + 1)
                pe.wait_ge(bwt_ready, k + 1)
                if k % (BLOCKS // 2) == 0:
                    pe.wait_ge(u_loaded[k // (BLOCKS // 2)], 16 * FR)
                if k:
                    pe.wait_ge(v_evac, k)
                for r in range(2):
                    for q in range(BP):
                        for g in range(2):
                            m = pe.matmul(psum[64 * g:64 * g + 64, 4 + r, STEPS * q:STEPS * (q + 1)],
                                          bwt[k % 2][:, r, q, 64 * g:64 * g + 64],
                                          u_in[:, 2 * (BP * k + q) + g, :], start=True, stop=True)
                m.then_inc(v_done, 1)
            pe.wait_ge(v_evac, BLOCKS)
            pe.wait_ge(k_ready, 2 * BLOCKS)
            pe.wait_ge(ones_ready, 1)
            pe.wait_ge(sel_ready, 1)
            pe.wait_ge(row_dve, 3)
            for t in range(TT):
                m = pe.matmul(psum[:, 7, 4 * t:4 * t + 4], r_m[:, P * t:P * (t + 1)], ident[0:4, 0:4],
                              start=True, stop=True)
            m.then_inc(em_done, 1)
            pe.wait_ge(row_act, 3)
            pe.wait_ge(silu_done, 9)
            for t in range(TT):
                rows = slice(P * t, P * (t + 1))
                mask = mask_prompt if t < SAMPLE else mask_sample
                if t:
                    pe.wait_ge(ct_ready, H * t)
                pe.matmul(psum[:, 0, :], ident[:], mask[:].unsqueeze(1).to_broadcast([P, H, P]),
                          start=True, stop=False)
                pe.matmul(psum[:, 0, :], r_b[:, rows], sel[:].rearrange("k h n -> k (h n)"),
                          start=False, stop=False)
                for h in range(H):
                    m = pe.matmul(psum[:, 0, P * h:P * (h + 1)], sel[:, h, :], r_a[:, rows],
                                  start=False, stop=(h == H - 1))
                m.then_inc(arg_done, 1)
                for h in range(H):
                    m = pe.matmul(psum[:, 1, P * h:P * (h + 1)], qk[:, H + h, rows], qk[:, h, rows],
                                  start=True, stop=True)
                m.then_inc(s_done, 1)
                for h in range(H):
                    m = pe.matmul(psum[:, 2, P * h:P * (h + 1)], sel[:, h, :], r_g[:, rows],
                                  start=True, stop=True)
                m.then_inc(gb_done, 1)
                for h in range(H):
                    m = pe.transpose(psum[:, 3, P * h:P * (h + 1)], qk[:, H + h, rows], ident[:])
                m.then_inc(kt_done, 1)
                pe.wait_ge(pt_ready, t + 1)
                pe.wait_ge(qg_ready, t + 1)
                if t < SAMPLE:
                    pe.wait_ge(kw_ready, t + 1)
                    pe.wait_ge(ct_ready, max(H * t, 0))
                    for h in range(H):
                        n = H * t + h
                        if n >= 2:
                            pe.wait_ge(num_evac, n - 1)
                        pe.matmul(psum[:, 4 + h % 2, 0:VA1], pt[:, h, :], va[:, t, h, :],
                                  start=True, stop=False)
                        pe.matmul(psum[:, 4 + h % 2, 0:VA1], qg[:, h, :], ct[:, h, :],
                                  start=False, stop=True).then_inc(num_done, 1)
                        pe.matmul(psum[:, h, 0:VA1], kw[:, h, :], va[:, t, h, :],
                                  start=True, stop=True).then_inc(dc_done, 1)
                    continue
                pe.wait_ge(ksb_ready, 1)
                for h in range(H):
                    for v in range(2):
                        m = pe.transpose(psum[:, h // 2, P * (2 * (h % 2) + v):P * (2 * (h % 2) + v + 1)],
                                         ct[:, h, P * v:P * (v + 1)], ident[:])
                m.then_inc(fin_tr, 1)
                pe.transpose(psum[0:4, 6, 0:P], ct[:, :, DV], ident[:]).then_inc(fin_tr, 1)
                pe.wait_ge(em_ready, 1)
                for h in range(H):
                    c0 = c0n[h % 2]
                    pe.wait_ge(c0_loaded[h % 2], 32 * (h // 2 + 1))
                    if h == 0:
                        pe.wait_ge(fin_ev, 1)
                    else:
                        pe.wait_ge(c_new, 4 * h)
                    for b in range(NB):
                        for v in range(2):
                            m = pe.transpose(
                                psum[:, b // 2, P * (2 * (b % 2) + v):P * (2 * (b % 2) + v + 1)],
                                c0[:, v, b, :], ident[:])
                        if b % 2:
                            m.then_inc(ctr_done, 1)
                    pe.wait_ge(num_evac, H * t + h - 1)
                    pe.matmul(psum[:, 4 + h % 2, 0:VA1], pt[:, h, :], va[:, t, h, :],
                              start=True, stop=False)
                    pe.wait_ge(qgm_ready, h + 1)
                    pe.wait_ge(cts_ready, 5 * (h + 1))
                    for b in range(NB):
                        m = pe.matmul(psum[:, 4 + h % 2, 0:VA1], qgm[:, P * b:P * (b + 1)],
                                      cts[:, b, :], start=False, stop=(b == NB - 1))
                    m.then_inc(num_done, 1)
                    pe.wait_ge(kwall_ready, h + 1)
                    for v in range(2):
                        for q in range(2):
                            pe.matmul(psum[:, 2 * v + q, :], va[:, t, h, P * v:P * (v + 1)],
                                      kwall[:, 4 * q:4 * q + 4, :], start=True,
                                      stop=True).then_inc(un_done, 1)
                    if h:
                        pe.wait_ge(ct_ready, H * t + h)
                    pe.matmul(psum[:, 7, NB * h:NB * (h + 1)], ksb[:, h, :],
                              dt[:, h, DSEQ - 1::DSEQ], start=True, stop=True).then_inc(nn_done, 1)
            pe.wait_ge(ct_ready, H * TT)
            pe.wait_ge(fin_ev, 2)
            pe.transpose(psum[0:NB * H, 6, P:2 * P], n_new[:].rearrange("p b h -> p (b h)"),
                         ident[:]).then_inc(fin_tr, 1)
            pe.wait_ge(scan_done, 1)
            pe.wait_ge(c_new, 4 * H)
            for r in range(2):
                m = pe.transpose(psum[0:PAIRS, 0, P * r:P * (r + 1)], fin[:, r, 0, :], ident[:])
            m.then_inc(fin_tr, 1)
            for r in range(2):
                for q in range(2):
                    m = pe.transpose(
                        psum[:, 1, P * (2 * r + q):P * (2 * r + q + 1)],
                        fin[:, r, 1 + 4 * q:5 + 4 * q, :].rearrange("p b a -> p (b a)"), ident[:])
            m.then_inc(fin_tr, 1)
            pe.wait_ge(num_evac, H * TT)
            for k in range(BLOCKS):
                if k < 2:
                    pe.wait_ge(cpw_loaded[k], 16 * BLOCKS // 2 + 64)
                else:
                    pe.wait_ge(cpy_loaded[k % 2], 64 * (k // 2))
                pe.wait_ge(sty_ready, k + 1)
                pe.wait_ge(toep_loaded[k % 4], 16 * FR * (k // 4 + 1))
                banks = (2, 3) if k % 2 else (4, 5)
                if k >= 2:
                    pe.wait_ge(y_evac, 2 * (k - 1))
                for q in range(BP):
                    for g in range(2):
                        out = psum[:, banks[g], STEPS * q:STEPS * (q + 1)]
                        pe.matmul(out, toep[k % 4][:, 2 * q + g, :], u_in[:, 2 * (BP * k + q) + g, :],
                                  start=True, stop=False)
                        m = pe.matmul(out, cpy[k % 2][:, 2 * q + g, :], sty[k % 2][:, 2 * q + g, :],
                                      start=False, stop=True)
                m.then_inc(y_done, 1)
            def mlstm_to_channels(t):
                pe.wait_ge(hrow_loaded[t % 2], 16 * (t // 2 + 1))
                for q in range(2):
                    n = 2 * t + q
                    if n >= 4:
                        pe.wait_ge(oat_lo, n - 3)
                    for k in range(4):
                        m = pe.transpose(psum[:, 4 + n % 4, P * k:P * (k + 1)],
                                         hrow[t % 2][:, P * (4 * q + k):P * (4 * q + k + 1)], ident[:])
                    m.then_inc(oat_done, 1)

            pe.wait_ge(y_evac, 2 * BLOCKS)
            pe.wait_ge(fin_ev, 5)
            mlstm_to_channels(0)
            mlstm_to_channels(1)
            for j in range(4):
                pe.wait_ge(lo_ready, U_GLU + j + 1)
                for c in range(2):
                    if 2 * j + c >= 2:
                        pe.wait_ge(ob_ready, 2 * j + c - 1)
                    channel_unit(j % 2, 2 * c, (z_hi, z_lo), 8, c,
                                 z_lo_ready if j + c == 0 else None).then_inc(pe_done, 2 + c)
                if j + 2 < TT:
                    mlstm_to_channels(j + 2)
            pe.wait_ge(oat_lo, 2 * TT)
            pe.wait_ge(tok_evac, 20)
            pe.wait_ge(ob_ready, 8)
            for j in range(4):
                if j == 2:
                    pe.wait_ge(ob_lo, 8)
                pe.wait_ge(lo_ready, U_OUT + j + 1)
                row_unit(j % 2, (ot_hi, ot_lo), 4 * j, j == 0, j == 3)
            with pe.Fori(1, 4) as i:
                for j in range(4):
                    pe.wait_ge(lo_ready, 4 * i + (U_OUT + j + 1))
                    row_unit(j % 2, (ot_hi, ot_lo), 4 * j, j == 0, j == 3, 5 * i + 16 if j == 0 else None)
            pe.wait_ge(tok_evac, 40)
            for t in range(TT):
                pe.wait_ge(normed, TT + t + 1)
                transpose_rows(mix[:, t, :], 4 * TT + 4 * t)
            pe.wait_ge(tr_lo, 8 * TT)
            BANKS = [q % 8 if q < 16 else q - 12 for q in range(20)]
            with pe.Fori(0, NFB) as i:
                for p in range(4):
                    if p == 0:
                        pe.wait_ge(tok_evac, 20 * i + 32)
                    elif p == 1:
                        pe.wait_ge(tok_evac, 20 * i + 40)
                    else:
                        pe.wait_ge(hid_ready, 8 * i + 2 * (p - 1))
                    for j in range(2):
                        pe.wait_ge(lo_ready, 12 * i + (U_FFN + 2 * p + j + 1))
                        channel_unit(j, 4 * (p % 2) + 2 * j, (ht_hi, ht_lo)).then_inc(pe_done, 5)
                for j in range(4):
                    pe.wait_ge(lo_ready, 12 * i + (U_FFN + 8 + j + 1))
                    w = (w_hi[j % 2], w_lo[j % 2])
                    for t in range(TT):
                        q = TT * j + t
                        if q == 0:
                            pe.wait_ge(h_lo_ready, 8 * i + 6)
                        elif q == 4:
                            pe.wait_ge(hid_ready, 8 * i + 8)
                        elif q >= 8:
                            pe.wait_ge(tok_evac, 20 * i + (40 + (q - 8 if q < 16 else q - 4) + 1))
                        for k in range(4):
                            if j == 0 and k == 3 and t == 0:
                                pe.wait_ge(h_lo_ready, 8 * i + 7)
                            if j == 0 and k == 3 and t == 2:
                                pe.wait_ge(h_lo_ready, 8 * i + 8)
                            for wp, rp in PARTS:
                                m = pe.matmul(psum[:, BANKS[q], :],
                                              (h_hi, h_lo)[rp][:, k, P * t:P * (t + 1)],
                                              w[wp][:, 512 * k:512 * (k + 1)],
                                              start=(k == 0 and wp == 0 and rp == 0),
                                              stop=(k == 3 and wp == 1))
                        m.then_inc(pe_done, 1)

        @block.scalar
        def _(act):
            chained = [0]

            def after(ins):
                chained[0] += 1
                ins.then_inc(act_chain, 1)
                act.wait_ge(act_chain, chained[0])

            def split(half, s):
                act.wait_ge(raw_loaded[s], 16 * half + 16)
                act.wait_ge(pe_done, 10 * half + (5 * s - 5))
                act.activation(w_hi[s][:], raw[s][:], ACT.Copy).then_inc(hi_ready, 1)

            act.dma_start(xrow[0][:], step_slices(0)).then_inc(rows_loaded[0], 16)
            act.dma_start(gbc[:], a["g_pre_mix"].broadcast_to((P, D))).then_inc(g_loaded, 16)
            for t in (2, 4):
                act.dma_start(xrow[t][:], step_slices(t)).then_inc(rows_loaded[t], 16)
            def rms_sums(n, src, scratch, means=None):
                act.activation(scratch, src, ACT.Square, accum_out=stat[:, 0, n:n + 1]).then_inc(ssq_ready, 1)
                act.wait_ge(mean_ready, (n if means is None else means) + 1)
                act.activation(stat[:, 2, n:n + 1], stat[:, 1, n:n + 1], ACT.Sqrt).then_inc(root_ready, 1)

            def tile_hi(dst, t, first):
                for q in range(4):
                    act.wait_ge(tr_done, first + q + 1)
                    act.activation(dst[:, 4 * q:4 * q + 4, P * t:P * (t + 1)],
                                   psum[:, q, :].rearrange("p (k n) -> p k n", k=4),
                                   ACT.Copy).then_inc(tr_hi, 1)

            for stage, t in PIPE:
                if stage == "sums":
                    act.wait_ge(rows_loaded[t], 16)
                    rms_sums(t, xrow[t][:], junk[:])
                    continue
                tile_hi(xt_hi, t, 4 * t)
                if t in (2, 4):
                    act.wait_ge(raw_loaded[t // 2 - 1], 16)
                    act.activation(w_hi[t // 2 - 1][:], raw[t // 2 - 1][:], ACT.Copy).then_inc(hi_ready, 1)
            act.wait_ge(small_tr, 1)
            act.activation(chan[:].rearrange("p c r -> p (c r)"), psum[:, 4, 0:8 * NROWS], ACT.Copy)
            act.activation(n0[:].rearrange("p b h -> p (b h)"), psum[:, 4, 320:320 + NB * H],
                           ACT.Copy).then_inc(small_ev, 1)
            act.wait_ge(small_tr, 2)
            act.wait_ge(normed, TT)
            act.activation(c0t[:, 0, :, :].rearrange("p a i -> p (a i)"), psum[:, 5, :],
                           ACT.Copy).then_inc(u_stored[1], 16)
            act.activation(c0t[:, 1, :, :].rearrange("p a i -> p (a i)"), psum[:, 6, :],
                           ACT.Copy, scale=-1.0).then_inc(small_ev, 1)
            act.wait_ge(gate_w_ready, 1)
            act.activation(gate_w_hi[:], gate_win[:], ACT.Copy).then_inc(dis_act, 1)
            act.activation(ldt[:, 1, :], ldt[:, 0, :], ACT.Exp).then_inc(dis_act, 1)
            act.wait_ge(dis_dve, 1)
            act.activation(dis[:, 10, :], dis[:, 6, :], ACT.Exp).then_inc(silu_done, 1)
            act.activation(dis[:, 11, :], dis[:, 7, :], ACT.Sin).then_inc(u_stored[0], 16)
            act.activation(dis[:, 12, :], dis[:, 9, :], ACT.Sin).then_inc(dis_act, 1)

            with act.Fori(0, 4) as i:
                for j in range(2):
                    act.wait_ge(pe_done, 10 * i + (5 * j + 5))
                    act.wait_ge(u_stored[j], 16 * i + 16)
                    act.activation(u_out[j][:, :, 0:40],
                                   psum[:, 2 * j, 0:HALF].rearrange("p (c r) -> p r c", r=FR),
                                   ACT.Copy).then_inc(u_evac, 1)
                    act.activation(u_out[j][:, :, 40:80],
                                   psum[:, 2 * j + 1, 0:HALF].rearrange("p (c r) -> p r c", r=FR),
                                   ACT.Copy).then_inc(bank_free, 1)
                    split(i + 1, j)
                    act.wait_ge(u_evac, 2 * i + (j + 1))
                    act.wait_ge(bank_free, 2 * i + (j + 1))
                    act.dma_start(u_dram[bass.ds(2 * P * i + P * j, P), :],
                                  u_out[j][:].rearrange("p r c -> p (r c)")).then_inc(u_stored[j], 16)
            act.wait_ge(gates_done, 1)
            for g in range(2):
                part = slice(32 * g, 32 * g + 4)
                for h in range(2):
                    m = act.activation(gate_tmp[part, HALF * h:HALF * (h + 1)], psum[part, 4 + h, 0:HALF],
                                       ACT.Identity, bias=bgate[part, :])
            m.then_inc(gates_evac, 1)
            act.wait_ge(gates_evac, 1)
            for g in range(2):
                act.dma_start(gate_dram[g], gate_tmp[32 * g:32 * g + 4, :]).then_inc(gates_stored, 16)
            act.wait_ge(s5_consts, 1)
            act.wait_ge(gates_stored, 32)
            with act.Fori(0, 4) as i:
                for j in range(2):
                    act.wait_ge(pe_done, 10 * i + (5 * (U_QK + j) + 5))
                    act.wait_ge(conv_read, 2 * i + (j + 1))
                    buf = conv_in[j]
                    act.activation(buf[:, HIST:HIST + HALF], psum[:, 2 * j, 0:HALF],
                                   ACT.Copy).then_inc(conv_filled, 1)
                    act.activation(buf[:, HIST + HALF:HIST + SEQ], psum[:, 2 * j + 1, 0:SEQ - HALF],
                                   ACT.Copy).then_inc(conv_filled, 1)
                    act.activation(streams(buf)[:, :, HIST:],
                                   psum[:, 2 * j + 1, SEQ - HALF:HALF].rearrange("p (b s) -> p b s", b=NB),
                                   ACT.Copy).then_inc(bank_free, 1)
                    split(i + (U_QK // 2 + 1), j)
                    act.wait_ge(conv_summed, 2 * i + (j + 1))
                    act.activation(qk[:, bass.ds(2 * i + j, 1), :], conv_acc[:].unsqueeze(1),
                                   ACT.Silu).then_inc(silu_done, 1)
            act.wait_ge(ones_ready, 1)
            with act.Fori(0, 2) as i:
                for j in range(4):
                    if j == 3:
                        for t in range(TT):
                            act.wait_ge(pe_done, 20 * i + (5 * (U_V + 3) + t + 1))
                            act.activation(va[:, t, bass.ds(2 * i, 2), 0:DV],
                                           psum[:, t, :].rearrange("p (h v) -> p h v", h=2),
                                           ACT.Copy).then_inc(tok_evac, 1)
                    split(2 * i + (U_V // 2 + 1 + j // 2), j % 2)
            for c in range(2):
                for j in range(4):
                    if j == 3:
                        for t in range(TT):
                            n = TT * c + t
                            act.wait_ge(pe_done, 5 * (U_OG + 4 * c + 3) + t + 1)
                            if n >= 2:
                                act.wait_ge(og_stored[n % 2], 16 * (n // 2))
                            act.activation(og_out[n % 2][:], psum[:, t, :], ACT.Sigmoid).then_inc(tok_evac, 1)
                            act.wait_ge(tok_evac, 10 + n + 1)
                            act.dma_start(og_dram[P * t:P * (t + 1), 512 * c:512 * (c + 1)],
                                          og_out[n % 2][:]).then_inc(og_stored[n % 2], 16)
                    if c == 0 or j < 2:
                        split(U_OG // 2 + 1 + 2 * c + j // 2, j % 2)
                    if (c, j) == (0, 1):
                        act.wait_ge(row_dve, 1)
                        act.activation(r_x[:], r_x[:], ACT.Exp, scale=-1.0).then_inc(row_act, 1)
                    if (c, j) == (0, 2):
                        act.wait_ge(row_dve, 2)
                        act.activation(r_z[:], r_y[:], ACT.Ln).then_inc(row_act, 1)
                    if (c, j) == (1, 1):
                        act.wait_ge(row_dve, 4)
                        act.activation(r_g[:], r_g[:], ACT.Exp).then_inc(row_act, 1)
            act.wait_ge(tail_done, 1)
            act.activation(tail_out[:], psum[0:27, 6:8, :].rearrange("p b n -> p (b n)"),
                           ACT.Copy).then_inc(tail_ev, 1)
            act.wait_ge(s5_state_tr, 1)
            for r in range(2):
                act.activation(sst[:, r, :, PSTEPS::2].rearrange("p a b -> p b a"),
                               psum[:, 5, 256 * r:256 * (r + 1)].rearrange("p (b a) -> p b a", b=NB),
                               ACT.Copy).then_inc(s5_state_in, 1)
            act.wait_ge(tail_ev, 1)
            act.dma_start(o["conv_p"].rearrange("o b j c -> (o b j) c"), tail_out[0:3, :]).then_inc(tail_stored, 16)
            act.dma_start(o["conv_s"].rearrange("o b j c -> (o b j) c"), tail_out[3:27, :]).then_inc(tail_stored, 16)
            act.dma_start(o["m_p"].rearrange("o b h -> h (o b)"), r_m[:, SEQ - 1:SEQ]).then_inc(out_stored, 16)
            with nc.allow_non_contiguous_dma(reason="32 words"):
                act.dma_start(o["m_s"].rearrange("o b h -> h (o b)"), r_m[:, SEQ + DSEQ - 1::DSEQ]
                              ).then_inc(out_stored, 16)
            for k in range(BLOCKS):
                pairs = slice(BP * k, BP * (k + 1))
                act.wait_ge(bwt_done, k + 1)
                if k >= 2:
                    act.wait_ge(v_done, k - 1)
                act.activation(bwt[k % 2][:].rearrange("p r q n -> p r (q n)"), psum[:, 6:8, :],
                               ACT.Copy).then_inc(bwt_ready, 1)
                act.wait_ge(v_done, k + 1)
                for r in range(2):
                    v = psum[:, 4 + r, 0:BP * STEPS].rearrange("p (q c) -> p q c", q=BP)
                    act.activation(sst[:, r, pairs, 1:PSTEPS], v[:, :, 0:PSTEPS - 1], ACT.Copy)
                    act.activation(fin[:, r, 0, pairs], v[:, :, PSTEPS - 1], ACT.Copy)
                    act.activation(sst[:, r, pairs, PSTEPS + 1::2], v[:, :, PSTEPS::2], ACT.Copy)
                    m = act.activation(fin[:, r, 1:, pairs].rearrange("p b a -> p a b"), v[:, :, PSTEPS + 1::2], ACT.Copy)
                m.then_inc(v_evac, 1)
            def head_sums(t):
                act.wait_ge(num_evac, H * (t + 1))
                for h in range(H):
                    m = act.activation(sq_out[:], hraw[t % 2][:, h, 0:DV], ACT.Square,
                                       accum_out=stat[:, 4, 4 * t + h:4 * t + h + 1])
                    if h < H - 1:
                        after(m)
                m.then_inc(oa_sums, 1)
                act.wait_ge(oa_mean, t + 1)
                act.activation(stat[:, 6, 4 * t:4 * t + 4], stat[:, 5, 4 * t:4 * t + 4],
                               ACT.Sqrt).then_inc(oa_root, 1)

            def store_ha(t):
                act.wait_ge(oa_ready, t + 1)
                act.dma_start(ha_dram[P * t:P * (t + 1), :], og_in[t % 2][:].rearrange("p h v -> p (h v)")
                              ).then_inc(ha_stored[t % 2], 16)

            act.wait_ge(em_done, 1)
            act.activation(exp_neg_m[:].rearrange("p t h -> p (t h)"), psum[:, 7, 0:TT * H], ACT.Exp,
                           scale=-1.0).then_inc(em_ready, 1)
            for t in range(TT):
                act.wait_ge(arg_done, t + 1)
                act.activation(dt[:].rearrange("p h n -> p (h n)"), psum[:, 0, :], ACT.Exp).then_inc(dt_ready, 1)
                if t:
                    head_sums(t - 1)
                if t == SAMPLE:
                    act.wait_ge(kt_done, TT)
                    act.activation(ksb[:].rearrange("p h n -> p (h n)"), psum[:, 3, :],
                                   ACT.Copy).then_inc(ksb_ready, 1)
                    act.wait_ge(fin_tr, 1)
                    act.wait_ge(oa_ready, TT - 1)
                    act.activation(cp_out[:].rearrange("p (b n) d -> p b (n d)", b=2), psum[:, 0:2, :],
                                   ACT.Copy).then_inc(fin_ev, 1)
                    act.wait_ge(fin_tr, 2)
                    act.activation(np_out[:], psum[0:4, 6, 0:P], ACT.Copy).then_inc(fin_ev, 1)
                if t >= 2:
                    act.wait_ge(oa_ready, t - 1)
                for h in range(H):
                    if t == SAMPLE:
                        for q in range(4):
                            act.wait_ge(ctr_done, 4 * h + q + 1)
                            act.activation(cts[:, 2 * q:2 * q + 2, 0:DV],
                                           psum[:, q, :].rearrange("p (b v) -> p b v", b=2),
                                           ACT.Copy).then_inc(cts_ready, 1)
                    act.wait_ge(num_done, H * t + h + 1)
                    act.activation(hraw[t % 2][:, h, :], psum[:, 4 + h % 2, 0:VA1], ACT.Copy).then_inc(num_evac, 1)
                if t:
                    store_ha(t - 1)
            head_sums(TT - 1)
            store_ha(TT - 1)
            act.wait_ge(fin_ev, 2)
            act.dma_start(o["c_p"][0, 0].rearrange("h (v p) d -> p (h v) d", v=2), cp_out[:]).then_inc(out_stored, 16)
            act.dma_start(o["n_p"][0, 0], np_out[:]).then_inc(out_stored, 16)
            act.wait_ge(fin_tr, 3)
            act.activation(ns_out[:], psum[0:NB * H, 6, P:2 * P], ACT.Copy).then_inc(fin_ev, 1)
            act.wait_ge(fin_tr, 4)
            act.activation(s5p_out[:].rearrange("a r p -> a (r p)"), psum[0:PAIRS, 0, 0:2 * P],
                           ACT.Copy).then_inc(fin_ev, 1)
            act.wait_ge(fin_tr, 5)
            act.activation(s5_io[:].rearrange("x r q p -> x (r q p)"), psum[:, 1, :],
                           ACT.Copy).then_inc(fin_ev, 1)
            act.wait_ge(fin_ev, 5)
            act.dma_start(o["n_s"][0].rearrange("b h d -> (b h) d"), ns_out[:]).then_inc(out_stored, 16)
            for r in range(2):
                act.dma_start(o[("s5re_p", "s5im_p")[r]][0, 0].rearrange("(a g) p -> a (g p)", g=2),
                              s5p_out[:, r, :]).then_inc(out_stored, 16)
                act.dma_start(o[("s5re_s", "s5im_s")[r]][0].rearrange("b (a g) p -> (b a) (g p)", g=2)
                              .rearrange("(q x) p -> x q p", q=2), s5_io[:, r, :, :]).then_inc(out_stored, 16)
            def z_part(c):
                if 0 <= c < BLOCKS:
                    act.wait_ge(z_loaded[c % 2], 16 * (c // 2 + 1))
                    act.activation(z[:, c, :], z[:, c, :], ACT.Gelu_apprx_tanh).then_inc(z_ready, 1)
                if c >= 1:
                    act.wait_ge(z_ready, c)
                    act.activation(z_hi[:, c - 1, :], z[:, c - 1, :], ACT.Copy).then_inc(z_hi_ready, 1)

            for k in range(BLOCKS):
                banks = (2, 3) if k % 2 else (4, 5)
                act.wait_ge(y_done, k + 1)
                if k >= 2:
                    act.wait_ge(y_stored[k % 2], 16 * FR * (k // 2))
                for g in range(2):
                    act.activation(y_out[k % 2][:, :, g, :],
                                   psum[:, banks[g], 0:BP * STEPS].rearrange("p (q c) -> p q c", q=BP),
                                   ACT.Copy).then_inc(y_evac, 1)
                if k in (2, 3):
                    split(U_GLU // 2, k - 2)
                z_part(k - 2)
            for c in range(BLOCKS - 2, BLOCKS + 1):
                z_part(c)

            def mlstm_tile(t):
                for q in range(2):
                    n = 2 * t + q
                    act.wait_ge(oat_done, n + 1)
                    for k in range(4):
                        m = act.activation(ot_hi[:, 4 * q + k, P * t:P * (t + 1)],
                                           psum[:, 4 + n % 4, P * k:P * (k + 1)], ACT.Copy,
                                           scale=chan[:, 4 * q + k, R_GMH:R_GMH + 1])
                    m.then_inc(oat_hi, 1)

            mlstm_tile(0)
            mlstm_tile(1)
            for j in range(4):
                for c in range(2):
                    n = 2 * j + c
                    act.wait_ge(pe_done, 5 * (U_GLU + j) + 2 + 3 * c)
                    act.activation(psum[:, 2 * c:2 * c + 2, 0:HALF], psum[:, 2 * c:2 * c + 2, 0:HALF],
                                   ACT.Sigmoid, bias=chan[:, n, R_BGLU:R_BGLU + 1]).then_inc(gate_ready, 1)
                    act.wait_ge(ob_ready, n + 1)
                    act.activation(ot_hi[:, 8 + n, :], ob[:], ACT.Copy).then_inc(ob_hi, 1)
                split((U_GLU + 2 + j) // 2, j % 2)
                if j + 2 < TT:
                    mlstm_tile(j + 2)
            def mix_root(t):
                act.wait_ge(mean_ready, TT + NORMS.index(("mix", t)) + 1)
                act.activation(stat[:, 2, TT + t:TT + t + 1], stat[:, 1, TT + t:TT + t + 1],
                               ACT.Sqrt).then_inc(root_ready, 1)

            def out_chunk(i, last=False):
                for j in range(4):
                    if j == 3:
                        for t in range(TT):
                            act.wait_ge(pe_done, 20 * i + (5 * (U_OUT + 3) + t + 1))
                            act.activation(mix[:, t, bass.ds(512 * i, 512)], psum[:, t, :],
                                           ACT.Copy).then_inc(mix_copied, 1)
                            act.wait_ge(mix_copied, 5 * i + (t + 1))
                            act.activation(psum[:, t, :], psum[:, t, :], ACT.Square,
                                           accum_out=mix_sq[:, bass.ds(i, 1), t]).then_inc(tok_evac, 1)
                            if last and 1 <= t <= 3:
                                mix_root(t - 1)
                    if not (last and j >= 2):
                        split(2 * i + (U_OUT // 2 + 1 + j // 2), j % 2)

            with act.Fori(0, 3) as i:
                out_chunk(i)
            out_chunk(3, last=True)
            act.wait_ge(tok_evac, 40)
            for stage, t in PIPE2[3:]:
                if stage == "mix":
                    mix_root(t)
                elif stage == "hidden":
                    act.wait_ge(xr_ready, t + 1)
                    rms_sums(2 * TT + t, xres[t % 4][:], psum[:, 4:8, :], TT + NORMS.index((stage, t)))
                else:
                    tile_hi(ht_hi, t, 4 * TT + 4 * t)
                    if t >= 3:
                        split(U_FFN // 2, t - 3)
            for s in range(2):
                act.wait_ge(xr_stored[s], 16 * (2 - s))

            def ffn_block(i, last=False):
                for j in range(12):
                    p = j // 2
                    bank = 4 * (p % 2)
                    if j < 8 and j % 2 == 0:
                        act.wait_ge(pe_done, 60 * i + (5 * (U_FFN + j) + 5))
                        if p:
                            act.wait_ge(hid_ready, 8 * i + 2 * p)
                        for h in range(2):
                            act.activation(sg[:, h, :], psum[:, bank + h, 0:HALF], ACT.Silu).then_inc(sg_ready, 1)
                    elif j < 8:
                        for h in range(2):
                            act.wait_ge(hid_ready, 8 * i + (2 * p + h + 1))
                            if p == 0 and h == 0:
                                act.wait_ge(pe_done, 60 * i + 5 * U_FFN)
                            act.activation(h_hi[:, p, HALF * h:HALF * (h + 1)], hid[:, h, :],
                                           ACT.Copy).then_inc(h_hi_ready, 1)
                    if not (last and j >= 10):
                        split(6 * i + ((U_FFN + 2 + j) // 2), j % 2)

            with act.Fori(0, NFB - 1) as i:
                ffn_block(i)
            ffn_block(NFB - 1, last=True)
            for t in range(TT):
                act.wait_ge(tok_evac, 40 + 20 * NFB - TT + t + 1)
                rms_sums(3 * TT + t, acc[:, t, :], psum[:, 0:4, :])

        @block.vector
        def _(dve):
            chained = [0]

            def after(ins):
                chained[0] += 1
                ins.then_inc(dve_chain, 1)
                dve.wait_ge(dve_chain, chained[0])

            def split(n, s):
                dve.wait_ge(hi_ready, n + 1)
                dve.tensor_tensor(w_lo[s][:], raw[s][:], w_hi[s][:].bitcast(F32),
                                  ALU.subtract).then_inc(lo_ready, 1)

            def rms_factor(n, sums, roots=None):
                dve.wait_ge(ssq_ready, sums + 1)
                dve.tensor_scalar(stat[:, 1, n:n + 1], stat[:, 0, n:n + 1], 1.0 / D, EPS, ALU.mult,
                                  ALU.add).then_inc(mean_ready, 1)
                dve.wait_ge(root_ready, (n if roots is None else roots) + 1)
                after(dve.reciprocal(stat[:, 3, n:n + 1], stat[:, 2, n:n + 1]))
                return stat[:, 3, n:n + 1]

            def tile_lo(hi, lo, t, first):
                for q in range(4):
                    dve.wait_ge(tr_hi, first + q + 1)
                    cols = (slice(None), slice(4 * q, 4 * q + 4), slice(P * t, P * (t + 1)))
                    dve.tensor_tensor(lo[cols], psum[:, q, :].rearrange("p (k n) -> p k n", k=4),
                                      hi[cols].bitcast(F32), ALU.subtract).then_inc(tr_lo, 1)

            for stage, t in PIPE:
                if stage == "sums":
                    f = rms_factor(t, t)
                    if t == 0:
                        dve.wait_ge(g_loaded, 16)
                    dve.scalar_tensor_tensor(out=xrow[t][:], in0=xrow[t][:], scalar=f, in1=gbc[:],
                                             op0=ALU.mult, op1=ALU.mult).then_inc(normed, 1)
                    continue
                tile_lo(xt_hi, xt_lo, t, 4 * t)
                if t == TT - 1:
                    dve.wait_ge(lo_ready, 1)
                    split(1, 1)
            after(dve.memset(gate_win[:], 0.0))
            dve.wait_ge(small_loaded, 16 * N_SMALL)
            for g in range(2):
                m = dve.tensor_copy(gate_win[:, 32 * g:32 * g + GP * KT].rearrange("p (k c) -> p k c", c=GP)[:, :, 0:4],
                                    gate_w[:, :, 4 * g:4 * g + 4])
            m.then_inc(gate_w_ready, 1)
            dve.wait_ge(dis_act, 1)
            dve.tensor_tensor(gate_w_lo[:], gate_win[:], gate_w_hi[:].bitcast(F32),
                              ALU.subtract).then_inc(gate_w_ready, 1)
            for s in range(2):
                dve.memset(conv_in[s][:, 0:HIST], 0.0).then_inc(conv_read, 1)
            dve.wait_ge(const_ready, 3)
            after(dve.tensor_reduce(diag16[:], ident[:].rearrange("p (g i) -> p i g", g=8), AX.X, ALU.add))

            def v(n):
                return dis[:, n, :]

            def tt(out, x, y, op):
                after(dve.tensor_tensor(v(out), v(x), v(y), op))

            LAM_RE, LAM_IM, EXPO, ANGLE, TURNS, COMP, MAG, SIN, COS, NR, DEN, T0 = range(4, 16)
            dve.wait_ge(dis_act, 2)
            step = ldt[:, 1, :].unsqueeze(2).to_broadcast([PAIRS, 2, NS])
            for dst, src in ((EXPO, LAM_RE), (ANGLE, LAM_IM)):
                after(dve.tensor_tensor(v(dst).rearrange("a (g p) -> a g p", g=2),
                                        v(src).rearrange("a (g p) -> a g p", g=2), step, ALU.mult))
            after(dve.tensor_scalar(v(TURNS), v(ANGLE), 1.0 / TWO_PI, ROUND, ALU.mult, ALU.add))
            after(dve.tensor_scalar(v(TURNS), v(TURNS), -ROUND, None, ALU.add))
            for part in (PI2_A, PI2_B, PI2_C):
                after(dve.scalar_tensor_tensor(out=v(ANGLE), in0=v(TURNS), scalar=-part, in1=v(ANGLE),
                                               op0=ALU.mult, op1=ALU.add))
            after(dve.tensor_scalar(v(ANGLE), v(ANGLE), 3.1415925, -3.1415925, ALU.min, ALU.max))
            after(dve.scalar_tensor_tensor(out=v(COMP), in0=v(ANGLE), scalar=-1.0, in1=v(ANGLE),
                                           op0=ALU.mult, op1=ALU.max))
            dve.tensor_scalar(v(COMP), v(COMP), -1.0, float(np.pi / 2), ALU.mult, ALU.add).then_inc(dis_dve, 1)
            dve.wait_ge(dis_act, 3)
            tt(0, MAG, COS, ALU.mult)
            tt(1, MAG, SIN, ALU.mult)
            after(dve.tensor_scalar(v(NR), v(0), -1.0, None, ALU.add))
            tt(DEN, LAM_RE, LAM_RE, ALU.mult)
            tt(T0, LAM_IM, LAM_IM, ALU.mult)
            tt(DEN, DEN, T0, ALU.add)
            after(dve.reciprocal(v(DEN), v(DEN)))
            tt(2, NR, LAM_RE, ALU.mult)
            tt(T0, 1, LAM_IM, ALU.mult)
            tt(2, 2, T0, ALU.add)
            tt(2, 2, DEN, ALU.mult)
            tt(3, 1, LAM_RE, ALU.mult)
            tt(T0, NR, LAM_IM, ALU.mult)
            tt(3, 3, T0, ALU.subtract)
            dve.tensor_tensor(v(3), v(3), v(DEN), ALU.mult).then_inc(dis_dve, 1)

            with dve.Fori(0, 4) as i:
                for j in range(2):
                    split(2 * i + (j + 2), j)
            dve.wait_ge(small_tr, 3)
            for r in range(2):
                dve.tensor_copy(lbp[:, r, :, 1], psum[:, 6, PAIRS * r:PAIRS * (r + 1)])
            dve.tensor_copy(fct[:].rearrange("p r a -> p (r a)"), psum[:, 6, 2 * PAIRS:4 * PAIRS]).then_inc(small_ev, 1)
            dve.wait_ge(small_ev, 3)
            STEPS_CONV = 9
            with dve.Fori(0, 4) as i:
                for j in range(2):
                    n = 2 * i + j
                    split(2 * i + (U_QK + j + 2), j)
                    buf = conv_in[j]
                    dve.wait_ge(conv_filled, 4 * i + (2 * j + 2))
                    dve.wait_ge(bank_free, 2 * i + (U_QK + j + 1))
                    base_n = 2 * STEPS_CONV * i + STEPS_CONV * j
                    dve.tensor_copy(vec[:], chan[:, bass.ds(n, 1), :].rearrange("p o r -> p (o r)")
                                    ).then_inc(conv_step, 1)
                    dve.tensor_copy(conv_tail[:, bass.ds(n, 1), 0:HIST].rearrange("p o j -> p (o j)"),
                                    buf[:, SEQ:SEQ + HIST])
                    dve.tensor_copy(conv_tail[:, bass.ds(n, 1), HIST:].rearrange("p o (b j) -> p (o b) j", b=NB),
                                    streams(buf)[:, :, DSEQ:]).then_inc(conv_step, 1)
                    dve.wait_ge(conv_step, base_n + 2)
                    dve.tensor_copy(streams(buf)[:, :, 0:HIST],
                                    vec[:, R_HIST:].rearrange("p (b j) -> p b j", b=NB)).then_inc(conv_step, 1)
                    dve.wait_ge(conv_step, base_n + 3)
                    dve.wait_ge(silu_done, n + 1)
                    for tap in range(CONV):
                        w = vec[:, tap:tap + 1]
                        for part in range(2):
                            if part == 0:
                                src, dst = buf[:, tap:tap + SEQ], conv_acc[:, 0:SEQ]
                            else:
                                src = streams(buf)[:, :, tap:tap + DSEQ]
                                dst = conv_acc[:, SEQ:].rearrange("p (b s) -> p b s", b=NB)
                            if tap == 0:
                                m = dve.tensor_scalar(dst, src, w, vec[:, R_BCONV:R_BCONV + 1], ALU.mult, ALU.add)
                            else:
                                m = dve.scalar_tensor_tensor(out=dst, in0=src, scalar=w, in1=dst,
                                                             op0=ALU.mult, op1=ALU.add)
                            if tap < CONV - 1:
                                m.then_inc(conv_step, 1)
                            elif part:
                                m.then_inc(conv_summed, 1)
                            else:
                                m.then_inc(conv_read, 1)
                        if tap < CONV - 1:
                            dve.wait_ge(conv_step, base_n + (3 + 2 * tap + 2))
            dve.wait_ge(s5_consts, 1)
            dve.wait_ge(gates_done, 1)
            dve.memset(va[:, :, :, DV:VA1].rearrange("p t h o -> p t (h o)"), 1.0).then_inc(ones_ready, 1)
            with dve.Fori(0, 2) as i:
                for j in range(4):
                    split(4 * i + (U_V + 2 + j), j % 2)
            li, lf, x, y, w = r_li[:], r_lf[:], r_x[:], r_y[:], r_z[:]
            dve.wait_ge(gates_loaded, 32)
            dve.wait_ge(silu_done, 9)
            dve.scalar_tensor_tensor(out=x, in0=lf, scalar=-1.0, in1=lf, op0=ALU.mult,
                                     op1=ALU.max).then_inc(row_dve, 1)
            split(U_OG + 2, 0)
            split(U_OG + 3, 1)
            dve.wait_ge(row_act, 1)
            dve.tensor_scalar(y, x, 1.0, None, ALU.add).then_inc(row_dve, 1)
            split(U_OG + 4, 0)
            dve.wait_ge(row_dve, 2)
            after(dve.scalar_tensor_tensor(out=x, in0=y, scalar=-1.0, in1=x, op0=ALU.add, op1=ALU.subtract))
            dve.wait_ge(row_act, 2)
            after(dve.reciprocal(y, y))
            after(dve.tensor_tensor(x, x, y, ALU.mult))
            after(dve.tensor_tensor(w, w, x, ALU.subtract))
            after(dve.scalar_tensor_tensor(out=lf, in0=lf, scalar=0.0, in1=w, op0=ALU.min, op1=ALU.subtract))
            zero = ident[0:4, 64:65]
            for c in range(SAMPLE):
                seg = slice(P * c, P * (c + 1))
                dve.tensor_tensor_scan(w[:, seg], lf[:, seg], zero.to_broadcast([4, P]), 0.0, ALU.add, ALU.add)
            dve.tensor_tensor_scan(r_m[:, 0:SEQ], lf[:, 0:SEQ], li[:, 0:SEQ], 0.0, ALU.add, ALU.max)
            for b in range(NB):
                seg = slice(SEQ + DSEQ * b, SEQ + DSEQ * (b + 1))
                dve.tensor_tensor_scan(w[:, seg], lf[:, seg], zero.to_broadcast([4, DSEQ]), 0.0, ALU.add, ALU.add)
                m = dve.tensor_tensor_scan(r_m[:, seg], lf[:, seg], li[:, seg], m0s[:, b:b + 1],
                                           ALU.add, ALU.max)
            after(m)
            after(dve.tensor_tensor(r_a[:], w, r_m[:], ALU.subtract))
            after(dve.tensor_tensor(r_b[:], li, w, ALU.subtract))
            dve.tensor_copy(r_g[:, 0:P], r_a[:, 0:P]).then_inc(row_dve, 1)
            for c in range(1, SAMPLE):
                seg = slice(P * c, P * (c + 1))
                dve.tensor_scalar(r_g[:, seg], r_a[:, seg], r_m[:, P * c - 1:P * c], None, ALU.add)
            dve.tensor_tensor(r_g[:, SEQ:].rearrange("p (b s) -> p b s", b=NB),
                              r_a[:, SEQ:].rearrange("p (b s) -> p b s", b=NB),
                              m0s[:].unsqueeze(2).to_broadcast([4, NB, DSEQ]), ALU.add).then_inc(row_dve, 1)
            for j in range(3):
                split(U_OG + 5 + j, (5 + j) % 2)
            dve.wait_ge(pe_done, 5 * U_GLU)
            dve.memset(bdiag[0][:], 0.0)
            after(dve.memset(bdiag[1][:], 0.0))
            def block_diagonal(k):
                if k >= 2:
                    dve.wait_ge(k_done, k - 1)
                for g in range(2):
                    dve.tensor_copy(bdiag[k % 2][64 * g:64 * g + 64, :, :, GI * g:GI * (g + 1)],
                                    bbar[64 * g:64 * g + 64, :, BP * k:BP * (k + 1), :]).then_inc(bdiag_ready, 1)

            block_diagonal(0)
            input_powers(dve, after, 0).then_inc(bpw_ready[0], 1)
            dve.tensor_copy(lam8[:, 0, 0, :], lbp[:, 0, :, FR])
            dve.tensor_copy(lam8[:, 0, 1, :], lbp[:, 0, :, FR])
            dve.tensor_scalar(lam8[:, 1, 0, :], lbp[:, 1, :, FR], -1.0, None, ALU.mult)
            dve.tensor_copy(lam8[:, 1, 1, :], lbp[:, 1, :, FR])
            dve.memset(sst[:, :, :, 0:1].rearrange("p r a o -> p r (a o)"), 0.0)
            for s in range(2):
                dve.memset(kpad[s][:, 0:7 * GI], 0.0)
            dve.wait_ge(cpw_ready, 2 * BLOCKS)
            dve.memset(qgm[:], 0.0)
            after(dve.memset(ct[:], 0.0))
            for k in range(BLOCKS):
                if k + 1 < BLOCKS:
                    block_diagonal(k + 1)
                if k % 2 and k + 1 < BLOCKS:
                    dve.wait_ge(bwt_done, k)
                    dve.wait_ge(bpw_ready[0], (k + 1) // 2)
                    input_powers(dve, after, k + 1).then_inc(bpw_ready[0], 1)
                dve.wait_ge(k_done, k + 1)
                if k >= 2:
                    dve.wait_ge(k_stored[k % 2], 16 * (k // 2))
                dve.scalar_tensor_tensor(out=kpad[k % 2][:, 7 * GI:8 * GI], in0=diag16[:],
                                         scalar=chan[:, k, R_S5D:R_S5D + 1], in1=psum[:, 3, 0:GI],
                                         op0=ALU.mult, op1=ALU.add).then_inc(k_ready, 1)
                dve.tensor_copy(kpad[k % 2][:, 8 * GI:], psum[:, 3, GI:P]).then_inc(k_ready, 1)
            scale = float(DQK) ** -0.5

            def head_norm(t):
                f = stat[:, 7, 4 * t:4 * t + 4]
                mean = stat[:, 5, 4 * t:4 * t + 4]
                den = hraw[t % 2][:, :, DV]
                dve.wait_ge(num_evac, H * (t + 1))
                after(dve.scalar_tensor_tensor(out=f, in0=den, scalar=-1.0, in1=den, op0=ALU.mult, op1=ALU.max))
                after(dve.tensor_tensor(f, f, exp_neg_m[:, t, :], ALU.max))
                after(dve.reciprocal(f, f))
                dve.wait_ge(oa_sums, t + 1)
                after(dve.tensor_tensor(mean, stat[:, 4, 4 * t:4 * t + 4], f, ALU.mult))
                after(dve.tensor_tensor(mean, mean, f, ALU.mult))
                dve.tensor_scalar(mean, mean, 1.0 / DV, EPS, ALU.mult, ALU.add).then_inc(oa_mean, 1)
                dve.wait_ge(oa_root, t + 1)
                after(dve.reciprocal(stat[:, 6, 4 * t:4 * t + 4], stat[:, 6, 4 * t:4 * t + 4]))
                after(dve.tensor_tensor(f, f, stat[:, 6, 4 * t:4 * t + 4], ALU.mult))
                dve.wait_ge(og_loaded[t % 2], 16 * (t // 2 + 1))
                for h in range(H):
                    m = dve.scalar_tensor_tensor(out=og_in[t % 2][:, h, :], in0=hraw[t % 2][:, h, 0:DV],
                                                 scalar=f[:, h:h + 1], in1=og_in[t % 2][:, h, :],
                                                 op0=ALU.mult, op1=ALU.mult)
                m.then_inc(oa_ready, 1)

            dve.wait_ge(em_ready, 1)
            for t in range(TT):
                rows = slice(P * t, P * (t + 1))
                dve.wait_ge(s_done, t + 1)
                dve.wait_ge(dt_ready, t + 1)
                dve.scalar_tensor_tensor(out=pt[:].rearrange("p h n -> p (h n)"), in0=psum[:, 1, :],
                                         scalar=scale, in1=dt[:].rearrange("p h n -> p (h n)"),
                                         op0=ALU.mult, op1=ALU.mult).then_inc(pt_ready, 1)
                dve.wait_ge(gb_done, t + 1)
                gb = psum[:, 2, :].rearrange("p (h n) -> p h n", h=H)
                if t < SAMPLE:
                    after(dve.tensor_copy(decay[:, :, 0], gb[:, :, P - 1]))
                else:
                    after(dve.tensor_copy(decay[:], gb[:, :, DSEQ - 1::DSEQ]))
                dve.scalar_tensor_tensor(out=qg[:], in0=qk[:, 0:H, rows], scalar=scale, in1=gb,
                                         op0=ALU.mult, op1=ALU.mult).then_inc(qg_ready, 1)
                if t < SAMPLE:
                    dve.wait_ge(kt_done, t + 1)
                    dve.tensor_tensor(kw[:], psum[:, 3, :].rearrange("p (h n) -> p h n", h=H),
                                      dt[:, :, P - 1:P].to_broadcast([P, H, P]), ALU.mult).then_inc(kw_ready, 1)
                    if t:
                        head_norm(t - 1)
                    for h in range(H):
                        dve.wait_ge(dc_done, H * t + h + 1)
                        dve.scalar_tensor_tensor(out=ct[:, h, :], in0=ct[:, h, :], scalar=decay[:, h, 0:1],
                                                 in1=psum[:, h, 0:VA1], op0=ALU.mult,
                                                 op1=ALU.add).then_inc(ct_ready, 1)
                    continue
                head_norm(t - 1)
                dve.wait_ge(qg_ready, TT)
                dve.wait_ge(ksb_ready, 1)
                for h in range(H):
                    if h:
                        dve.wait_ge(num_done, H * t + h)
                    dve.tensor_copy(qgm[:].rearrange("p (b s) -> p b s", b=NB)[:, :, 0:DSEQ],
                                    qg[:, h, :].rearrange("p (b s) -> p b s", b=NB)).then_inc(qgm_ready, 1)
                    dve.tensor_copy(cts[:, :, DV], n0[:, :, h]).then_inc(cts_ready, 1)
                    if h:
                        dve.wait_ge(un_done, 4 * h)
                    dve.tensor_tensor(kwall[:], ksb[:, h, :].unsqueeze(1).to_broadcast([P, NB, P]),
                                      dt[:, h, DSEQ - 1::DSEQ].unsqueeze(2).to_broadcast([P, NB, P]),
                                      ALU.mult).then_inc(kwall_ready, 1)
                    for v2 in range(2):
                        for q in range(2):
                            dve.wait_ge(un_done, 4 * h + 2 * v2 + q + 1)
                            for b in range(4 * q, 4 * q + 4):
                                c0 = c0n[h % 2][:, v2, b, :]
                                m = dve.scalar_tensor_tensor(out=c0, in0=c0, scalar=decay[:, h, b:b + 1],
                                                             in1=psum[:, 2 * v2 + q, P * (b % 4):P * (b % 4 + 1)],
                                                             op0=ALU.mult, op1=ALU.add)
                            m.then_inc(c_new, 1)
                    after(dve.tensor_tensor(n_new[:, :, h], n0[:, :, h], decay[:, h, :], ALU.mult))
                    dve.wait_ge(nn_done, h + 1)
                    dve.tensor_tensor(n_new[:, :, h], n_new[:, :, h], psum[:, 7, NB * h:NB * (h + 1)],
                                      ALU.add).then_inc(ct_ready, 1)
            def z_lo_part(c):
                dve.wait_ge(z_hi_ready, c + 1)
                dve.tensor_tensor(z_lo[:, c, :], z[:, c, :], z_hi[:, c, :].bitcast(F32),
                                  ALU.subtract).then_inc(z_lo_ready, 1)

            head_norm(TT - 1)
            dve.wait_ge(scan_done, 1)
            for s in range(2):
                dve.wait_ge(k_stored[s], 16 * BLOCKS // 2)
            for k in range(BLOCKS):
                if k >= 2:
                    dve.wait_ge(y_done, k - 1)
                for r in range(2):
                    for g in range(2):
                        m = dve.tensor_copy(sty[k % 2][64 * r:64 * r + 64, g::2, :],
                                            sst[64 * g:64 * g + 64, r, BP * k:BP * (k + 1), :])
                m.then_inc(sty_ready, 1)
                if k in (4, 5):
                    split(U_GLU + k - 4, k - 4)
                if k >= 4:
                    z_lo_part(k - 4)
            for c in range(BLOCKS - 4, BLOCKS):
                z_lo_part(c)

            def mlstm_tile(t):
                for q in range(2):
                    n = 2 * t + q
                    dve.wait_ge(oat_hi, n + 1)
                    for k in range(4):
                        kt = 4 * q + k
                        m = dve.scalar_tensor_tensor(
                            out=ot_lo[:, kt, P * t:P * (t + 1)], in0=psum[:, 4 + n % 4, P * k:P * (k + 1)],
                            scalar=chan[:, kt, R_GMH:R_GMH + 1],
                            in1=ot_hi[:, kt, P * t:P * (t + 1)].bitcast(F32), op0=ALU.mult, op1=ALU.subtract)
                    m.then_inc(oat_lo, 1)

            mlstm_tile(0)
            mlstm_tile(1)
            for j in range(4):
                for c in range(2):
                    n = 2 * j + c
                    dve.wait_ge(gate_ready, n + 1)
                    if n:
                        dve.wait_ge(ob_lo, n)
                    for h in range(2):
                        fr = slice(4 * h, 4 * h + 4)
                        m = dve.tensor_tensor(
                            ob[:].rearrange("p (c r) -> p r c", r=FR)[:, fr, :],
                            z[:, n, :].rearrange("p (r c) -> p r c", r=FR)[:, fr, :],
                            psum[:, 2 * c + h, 0:HALF].rearrange("p (r c) -> p r c", r=4), ALU.mult)
                        m.then_inc(ob_ready if h else ob_first, 1)
                    dve.wait_ge(ob_first, n + 1)
                    dve.wait_ge(ob_hi, n + 1)
                    dve.tensor_tensor(ot_lo[:, 8 + n, :], ob[:], ot_hi[:, 8 + n, :].bitcast(F32),
                                      ALU.subtract).then_inc(ob_lo, 1)
                split(U_GLU + 2 + j, j % 2)
                if j + 2 < TT:
                    mlstm_tile(j + 2)
            with dve.Fori(0, 3) as i:
                for j in range(4):
                    split(4 * i + (U_OUT + 2 + j), j % 2)
            for j in range(2):
                split(U_FFN - 2 + j, j)
            dve.wait_ge(gp_loaded, 32)
            def mix_norm(t):
                n = TT + t
                dve.wait_ge(tok_evac, 35 + t + 1)
                after(dve.tensor_reduce(stat[:, 0, n:n + 1], mix_sq[:, :, t], AX.X, ALU.add))
                dve.tensor_scalar(stat[:, 1, n:n + 1], stat[:, 0, n:n + 1], 1.0 / D, EPS, ALU.mult,
                                  ALU.add).then_inc(mean_ready, 1)
                dve.wait_ge(root_ready, TT + NORMS.index(("mix", t)) + 1)
                after(dve.reciprocal(stat[:, 3, n:n + 1], stat[:, 2, n:n + 1]))
                dve.scalar_tensor_tensor(out=mix[:, t, :], in0=mix[:, t, :], scalar=stat[:, 3, n:n + 1],
                                         in1=g_post[:], op0=ALU.mult, op1=ALU.mult).then_inc(mix_normed, 1)

            for stage, t in PIPE2:
                if stage == "mix":
                    mix_norm(t)
                elif stage == "hidden":
                    f = rms_factor(2 * TT + t, TT + t, TT + NORMS.index((stage, t)))
                    dve.scalar_tensor_tensor(out=mix[:, t, :], in0=xres[t % 4][:], scalar=f, in1=g_ffn[:],
                                             op0=ALU.mult, op1=ALU.mult).then_inc(normed, 1)
                else:
                    tile_lo(ht_hi, ht_lo, t, 4 * TT + 4 * t)
            def ffn_block(i, last=False):
                for j in range(12):
                    p = j // 2
                    bank = 4 * (p % 2)
                    if j < 8 and j % 2:
                        dve.wait_ge(pe_done, 60 * i + (5 * (U_FFN + j) + 5))
                        for h in range(2):
                            dve.wait_ge(sg_ready, 8 * i + (2 * p + h + 1))
                            if p:
                                dve.wait_ge(h_lo_ready, 8 * i + 2 * p)
                            dve.tensor_tensor(hid[:, h, :], sg[:, h, :], psum[:, bank + 2 + h, 0:HALF],
                                              ALU.mult).then_inc(hid_ready, 1)
                        for h in range(2):
                            dve.wait_ge(h_hi_ready, 8 * i + (2 * p + h + 1))
                            cols = (slice(None), p, slice(HALF * h, HALF * (h + 1)))
                            dve.tensor_tensor(h_lo[cols], hid[:, h, :], h_hi[cols].bitcast(F32),
                                              ALU.subtract).then_inc(h_lo_ready, 1)
                    if j >= 8:
                        dve.wait_ge(acc_zero, 1)
                        for t in range(TT):
                            q = TT * (j - 8) + t
                            if last and j == 11 and t >= 2:
                                finish(t - 2)
                            dve.wait_ge(pe_done, 60 * i + (5 * (U_FFN + j) + t + 1))
                            if q == 0:
                                dve.wait_ge(tok_evac, 20 * i + 40)
                            bank = q % 8 if q < 16 else q - 12
                            cols = slice(512 * (j - 8), 512 * (j - 7))
                            dve.tensor_tensor(acc[:, t, cols], acc[:, t, cols], psum[:, bank, :],
                                              ALU.add).then_inc(tok_evac, 1)
                    if not (last and j >= 10):
                        split(12 * i + (U_FFN + 2 + j), j % 2)

            def finish(t):
                f = rms_factor(3 * TT + t, 2 * TT + t)
                if t == 0:
                    dve.wait_ge(gp_loaded, 48)
                m = dve.scalar_tensor_tensor(out=acc[:, t, :], in0=acc[:, t, :], scalar=f, in1=g_last[:],
                                             op0=ALU.mult, op1=ALU.mult)
                if t in ON_POOL:
                    m.then_inc(ff_normed, 1)
                    return
                after(m)
                dve.wait_ge(last_loaded, 16 * TT)
                dve.tensor_tensor(xlast[t][:], xlast[t][:], acc[:, t, :], ALU.add).then_inc(y_by_dve, 1)

            dve.wait_ge(lo_ready, U_FFN + 2)
            with dve.Fori(0, NFB - 1) as i:
                ffn_block(i)
            ffn_block(NFB - 1, last=True)
            for t in range(TT - 2, TT):
                finish(t)

        @block.gpsimd
        def _(pool):
            chained = [0]

            def after(ins):
                chained[0] += 1
                ins.then_inc(pool_chain, 1)
                pool.wait_ge(pool_chain, chained[0])

            pool.memset(ident[:], 0.0)
            pool.memset(mask_prompt[:], 0.0)
            after(pool.memset(mask_sample[:], 0.0))
            pool.affine_select(out=ident[:], in_=ident[:], compare_op=ALU.not_equal, fill=1.0, base=0,
                               pattern=[[-1, P]], channel_multiplier=1).then_inc(const_ready, 1)
            pool.affine_select(out=mask_prompt[:], in_=mask_prompt[:], compare_op=ALU.is_ge, fill=MASKED,
                               base=0, pattern=[[1, P]], channel_multiplier=-1).then_inc(const_ready, 1)
            after(pool.affine_select(out=mask_sample[:], in_=mask_sample[:], compare_op=ALU.is_ge, fill=MASKED,
                                     base=0, pattern=[[1, P]], channel_multiplier=-1))
            per_stream = mask_sample[:].rearrange("p (b s) -> p b s", b=NB)
            pool.affine_select(out=per_stream, in_=per_stream, compare_op=ALU.is_ge, fill=MASKED, base=0,
                               pattern=[[-DSEQ, NB], [0, DSEQ]], channel_multiplier=1).then_inc(const_ready, 1)

            def split(n, s):
                pool.wait_ge(hi_ready, n + 1)
                pool.tensor_tensor(w_lo[s][:], raw[s][:], w_hi[s][:].bitcast(F32),
                                   ALU.subtract).then_inc(lo_ready, 1)

            pool.wait_ge(tr_done, 4 * 3)
            split(0, 0)

            def cmul(dst, x, y, tmp):
                pool.tensor_tensor(dst[0], x[0], y[0], ALU.mult)
                after(pool.tensor_tensor(tmp, x[1], y[1], ALU.mult))
                after(pool.tensor_tensor(dst[0], dst[0], tmp, ALU.subtract))
                pool.tensor_tensor(dst[1], x[0], y[1], ALU.mult)
                after(pool.tensor_tensor(tmp, x[1], y[0], ALU.mult))
                after(pool.tensor_tensor(dst[1], dst[1], tmp, ALU.add))

            pool.wait_ge(small_ev, 3)
            pool.memset(lbp[:, 0, :, 0:1].rearrange("p a o -> p (a o)"), 1.0)
            after(pool.memset(lbp[:, 1, :, 0:1].rearrange("p a o -> p (a o)"), 0.0))
            lb = [lbp[:, r, :, 1] for r in range(2)]
            for k in range(2, FR + 1):
                cmul([lbp[:, r, :, k] for r in range(2)], [lbp[:, r, :, k - 1] for r in range(2)], lb,
                     stmp[:, 1, :, 0])
            cmul([bbar[:, r, :, :] for r in range(2)],
                 [fct[:, r, :].unsqueeze(2).to_broadcast([P, PAIRS, GI]) for r in range(2)],
                 [b_in[:, r, :, :] for r in range(2)], stmp[:, 0, :, :])
            pool.memset(stmp[:, 1, 0, 0:1], 0.0).then_inc(s5_consts, 1)
            pool.wait_ge(small_ev, 2)
            pool.wait_ge(conv_summed, 8)
            for n in range(2 * BLOCKS):
                if n:
                    pool.wait_ge(cpw_stored, 16 * n)
                    pool.wait_ge(cpw_ready, n)
                powers(pool, after, cpw_out, cpw_tmp, 1, c0t, slice(2 * n, 2 * n + 2), 1).then_inc(cpw_ready, 1)
                pool.wait_ge(cpw_ready, n + 1)
                pool.dma_start(cpw_dram[n // 2][:, :, 2 * (n % 2):2 * (n % 2) + 2, :], cpw_out[:]
                               ).then_inc(cpw_stored, 16)
            pool.wait_ge(pe_done, 5 * U_GLU)
            after(pool.memset(sel[:], 0.0))
            pool.affine_select(out=sel[:], in_=sel[:], compare_op=ALU.not_equal, fill=1.0, base=0,
                               pattern=[[-1, 4], [0, P]], channel_multiplier=1).then_inc(sel_ready, 1)
            for k in range(1, BLOCKS, 2):
                if k >= 2:
                    pool.wait_ge(bwt_done, k - 1)
                    pool.wait_ge(bpw_ready[1], k // 2)
                input_powers(pool, after, k).then_inc(bpw_ready[1], 1)
            pool.wait_ge(v_evac, BLOCKS)
            pool.wait_ge(s5_state_in, 2)

            def advance(dst, state, tmp, done):
                shape = list(state.shape)
                lam = [lam8[:, r, :, :] if len(shape) == 3 else
                       lam8[:, r, :, :].unsqueeze(3).to_broadcast(shape) for r in range(2)]
                pool.tensor_tensor(tmp[0], lam[0], state, ALU.mult).then_inc(scan_step, 1)
                pool.tensor_tensor(tmp[1], lam[1], state[:, ::-1], ALU.mult).then_inc(scan_step, 1)
                pool.wait_ge(scan_step, done + 1)
                pool.tensor_tensor(dst, dst, tmp[0], ALU.add).then_inc(scan_step, 1)
                pool.wait_ge(scan_step, done + 3)
                pool.tensor_tensor(dst, dst, tmp[1], ALU.add).then_inc(scan_step, 1)
                pool.wait_ge(scan_step, done + 4)

            one = [scan_tmp[:, r, :, :] for r in range(2)]
            for c in range(PSTEPS):
                advance(sst[:, :, :, c + 1] if c < PSTEPS - 1 else fin[:, :, 0, :], sst[:, :, :, c], one, 4 * c)
            many = [t[:] for t in stream_tmp]
            advance(sst[:, :, :, PSTEPS + 1::2], sst[:, :, :, PSTEPS::2], many, 4 * PSTEPS)
            advance(fin[:, :, 1:, :].rearrange("p r b a -> p r a b"), sst[:, :, :, PSTEPS + 1::2], many,
                    4 * PSTEPS + 4)
            pool.memset(scan_tmp[:, 0, 0, 0:1], 0.0).then_inc(scan_done, 1)
            for k in range(BLOCKS - 2):
                pool.wait_ge(y_done, k + 1)
                load_cpy(pool, k + 2, cpy_loaded)
            for t in range(TT):
                pool.wait_ge(mix_normed, t + 1)
                pool.wait_ge(rows_loaded[t % 4], 16 * (t // 4 + 2))
                pool.tensor_tensor(xres[t % 4][:], xres[t % 4][:], mix[:, t, :], ALU.add).then_inc(xr_ready, 1)
            for s in range(2):
                pool.wait_ge(xr_stored[s + 2], 16)
                pool.wait_ge(normed, TT + s + 3)
                split(U_FFN + s, s)
            pool.wait_ge(tr_done, 8 * TT)
            pool.memset(acc[:].rearrange("p t d -> p (t d)"), 0.0).then_inc(acc_zero, 1)
            for n, t in enumerate(ON_POOL):
                pool.wait_ge(ff_normed, n + 1)
                pool.wait_ge(last_loaded, 16 * TT)
                pool.tensor_tensor(xlast[t][:], xlast[t][:], acc[:, t, :], ALU.add).then_inc(y_by_pool, 1)


_INS = ["x_prompt", "x_sample", "state_conv", "state_mlstm_c", "state_mlstm_n", "state_mlstm_m",
        "state_s5_re", "state_s5_im", "g_pre_mix", "w_in", "w_conv", "b_conv", "b_igate", "b_fgate",
        "g_mh", "s5_lam_re", "s5_lam_im", "s5_log_dt", "s5_b_re", "s5_b_im", "s5_c_re", "s5_c_im",
        "s5_d", "w_glu", "b_glu", "w_out", "g_post_mix", "g_pre_ffn", "w_gate", "w_up", "w_down",
        "g_post_ffn"]
_OUTS = {"y_prompt": (1, SEQ, D), "y_sample": (NB, DSEQ, D),
         "conv_p": (1, 1, HIST, QK), "c_p": (1, 1, H, DV, DQK), "n_p": (1, 1, H, DQK), "m_p": (1, 1, H),
         "s5re_p": (1, 1, G, NS), "s5im_p": (1, 1, G, NS),
         "conv_s": (1, NB, HIST, QK), "c_s": (1, NB, H, DV, DQK), "n_s": (1, NB, H, DQK), "m_s": (1, NB, H),
         "s5re_s": (1, NB, G, NS), "s5im_s": (1, NB, G, NS)}


def kernel(**inputs):
    import concourse.bacc as bacc
    from concourse.bass_utils import run_bass_kernel_spmd

    nc = bacc.Bacc("TRN2", target_bir_lowering=False, num_devices=1)
    arrays, ins, outs = {}, {}, {}
    for name in _INS:
        x = np.ascontiguousarray(inputs[name])
        arrays[f"in_{name}"] = x
        ins[name] = nc.dram_tensor(f"in_{name}", x.shape, mybir.dt.from_np(x.dtype), kind="ExternalInput").ap()
    for name, shape in _OUTS.items():
        outs[name] = nc.dram_tensor(f"out_{name}", shape, F32, kind="ExternalOutput").ap()
    build(nc, ins, outs)
    r = run_bass_kernel_spmd(nc, [arrays], core_ids=[0])
    return tuple(r.results[0][f"out_{name}"] for name in _OUTS)
```
